# Optimizing a Trainium2 kernel written in Bass

```python
import jax
import jax.numpy as jnp
from jax import lax
import numpy as np

D_MODEL = 2048
BATCH = 1
SEQ = 128
DEPTH = 1
DEC_BATCH = 1
DEC_SEQ = 512
PAST_LEN = 128

GRID_W = 64
RW_HEADS = 16
RW_HEAD = 64
RW_DIM = RW_HEADS * RW_HEAD
DECAY_LORA = 64
AAA_LORA = 64
GATE_LORA = 128
RW_LN_EPS = 64e-5
HG_HEADS = 8
HG_DK = 128
HG_DV = 128
HG_KDIM = HG_HEADS * HG_DK
HG_VDIM = HG_HEADS * HG_DV
HG_CHUNK = 32
N_EXPERTS = 16
EXPERT_FF = 1024
CAPACITY_FACTOR = 2
NORM_EPS = 1e-6
N_MOD = 6
RW_COLS = 3 * RW_DIM + 2 * DECAY_LORA + 2 * AAA_LORA + GATE_LORA
HG_COLS = 3 * HG_KDIM + 2 * HG_VDIM
GATE_COLS = 2 * D_MODEL
IN_COLS = RW_COLS + HG_COLS + GATE_COLS

kernel_name = 'hybrid_rwkv7_hgrn2_ecmoe_diffusion_step'

def _rmsnorm(x, g, eps=NORM_EPS):
    x32 = x.astype(jnp.float32)
    y = x32 * lax.rsqrt(jnp.mean(x32 * x32, axis=-1, keepdims=True) + eps)
    return (y * g.astype(jnp.float32)).astype(x.dtype)

def _neighbours(u, grid):
    B, T, C = u.shape
    if grid is not None:
        u = u.reshape(B, grid[0], grid[1], C)
    axis = u.ndim - 2
    n = u.shape[axis]
    pad = [(0, 0)] * u.ndim
    pad[axis] = (1, 1)
    up = jnp.pad(u, pad)
    prev = lax.slice_in_dim(up, 0, n, axis=axis).reshape(B, T, C)
    nxt = lax.slice_in_dim(up, 2, n + 2, axis=axis).reshape(B, T, C)
    return prev, nxt

def _rwkv7_scan(s0, r, w, k, v, kk, a):
    def step(s, inp):
        r_t, w_t, k_t, v_t, kk_t, a_t = inp
        sa = jnp.einsum('bhvk,bhk->bhv', s, -kk_t)
        s = (s * w_t[:, :, None, :] + sa[..., None] * (kk_t * a_t)[:, :, None, :]
             + v_t[..., None] * k_t[:, :, None, :])
        return s, jnp.einsum('bhvk,bhk->bhv', s, r_t)
    xs = tuple(jnp.swapaxes(t, 0, 1) for t in (r, w, k, v, kk, a))
    s, y = lax.scan(step, s0, xs)
    return s, jnp.swapaxes(y, 0, 1)

def _rwkv7_branch(pr, s0_f, s0_b, grid, p):
    B, T, _ = pr.shape
    pr = pr.astype(jnp.float32)
    prev, nxt = _neighbours(pr, grid)
    mu = p['rw_mu'].astype(jnp.float32)
    pr = pr + mu[0] * (prev - pr) + mu[1] * (nxt - pr)
    o0 = 3 * RW_DIM
    cuts = [RW_DIM, 2 * RW_DIM, o0, o0 + DECAY_LORA, o0 + 2 * DECAY_LORA,
            o0 + 2 * DECAY_LORA + AAA_LORA, o0 + 2 * DECAY_LORA + 2 * AAA_LORA]
    r, k, v, wd_f, wd_b, ad_f, ad_b, gd = jnp.split(pr, cuts, axis=-1)
    heads = lambda u: u.reshape(B, T, RW_HEADS, RW_HEAD)
    kk = heads(k * p['rw_k_k'])
    kk = kk * lax.rsqrt(jnp.maximum(jnp.sum(kk * kk, axis=-1, keepdims=True), 1e-24))
    y = jnp.zeros((B, T, RW_HEADS, RW_HEAD), jnp.float32)
    bonus = jnp.zeros((B, T, RW_HEADS, RW_HEAD), jnp.float32)
    finals = []
    for d, (wd, ad, s0) in enumerate(((wd_f, ad_f, s0_f), (wd_b, ad_b, s0_b))):
        w_log = -jax.nn.softplus(-(p['rw_w0'][d] + jnp.tanh(wd) @ p['rw_w2'][d])) - 0.5
        decay = jnp.exp(-jnp.exp(w_log))
        a = jax.nn.sigmoid(p['rw_a0'][d] + ad @ p['rw_a2'][d])
        kd = k * (1.0 + (a - 1.0) * p['rw_k_a'])
        ins = (heads(r), heads(decay), heads(kd), heads(v), kk, heads(a))
        if d == 1:
            ins = tuple(jnp.flip(t, axis=1) for t in ins)
        s_fin, yd = _rwkv7_scan(s0, *ins)
        if d == 1:
            yd = jnp.flip(yd, axis=1)
        y = y + yd
        bonus = bonus + jnp.sum(heads(r) * heads(kd) * p['rw_r_k'], axis=-1, keepdims=True) * heads(v)
        finals.append(s_fin)
    mean = jnp.mean(y, axis=-1, keepdims=True)
    var = jnp.mean(jnp.square(y - mean), axis=-1, keepdims=True)
    y = ((y - mean) * lax.rsqrt(var + RW_LN_EPS)).reshape(B, T, RW_DIM) * p['rw_ln_w'] + p['rw_ln_b']
    g = jax.nn.sigmoid(gd) @ p['rw_g2']
    out = (y + bonus.reshape(B, T, RW_DIM)) * g
    return out, finals[0], finals[1]

def _gla_chunk_scan(s0, q, k, v, logf):
    B, T, H, DK = q.shape
    DV = v.shape[-1]
    n = T // HG_CHUNK
    blocks = lambda u: jnp.moveaxis(u.reshape(B, n, HG_CHUNK, H, u.shape[-1]), 1, 0)
    lower = jnp.tril(jnp.ones((HG_CHUNK, HG_CHUNK), dtype=bool))[None, :, :, None, None]

    def step(s, inp):
        qc, kc, vc, gc = inp
        b = jnp.cumsum(gc, axis=1)
        inter = jnp.einsum('blhk,bhkv->blhv', qc * jnp.exp(b), s)
        rel = jnp.exp(jnp.where(lower, b[:, :, None] - b[:, None, :], -jnp.inf))
        att = jnp.einsum('bthk,bshk,btshk->bhts', qc, kc, rel)
        intra = jnp.einsum('bhts,bshv->bthv', att, vc)
        b_last = b[:, -1]
        s = (s * jnp.exp(b_last)[..., None]
             + jnp.einsum('blhk,blhv->bhkv', kc * jnp.exp(b_last[:, None] - b), vc))
        return s, inter + intra

    s, o = lax.scan(step, s0, tuple(blocks(u) for u in (q, k, v, logf)))
    return s, jnp.moveaxis(o, 0, 1).reshape(B, T, H, DV)

def _hgrn2_branch(ph, s0_f, s0_b, lb, p):
    B, T, _ = ph.shape
    ph = ph.astype(jnp.float32)
    q, f_f, f_b, i, g = jnp.split(ph, [HG_KDIM, 2 * HG_KDIM, 3 * HG_KDIM, 3 * HG_KDIM + HG_VDIM], axis=-1)
    kh = lambda u: u.reshape(B, T, HG_HEADS, HG_DK)
    vh = lambda u: u.reshape(B, T, HG_HEADS, HG_DV)
    q = kh(jax.nn.silu(q))
    v = vh(i)
    o = jnp.zeros((B, T, HG_HEADS, HG_DV), jnp.float32)
    finals = []
    for d, (fl, s0) in enumerate(((f_f, s0_f), (f_b, s0_b))):
        f = lb[d] + (1.0 - lb[d]) * jax.nn.sigmoid(fl)
        ins = (q, kh(1.0 - f), v, kh(jnp.log(f)))
        if d == 1:
            ins = tuple(jnp.flip(t, axis=1) for t in ins)
        s_fin, od = _gla_chunk_scan(s0, *ins)
        if d == 1:
            od = jnp.flip(od, axis=1)
        o = o + od
        finals.append(s_fin)
    o = o * lax.rsqrt(jnp.mean(o * o, axis=-1, keepdims=True) + NORM_EPS)
    out = o.reshape(B, T, HG_VDIM) * p['hg_norm_g'] * jax.nn.silu(g)
    return out, finals[0], finals[1]

def _expert_choice_moe(h, w_router, w_gate, w_up, w_down):
    B, T, _ = h.shape
    cap = CAPACITY_FACTOR * T // N_EXPERTS
    aff = jax.nn.softmax(jnp.einsum('btd,de->bte', h, w_router).astype(jnp.float32), axis=-1)
    vals, idx = lax.top_k(jnp.swapaxes(aff, 1, 2), cap)
    bidx = jnp.arange(B)[:, None, None]
    xg = h[bidx, idx]
    hid = jax.nn.silu(jnp.einsum('becd,edf->becf', xg, w_gate)) * jnp.einsum('becd,edf->becf', xg, w_up)
    yo = jnp.einsum('becf,efd->becd', hid, w_down) * vals[..., None].astype(h.dtype)
    return jnp.zeros_like(h).at[bidx, idx].add(yo.astype(h.dtype))

def _layer(x, cond, s_rw, s_hg, grid, lb, p):
    mod = jax.nn.silu(cond) @ p['ada_w'] + p['ada_b']
    sh1, sc1, gt1, sh2, sc2, gt2 = jnp.split(mod[:, None, :], N_MOD, axis=-1)
    h = _rmsnorm(x, p['norm1_g']) * (1 + sc1) + sh1
    w_in = p['w_in']
    pr = h @ w_in[:, :RW_COLS]
    ph = h @ w_in[:, RW_COLS:RW_COLS + HG_COLS]
    pg = h @ w_in[:, RW_COLS + HG_COLS:]
    s_rw = s_rw.astype(jnp.float32)
    s_hg = s_hg.astype(jnp.float32)
    out_r, srf, srb = _rwkv7_branch(pr, s_rw[:, 0], s_rw[:, 1], grid, p)
    out_h, shf, shb = _hgrn2_branch(ph, s_hg[:, 0], s_hg[:, 1], lb, p)
    gate_r, gate_h = jnp.split(jax.nn.sigmoid(pg.astype(jnp.float32)), 2, axis=-1)
    merged = gate_r * (out_r @ p['w_br_rwkv']) + gate_h * (out_h @ p['w_br_hgrn'])
    x = x + gt1 * (merged.astype(x.dtype) @ p['w_out'])
    h2 = _rmsnorm(x, p['norm2_g']) * (1 + sc2) + sh2
    x = x + gt2 * _expert_choice_moe(h2, p['moe_router'], p['moe_w_gate'], p['moe_w_up'], p['moe_w_down'])
    return x, jnp.stack([srf, srb], axis=1), jnp.stack([shf, shb], axis=1)

def setup_inputs(seed: int = 0) -> dict:
    key = jax.random.key(seed)
    ks = iter(jax.random.split(key, 32))
    nrm = lambda shape, scale: jax.random.normal(next(ks), shape, jnp.float32) * scale
    uni = lambda shape, lo, hi: jax.random.uniform(next(ks), shape, jnp.float32, lo, hi)
    D = D_MODEL
    return {
        'x_prompt': nrm((BATCH, SEQ, D), 1.0),
        'x_sample': nrm((DEC_BATCH, DEC_SEQ, D), 1.0),
        'c': nrm((DEC_BATCH, D), 1.0),
        'state_rwkv': nrm((DEC_BATCH, DEPTH, 2, RW_HEADS, RW_HEAD, RW_HEAD), 0.5),
        'state_hgrn': nrm((DEC_BATCH, DEPTH, 2, HG_HEADS, HG_DK, HG_DV), 0.5),
        'c_ctx': nrm((D,), 1.0),
        'norm1_g': 1.0 + nrm((DEPTH, D), 0.02),
        'norm2_g': 1.0 + nrm((DEPTH, D), 0.02),
        'final_norm_g': 1.0 + nrm((D,), 0.02),
        'ada_w': nrm((DEPTH, D, N_MOD * D), D ** -0.5),
        'ada_b': nrm((DEPTH, N_MOD * D), 0.02),
        'w_in': nrm((DEPTH, D, IN_COLS), D ** -0.5),
        'rw_mu': uni((DEPTH, 2, RW_COLS), 0.0, 0.5),
        'rw_w0': uni((DEPTH, 2, RW_DIM), -5.0, 1.0),
        'rw_w2': nrm((DEPTH, 2, DECAY_LORA, RW_DIM), 0.5 * DECAY_LORA ** -0.5),
        'rw_a0': nrm((DEPTH, 2, RW_DIM), 0.5),
        'rw_a2': nrm((DEPTH, 2, AAA_LORA, RW_DIM), 0.5 * AAA_LORA ** -0.5),
        'rw_g2': nrm((DEPTH, GATE_LORA, RW_DIM), GATE_LORA ** -0.5),
        'rw_k_k': 0.85 + nrm((DEPTH, RW_DIM), 0.05),
        'rw_k_a': 1.0 + nrm((DEPTH, RW_DIM), 0.05),
        'rw_r_k': nrm((DEPTH, RW_HEADS, RW_HEAD), 0.1),
        'rw_ln_w': 1.0 + nrm((DEPTH, RW_DIM), 0.05),
        'rw_ln_b': nrm((DEPTH, RW_DIM), 0.02),
        'hg_lb': nrm((DEPTH + 1, 2, HG_KDIM), 1.0),
        'hg_norm_g': 1.0 + nrm((DEPTH, HG_VDIM), 0.02),
        'w_br_rwkv': nrm((DEPTH, RW_DIM, D), RW_DIM ** -0.5),
        'w_br_hgrn': nrm((DEPTH, HG_VDIM, D), HG_VDIM ** -0.5),
        'w_out': nrm((DEPTH, D, D), D ** -0.5),
        'moe_router': nrm((DEPTH, D, N_EXPERTS), D ** -0.5),
        'moe_w_gate': nrm((DEPTH, N_EXPERTS, D, EXPERT_FF), D ** -0.5),
        'moe_w_up': nrm((DEPTH, N_EXPERTS, D, EXPERT_FF), D ** -0.5),
        'moe_w_down': nrm((DEPTH, N_EXPERTS, EXPERT_FF, D), EXPERT_FF ** -0.5),
    }

def reference(x_prompt, x_sample, c, state_rwkv, state_hgrn, c_ctx, norm1_g, norm2_g, final_norm_g,
              ada_w, ada_b, w_in, rw_mu, rw_w0, rw_w2, rw_a0, rw_a2, rw_g2, rw_k_k, rw_k_a, rw_r_k,
              rw_ln_w, rw_ln_b, hg_lb, hg_norm_g, w_br_rwkv, w_br_hgrn, w_out, moe_router,
              moe_w_gate, moe_w_up, moe_w_down):
    rows = x_sample.shape[1] // GRID_W
    grid = (rows, GRID_W)
    lb_all = jnp.cumsum(jax.nn.softmax(hg_lb.astype(jnp.float32), axis=0), axis=0)
    bp = x_prompt.shape[0]
    xp, xs = x_prompt, x_sample
    new_rw, new_hg = [], []
    for l in range(DEPTH):
        p = dict(norm1_g=norm1_g[l], norm2_g=norm2_g[l], ada_w=ada_w[l], ada_b=ada_b[l], w_in=w_in[l],
                 rw_mu=rw_mu[l], rw_w0=rw_w0[l], rw_w2=rw_w2[l], rw_a0=rw_a0[l], rw_a2=rw_a2[l],
                 rw_g2=rw_g2[l], rw_k_k=rw_k_k[l], rw_k_a=rw_k_a[l], rw_r_k=rw_r_k[l],
                 rw_ln_w=rw_ln_w[l], rw_ln_b=rw_ln_b[l], hg_norm_g=hg_norm_g[l],
                 w_br_rwkv=w_br_rwkv[l], w_br_hgrn=w_br_hgrn[l], w_out=w_out[l],
                 moe_router=moe_router[l], moe_w_gate=moe_w_gate[l], moe_w_up=moe_w_up[l],
                 moe_w_down=moe_w_down[l])
        zero_rw = jnp.zeros((bp, 2, RW_HEADS, RW_HEAD, RW_HEAD), jnp.float32)
        zero_hg = jnp.zeros((bp, 2, HG_HEADS, HG_DK, HG_DV), jnp.float32)
        xp, s_rw, s_hg = _layer(xp, c_ctx[None, :], zero_rw, zero_hg, None, lb_all[l], p)
        new_rw.append(s_rw)
        new_hg.append(s_hg)
        xs, _, _ = _layer(xs, c, state_rwkv[:, l], state_hgrn[:, l], grid, lb_all[l], p)
    y_prompt = _rmsnorm(xp, final_norm_g)
    y_sample = _rmsnorm(xs, final_norm_g)
    new_state_rwkv = jnp.stack(new_rw, axis=1)
    new_state_hgrn = jnp.stack(new_hg, axis=1)
    return (y_prompt, y_sample, new_state_rwkv, new_state_hgrn)


_drawn_inputs = setup_inputs


def setup_inputs(seed=0):
    import zlib

    import numpy as np

    out = dict(_drawn_inputs(seed))
    spreads = {}
    factors = {'state_rwkv': 16.63,
     'state_hgrn': 8.0,
     'norm1_g': 2.673,
     'norm2_g': 3.02,
     'final_norm_g': 8.193,
     'rw_ln_w': 3.312,
     'rw_ln_b': 17.669,
     'hg_norm_g': 5.307}
    for name, (base, spread) in spreads.items():
        noise = np.random.default_rng([zlib.crc32(name.encode()), seed]).standard_normal(out[name].shape)
        drawn = base * np.exp(spread * noise) if base else spread * noise
        out[name] = jnp.asarray(drawn.astype(out[name].dtype))
    for name, factor in factors.items():
        out[name] = (out[name] * factor).astype(out[name].dtype)
    return out
```

```python
from contextlib import ExitStack, contextmanager
import math

import concourse.bass as bass
from concourse import mybir

P = 128
D = 2048
KT = D // P
NS, NP = 512, 128
T = NS + NP
TT = T // P
GRID_W = 64
RW_HEADS, RW_DIM = 16, 1024
PAIRS = RW_HEADS // 2
L = 64
NCH = T // L
HG_HEADS = 8
RW_COLS = 3456
HG0 = RW_COLS
HG_DIM = 1024
GATE0 = RW_COLS + 5 * HG_DIM
NE, FF = 16, 1024
CAP_S, CAP_P = 2 * NS // NE, 2 * NP // NE
EPS = 1e-6
LN_EPS = 64e-5
DECAY_SCALE = math.exp(-0.5)

F32 = mybir.dt.float32
I32 = mybir.dt.int32
ALU = mybir.AluOpType
ACT = mybir.ActivationFunctionType
AX_X = mybir.AxisListType.X

ADA_B, C_S, C_P = 0, 96, 112
MU0, MU1, K_K, K_A, R_K, W0, A0, LN_W, LN_B, MUL0, MUL1 = 0, 24, 48, 56, 64, 72, 88, 104, 112, 120, 123
G1, G2, LB0, LB1, HGN = 0, 16, 32, 48, 64


@contextmanager
def cleared_semaphores(nc):
    before = nc.snapshot_sems()
    yield
    nc.clear_and_free_semaphores(nc.allocated_since(before))
    nc.all_engine_barrier()


class Signal:

    def __init__(self, ctx, nc, name, per=0):
        self.sem, self.name, self.per = nc.alloc_semaphore(name), name, per

    def at(self, n, rnd=None):
        assert n > 0, self.name
        return n if rnd is None else rnd * self.per + n


def bcast(ap, n, axis):
    v = ap.unsqueeze(axis)
    shape = list(v.shape)
    shape[axis] = n
    return v.broadcast_to(shape)


def stage_modulation(nc, I, S):
    with ExitStack() as ctx:
        sb = lambda name, shape, dt=F32: ctx.enter_context(nc.sbuf_tensor(name, shape, dt))
        sg = lambda name: ctx.enter_context(nc.semaphore(name))
        RING, CT = 3, 4
        NBLK = 6 * D // (CT * P)
        rows = sb("rows", [P, 3, P])
        xt = sb("xt", [P, TT, D])
        junk = sb("junk", [P, D])
        ssq = sb("ssq", [P, TT])
        std = sb("std", [P, TT])
        rstd = sb("rstd", [P, TT])
        th = sb("th", [P, 2 * KT])
        cond = sb("cond", [P, KT, 2])
        eps = sb("eps", [P, 1])
        ring = [sb(f"ada{i}", [P, KT, CT * P]) for i in range(RING)]
        ps = ctx.enter_context(nc.psum_tensor("psA", [P, 8, 512], F32))
        s_par, s_x, s_id, s_const = sg("params_in"), sg("x_in"), sg("ident_made"), sg("consts_made")
        s_ada = [sg(f"ada_in{i}") for i in range(RING)]
        s_adaf = [sg(f"ada_free{i}") for i in range(RING)]
        s_ptr, s_ptab, s_th, s_cond = sg("param_rows_turned"), sg("param_tables"), sg("cond_tanh"), sg("cond_ready")
        s_mod, s_modT, s_ssq, s_std, s_xn = sg("mod_sums"), sg("mod_ready"), sg("ssq_ready"), sg("std_ready"), sg("x_normed")
        s_xT, s_h, s_hd, s_v = sg("x_turned"), sg("h_ready"), sg("h_bank_free"), sg("vector_line")
        block = ctx.enter_context(nc.Block())
        mod = ps[:, 0, 0:192].rearrange("p (n s) -> p n s", s=2)

        @block.sync
        def _(sp):
            def rowv(name, r):
                a = I[name]
                if name == "rw_r_k":
                    a = a.rearrange("o (n h) k -> (o n) (h k)", h=2)
                else:
                    letters = "abc"[:len(a.shape) - 1]
                    a = a.rearrange(" ".join(letters) + " (n p) -> (" + " ".join(letters) + " n) p", p=P)
                return a if r is None else a[r[0]:r[1], :]
            table = [(0, ADA_B, "ada_b", None), (0, C_S, "c", None),
                     (1, K_K, "rw_k_k", None), (1, K_A, "rw_k_a", None), (1, R_K, "rw_r_k", None),
                     (1, W0, "rw_w0", None), (1, A0, "rw_a0", None), (1, LN_W, "rw_ln_w", None),
                     (1, LN_B, "rw_ln_b", None),
                     (1, MU0, "rw_mu", (0, 24)), (1, MUL0, "rw_mu", (24, 27)), (1, MU1, "rw_mu", (27, 51)),
                     (1, MUL1, "rw_mu", (51, 54)),
                     (2, G1, "norm1_g", None), (2, G2, "norm2_g", None), (2, LB0, "hg_lb", None),
                     (2, HGN, "hg_norm_g", None)]
            n = 0
            for t, r, name, cut in table:
                v = rowv(name, cut)
                sp.dma_start(rows[r:r + v.shape[0], t, :], v).then_inc(s_par, 16)
                n += 1
            sp.dma_start(rows[C_P:C_P + KT, 0, :], I["c_ctx"].rearrange("(n p) -> n p", p=P)).then_inc(s_par, 16)
            assert n + 1 == 18
            for t in range(TT):
                src = I["x_sample"][0, t * P:(t + 1) * P, :] if t < TT - 1 else I["x_prompt"][0]
                sp.dma_start(xt[:, t, :], src).then_inc(s_x, 16)
            w = I["ada_w"][0].rearrange("(k p) n -> p k n", p=P)
            for r in range(RING):
                sp.dma_start(ring[r][:, :, :], w[:, :, r * CT * P:(r + 1) * CT * P]).then_inc(s_ada[r], 16)
            with sp.Fori(1, NBLK // RING) as i:
                for r in range(RING):
                    sp.wait_ge(s_adaf[r], i)
                    sp.dma_start(ring[r][:, :, :], w[:, :, bass.ds((i * RING + r) * (CT * P), CT * P)]).then_inc(s_ada[r], 16)

        @block.gpsimd
        def _(pool):
            C = S["consts"]
            steps = [0]

            def link(ins):
                steps[0] += 1
                ins.then_inc(s_id, 1)
                pool.wait_ge(s_id, steps[0])
            link(nc.gpsimd.memset(C["ident"][:, :], 0.0))
            link(nc.gpsimd.affine_select(out=C["ident"][:, :], in_=C["ident"][:, :], compare_op=ALU.not_equal, fill=1.0,
                                         base=0, pattern=[[-1, P]], channel_multiplier=1))
            nc.gpsimd.memset(eps[:, :], EPS).then_inc(s_const, 1)

        @block.tensor
        def _(pe):
            ident = S["consts"]["ident"]
            pe.wait_ge(s_id, 2)
            pe.wait_ge(s_par, 18 * 16)
            for t, n in enumerate((128, 126, 72)):
                mm = nc.tensor.transpose(ps[:, 1 + t, 0:n], rows[0:n, t, :], ident[0:n, 0:n])
            mm.then_inc(s_ptr, 1)
            pe.wait_ge(s_cond, 1)
            with pe.Fori(0, NBLK // RING) as i:
                for r in range(RING):
                    pe.wait_ge(s_ada[r], i * 16 + 16)
                    for ct in range(CT):
                        for k in range(KT):
                            mm = nc.tensor.matmul(ps[:, 0, bass.ds((i * RING + r) * (2 * CT) + 2 * ct, 2)],
                                                  ring[r][:, k, ct * P:(ct + 1) * P], cond[:, k, :],
                                                  start=(k == 0), stop=(k == KT - 1))
                    mm.then_inc(s_adaf[r], 1)
            pe.wait_ge(s_xn, TT)
            for j in range(KT):
                b = 4 + 2 * (j % 2)
                if j >= 2:
                    pe.wait_ge(s_h, 2 * (j - 1))
                for t in range(TT):
                    bank = ps[:, b, t * P:(t + 1) * P] if t < TT - 1 else ps[:, b + 1, 0:P]
                    mm = nc.tensor.transpose(bank, xt[:, t, j * P:(j + 1) * P], ident[:, :])
                mm.then_inc(s_xT, 1)

        @block.scalar
        def _(act):
            act.wait_ge(s_const, 1)
            act.wait_ge(s_ptab, 3)
            nc.scalar.activation(th[:, :], S["ptab"][:, 0, C_S:C_S + 2 * KT], ACT.Tanh, scale=0.5).then_inc(s_th, 1)
            for t in range(TT):
                act.wait_ge(s_x, 16 * TT)
                if t:
                    act.wait_ge(s_ssq, t)
                nc.scalar.activation(junk[:, :], xt[:, t, :], ACT.Square, accum_out=ssq[:, t:t + 1]).then_inc(s_ssq, 1)
            act.wait_ge(s_ssq, TT)
            nc.scalar.activation(std[:, :], ssq[:, :], ACT.Sqrt, scale=1.0 / D, bias=eps[:, 0:1]).then_inc(s_std, 1)

        @block.vector
        def _(dve):
            steps = [0]

            def link(ins):
                steps[0] += 1
                ins.then_inc(s_v, 1)
                dve.wait_ge(s_v, steps[0])
            ptab, modT, A1, A2 = S["ptab"], S["modT"], S["A1"], S["A2"]
            dve.wait_ge(s_ptr, 1)
            for t, n in enumerate((128, 126, 72)):
                nc.vector.tensor_copy(ptab[:, t, 0:n], ps[:, 1 + t, 0:n]).then_inc(s_ptab, 1)
            dve.wait_ge(s_ptab, 3)
            dve.wait_ge(s_th, 1)
            link(nc.vector.tensor_scalar(th[:, :], th[:, :], 0.5, 0.5, ALU.mult, ALU.add))
            nc.vector.tensor_tensor(cond[:, :, :].rearrange("p k s -> p s k"), th[:, :].rearrange("p (s k) -> p s k", s=2),
                                    ptab[:, 0, C_S:C_S + 2 * KT].rearrange("p (s k) -> p s k", s=2), ALU.mult).then_inc(s_cond, 1)
            dve.wait_ge(s_std, 1)
            link(nc.vector.reciprocal(rstd[:, :], std[:, :]))
            for t in range(TT):
                nc.vector.tensor_scalar(xt[:, t, :], xt[:, t, :], rstd[:, t:t + 1], None, ALU.mult).then_inc(s_xn, 1)
            for r in range(RING):
                dve.wait_ge(s_adaf[r], NBLK // RING)
            link(nc.vector.tensor_tensor(modT[:, :, :], mod, bcast(ptab[:, 0, 0:96], 2, 2), ALU.add))
            for A, c, g in ((A1, KT, G1), (A2, 4 * KT, G2)):
                link(nc.vector.scalar_tensor_tensor(out=A[:, :, :], in0=modT[:, c:c + KT, :], scalar=1.0,
                                                    in1=bcast(ptab[:, 2, g:g + KT], 2, 2), op0=ALU.add, op1=ALU.mult))
            for j in range(KT):
                dve.wait_ge(s_xT, j + 1)
                b = 4 + 2 * (j % 2)
                nc.vector.tensor_scalar(S["hT"][:, j, 0:NS], ps[:, b, :], A1[:, j, 0:1], modT[:, j, 0:1],
                                        ALU.mult, ALU.add).then_inc(s_h, 1)
                nc.vector.tensor_scalar(S["hT"][:, j, NS:T], ps[:, b + 1, 0:NP], A1[:, j, 1:2], modT[:, j, 1:2],
                                        ALU.mult, ALU.add).then_inc(s_h, 1)
            dve.wait_ge(s_h, 2 * KT)


GROUPS = ((0, 4), (4, 4), (8, 2))
HALF = T // 2
LEVELS = 5


def half_view(ps, b):
    return ps[:, b:b + 2, 0:HALF]


def as_halves(ap):
    return ap.rearrange("p (a n) -> p a n", a=2)


def chunks(ap):
    return ap.rearrange("p (c l) -> p c l", l=L)


def stage_masks(nc, S):
    with ExitStack() as ctx:
        s_m = ctx.enter_context(nc.semaphore("mask_steps"))
        block = ctx.enter_context(nc.Block())
        C = S["consts"]

        @block.gpsimd
        def _(pool):
            n = [0]

            def link(ins):
                n[0] += 1
                ins.then_inc(s_m, 1)
                pool.wait_ge(s_m, n[0])

            def sel(ap, op, base, pattern, cm):
                link(nc.gpsimd.affine_select(out=ap, in_=ap, compare_op=op, fill=0.0, base=base, pattern=pattern,
                                             channel_multiplier=cm))
            bd = C["bd"]
            link(nc.gpsimd.memset(bd[:, :, :, :], 1.0))
            link(nc.gpsimd.memset(bd[:, 3:5, :, :], -1.0))
            for m in range(5):
                sel(bd[:, m], ALU.is_ge, 0, [[-L, 2], [0, L]], 1)
                sel(bd[:, m], ALU.is_ge, L - 1, [[L, 2], [0, L]], -1)
            sel(bd[:, 1], ALU.is_gt, 0, [[L, 2], [1, L]], -1)
            sel(bd[:, 2], ALU.is_gt, 0, [[-L, 2], [-1, L]], 1)
            sel(bd[:, 3], ALU.is_gt, 0, [[L, 2], [1, L]], -1)
            sel(bd[:, 4], ALU.is_gt, 0, [[-L, 2], [-1, L]], 1)
            cm = C["cm"]
            link(nc.gpsimd.memset(cm[:, :, :], 1.0))
            link(nc.gpsimd.memset(cm[:, 0, :], -1.0))
            link(nc.gpsimd.memset(cm[:, 2, :], -1.0))
            for h in range(2):
                q = slice(L * h, L * h + L)
                sel(cm[q, 0, :], ALU.is_gt, 0, [[1, L]], -1)
                sel(cm[q, 1, :], ALU.is_ge, 0, [[1, L]], -1)
                sel(cm[q, 2, :], ALU.is_gt, 0, [[-1, L]], 1)
                sel(cm[q, 3, :], ALU.is_ge, 0, [[-1, L]], 1)
            link(nc.gpsimd.memset(C["ci"][:, :], 0.0))
            for h in range(2):
                link(nc.gpsimd.affine_select(out=C["ci"][L * h:L * h + L, :], in_=C["ci"][L * h:L * h + L, :],
                                             compare_op=ALU.not_equal, fill=1.0, base=0, pattern=[[-1, L]],
                                             channel_multiplier=1))
            link(nc.gpsimd.memset(C["ns"][:, :], 1.0))
            link(nc.gpsimd.memset(chunks(C["ns"][:, :])[:, :, 0:1], 0.0))
            link(nc.gpsimd.memset(C["ones"][:, :], 1.0))
            link(nc.gpsimd.memset(C["eps"][:, 0:1], EPS))
            link(nc.gpsimd.memset(C["eps"][:, 1:2], LN_EPS))


def mix_neighbours(nc, link, out, raw, c, mu0, mu1):
    link(nc.vector.tensor_scalar(out, raw, c, None, ALU.mult))
    for cut, w in ((slice(0, NS), GRID_W), (slice(NS, T), NP)):
        o, r = (a[:, cut].rearrange("p (n w) -> p n w", w=w) for a in (out, raw))
        link(nc.vector.scalar_tensor_tensor(out=o[:, :, 1:w], in0=r[:, :, 0:w - 1], scalar=mu0, in1=o[:, :, 1:w],
                                            op0=ALU.mult, op1=ALU.add))
        link(nc.vector.scalar_tensor_tensor(out=o[:, :, 0:w - 1], in0=r[:, :, 1:w], scalar=mu1, in1=o[:, :, 0:w - 1],
                                            op0=ALU.mult, op1=ALU.add))


def stage_lora(nc, I, S):
    with ExitStack() as ctx:
        sb = lambda name, shape, dt=F32: ctx.enter_context(nc.sbuf_tensor(name, shape, dt))
        sg = lambda name: ctx.enter_context(nc.semaphore(name))
        w = sb("wlora", [P, KT, 3 * P])
        raw = sb("rawlora", [P, 3, T])
        cl = sb("clora", [P, 3])
        ps = ctx.enter_context(nc.psum_tensor("psL", [P, 8, 512], F32))
        s_w, s_p, s_raw, s_v, s_mix, s_th, s_z, s_out = map(sg, (
            "lora_w_in", "lora_projected", "lora_raw", "lora_vec", "lora_mixed", "lora_tanh", "lora_zeroed", "lora_rows"))
        block = ctx.enter_context(nc.Block())
        lora = S["lora"]

        @block.sync
        def _(sp):
            sp.dma_start(w[:, :, :], I["w_in"][0].rearrange("(k p) n -> p k n", p=P)[:, :, 3 * RW_DIM:RW_COLS]).then_inc(s_w, 16)

        @block.gpsimd
        def _(pool):
            nc.gpsimd.memset(S["lw"][:, :, :, :], 0.0).then_inc(s_z, 1)
            pool.wait_ge(s_z, 1)

        @block.tensor
        def _(pe):
            pe.wait_ge(s_w, 16)
            for i in range(3):
                for h in range(2):
                    for k in range(KT):
                        mm = nc.tensor.matmul(ps[:, 2 * i + h, 0:HALF], w[:, k, i * P:(i + 1) * P],
                                              S["hT"][:, k, h * HALF:(h + 1) * HALF], start=(k == 0), stop=(k == KT - 1))
                mm.then_inc(s_p, 1)

        @block.scalar
        def _(act):
            for i in range(3):
                act.wait_ge(s_p, i + 1)
                nc.scalar.activation(as_halves(raw[:, i, :]), half_view(ps, 2 * i), ACT.Copy).then_inc(s_raw, 1)
            act.wait_ge(s_mix, 1)
            nc.scalar.activation(lora[:, 0, :], lora[:, 0, :], ACT.Tanh).then_inc(s_th, 1)
            nc.scalar.activation(lora[:, 2, :], lora[:, 2, :], ACT.Tanh, scale=0.5).then_inc(s_th, 1)

        @block.vector
        def _(dve):
            steps = [0]

            def link(ins):
                steps[0] += 1
                ins.then_inc(s_v, 1)
                dve.wait_ge(s_v, steps[0])
            t1 = S["ptab"][:, 1, :]
            link(nc.vector.tensor_tensor(cl[:, :], t1[:, MUL0:MUL0 + 3], t1[:, MUL1:MUL1 + 3], ALU.add))
            link(nc.vector.tensor_scalar(cl[:, :], cl[:, :], -1.0, 1.0, ALU.mult, ALU.add))
            for i in range(3):
                dve.wait_ge(s_raw, i + 1)
                mix_neighbours(nc, link, lora[:, i, :], raw[:, i, :], cl[:, i:i + 1], t1[:, MUL0 + i:MUL0 + i + 1],
                               t1[:, MUL1 + i:MUL1 + i + 1])
            dve.sem_inc(s_mix, 1)
            dve.wait_ge(s_th, 2)
            link(nc.vector.tensor_scalar(lora[:, 2, :], lora[:, 2, :], 0.5, 0.5, ALU.mult, ALU.add))


def stage_rwkv(nc, I, O, S, per):
    with ExitStack() as ctx:
        sb = lambda name, shape, dt=F32: ctx.enter_context(nc.sbuf_tensor(name, shape, dt))
        C = S["consts"]
        sig = {}

        def signal(name):
            if name not in sig:
                sig[name] = Signal(ctx, nc, "rw_" + name, per.get(name, 0))
            return sig[name]
        w = sb("wrkv", [P, 3, KT, P])
        raw = sb("raw", [P, 3, T])
        mix = sb("mix", [P, 3, T])
        kk, kds, ysum = sb("kk", [P, T]), sb("kds", [P, T]), sb("ysum", [P, T])
        t1, t2, t3, t4, t5 = (sb(f"t{i}", [P, T]) for i in range(1, 6))
        outr = sb("outr", [P, T])
        t6, t7, t8 = (raw[:, i, :] for i in range(3))
        pp, dp, tot, etot = sb("pp", [P, 15]), sb("dp", [P, 9]), sb("tot", [P, NCH]), sb("etot", [P, NCH])
        KR = sb("KR", [P, NCH, 2, L])
        cB = sb("cB", [P, NCH, L])
        bdB, bdK, bdKW, bdBn, bdKn, bdV = (sb(n, [P, NCH, 2, L]) for n in ("bdB", "bdK", "bdKW", "bdBn", "bdKn", "bdV"))
        cV, RbT, RkT, TTc, cN = (sb(n, [P, NCH, L]) for n in ("cV", "RbT", "RkT", "TTc", "cN"))
        bdAk, bdTT, bdNT = (sb(n, [P, NCH, 2, L]) for n in ("bdAk", "bdTT", "bdNT"))
        bdN = bdTT
        Sc, bdS, nR, cSA, bdSA = (sb("Sc", [P, 2, L]), sb("bdS", [P, 2, 2, L]), sb("nR", [P, L]), sb("cSA", [P, L]),
                                  sb("bdSA", [P, 2, L]))
        s0 = sb("s0", [P, 2, L])
        sout = sb("sout", [P, 2, L])
        ps = ctx.enter_context(nc.psum_tensor("psR", [P, 8, 512], F32))
        block = ctx.enter_context(nc.Block())
        g2 = S["lw"]
        lora = S["lora"]
        ident = C["ident"][:, :]
        blk = C["bd"][:, 0]
        blockones = blk.rearrange("p g l -> p (g l)")

        def bank(b, n, width):
            return ps[:, b, 0:n * width].rearrange("p (c l) -> p c l", l=width)
        GB = (4, 5, 6)

        def sq_view(g, n):
            return ps[:, GB[g], 0:n * L].rearrange("p (c l) -> p c l", l=L)

        def tt_view(g, n):
            return ps[:, GB[g], n * L:2 * n * L].rearrange("p (c l) -> p c l", l=L)

        def tr_view(g, n):
            return ps[:, 7, 0:n * P].rearrange("p (c l) -> p c l", l=P)

        def chain():
            return lambda d: [(c, c == 0, c == 7) if d == 0 else (7 - c, c == 0, c == 7) for c in range(8)] + \
                [(8 + e if d == 0 else 9 - e, e == 0, e == 1) for e in range(2)]
        steps_of = chain()

        @block.sync
        def _(sp):
            win = I["w_in"][0].rearrange("(k p) n -> p k n", p=P)
            rw = lambda n: signal(n)
            sp.sem_inc(rw("final_free").sem, 3)
            with sp.Fori(0, PAIRS) as r:
                sp.wait_ge(rw("w_free").sem, r * rw("w_free").per + 1)
                for i in range(3):
                    sp.dma_start(w[:, i, :, :], win[:, :, bass.ds(i * RW_DIM + r * P, P)]).then_inc(rw("w_in").sem, 16)
                sp.wait_ge(rw("lw_free").sem, r * rw("lw_free").per + 1)
                for j, name in enumerate(("rw_w2", "rw_a2")):
                    for d in range(2):
                        sp.dma_start(g2[L * d:L * d + L, j, d, :], I[name][0, d][:, bass.ds(r * P, P)]).then_inc(rw("lw_in").sem, 16)
                sp.dma_start(g2[:, 2, 0, :], I["rw_g2"][0][:, bass.ds(r * P, P)]).then_inc(rw("lw_in").sem, 16)
                for d in range(2):
                    sp.wait_ge(rw("s0_free").sem, r * 2 + d + 1)
                    sp.dma_start(s0[:, d, :], I["state_rwkv"][0, 0, d].rearrange("h v k -> (h v) k")[bass.ds(r * P, P), :])\
                        .then_inc(rw(f"s0_in{d}").sem, 16)
                for d in range(2):
                    sp.wait_ge(rw("final_ready").sem, r * 2 + d + 1)
                    sp.dma_start(O["new_state_rwkv"][0, 0, d].rearrange("h v k -> (h v) k")[bass.ds(r * P, P), :], sout[:, d, :])\
                        .then_inc(rw("final_out").sem, 16)
                    sp.wait_ge(rw("final_out").sem, r * 48 + 16 * (d + 1))
                    sp.sem_inc(rw("final_free").sem, 1)
                sp.wait_ge(rw("round_done").sem, r + 1)
                sp.dma_start(S["outr"][bass.ds(r, 1)].rearrange("o p n -> (o p) n"), outr[:, :]).then_inc(rw("final_out").sem, 16)
                sp.wait_ge(rw("final_out").sem, r * 48 + 48)
                sp.sem_inc(rw("final_free").sem, 1)

        @block.gpsimd
        def _(pool):
            nc.gpsimd.memset(bdK[:, :, :, :], 0.0).then_inc(signal("bdk_zeroed").sem, 1)
            with pool.Fori(0, PAIRS) as r:
                for d in range(2):
                    def bd(out, src, need):
                        pool.wait_ge(signal("factors").sem, signal("factors").at(4 * d + need, r))
                        nc.gpsimd.tensor_tensor(out[:, :, :, :], bcast(src, 2, 2), bcast(blk, NCH, 1), ALU.mult)\
                            .then_inc(signal("bd_factors").sem, 1)
                    bd(bdKW, KR[:, :, 0, :], 1)
                    bd(bdB, cB[:, :, :], 3)
                    bd(bdK, chunks(t3[:, :]), 4)

        @block.tensor
        def _(pe):
            W = lambda name, n, r: pe.wait_ge(signal(name).sem, signal(name).at(n, r))
            cnt = {}

            def inc(mm, name):
                mm.then_inc(signal(name).sem, 1)
                cnt[name] = cnt.get(name, 0) + 1
            pe.sem_inc(signal("w_free").sem, 1)
            pe.sem_inc(signal("lw_free").sem, 1)
            with pe.Fori(0, PAIRS) as r:
                cnt.clear()

                def sums(lhsT, rhs, b):
                    for h in range(2):
                        mm = nc.tensor.matmul(ps[:, b + h, 0:HALF], lhsT, rhs[:, h * HALF:(h + 1) * HALF], start=True, stop=True)
                    return mm
                pe.wait_ge(signal("w_in").sem, r * 48 + 48)
                for i in range(3):
                    if i == 2:
                        W("raw_ready", 1, r)
                    for h in range(2):
                        for k in range(KT):
                            mm = nc.tensor.matmul(ps[:, 2 * (i % 2) + h, 0:HALF], w[:, i, k, :],
                                                  S["hT"][:, k, h * HALF:(h + 1) * HALF], start=(k == 0), stop=(k == KT - 1))
                    if i == 2:
                        mm.then_inc(signal("projected").sem, 1)
                    else:
                        mm.then_inc(signal("projected").sem, 1)
                cnt["projected"] = 3
                pe.wait_ge(signal("projected").sem, signal("projected").at(3, r))
                pe.sem_inc(signal("w_free").sem, 1)
                cnt["w_free"] = 1
                W("kk_squares", 1, r)
                inc(sums(blockones, t1[:, :], 4), "kk_sums")
                W("v_spread", 2, r)
                W("kk_max", 1, r)
                for g, (c0, n) in enumerate(GROUPS):
                    for c in range(c0, c0 + n):
                        mm = nc.tensor.transpose(ps[:, 4 + g, (c - c0) * P:(c - c0 + 1) * P], bdK[:, c].rearrange("p g l -> p (g l)"), ident)
                    inc(mm, "v_turned")
                W("bdv_ready", 3, r)
                pe.wait_ge(signal("lw_in").sem, r * 80 + 80)
                for d in range(2):
                    if d:
                        W("y_taken", 1, r)
                        W("final_taken", 1, r)
                    sums(g2[:, 0, d, :], lora[:, 0, :], 4)
                    inc(sums(g2[:, 1, d, :], lora[:, 1, :], 6), "lora_sums")
                    W("lora_taken", 2 * d + 2, r)
                    W("bd_factors", 3 * d + 3, r)
                    flat = lambda a, c: a[:, c].rearrange("p g l -> p (g l)")
                    for g, (c0, n) in enumerate(GROUPS):
                        if g:
                            W("grams_taken", 3 * d + g, r)
                        for b, lhs in ((4, bdB), (5, bdK)):
                            for c in range(c0, c0 + n):
                                nc.tensor.matmul(ps[:, b, (c - c0) * P:(c - c0 + 1) * P], flat(lhs, c), flat(KR, c), start=True, stop=True)
                        for c in range(c0, c0 + n):
                            mm = nc.tensor.matmul(ps[:, 6, (c - c0) * L:(c - c0 + 1) * L], flat(bdKW, c), cB[:, c, :], start=True, stop=True)
                        inc(mm, "grams")
                        for b, src in ((7, bdB), (7, bdK)):
                            k = 6 * d + 2 * g + (src is bdK)
                            if k:
                                W("rows_taken", k, r)
                            for c in range(c0, c0 + n):
                                mm = nc.tensor.transpose(ps[:, b, (c - c0) * P:(c - c0 + 1) * P], flat(src, c), ident)
                            inc(mm, "rows_turned")
                    W("grams_taken", 3 * d + 3, r)
                    W("rows_taken", 6 * d + 6, r)
                    for i in range(LEVELS):
                        last = i == LEVELS - 1
                        for g, (c0, n) in enumerate(GROUPS):
                            if i:
                                W("bdnt_ready", 4 * 3 * d + 3 * (i - 1) + g + 1, r)
                                W("cn_ready", 2 * (12 * d + 3 * (i - 1) + g + 1), r)
                                W("tt_ready", 15 * d + 3 * (i - 1) + g + 1, r)
                            for c in range(c0, c0 + n):
                                mm = nc.tensor.matmul(sq_view(g, n)[:, c - c0, :], flat(bdNT, c), cN[:, c, :], start=True, stop=True)
                            inc(mm, "squared")
                        for g, (c0, n) in enumerate(GROUPS):
                            k = 15 * d + 3 * i + g + 1
                            W("bdn_ready", k, r)
                            for c in range(c0, c0 + n):
                                mm = nc.tensor.matmul(tt_view(g, n)[:, c - c0, :], flat(bdN, c), TTc[:, c, :], start=True, stop=True)
                            inc(mm, "tt_sums")
                            if not last:
                                if g:
                                    W("bdnt_ready", 12 * d + 3 * i + g, r)
                                for c in range(c0, c0 + n):
                                    mm = nc.tensor.transpose(tr_view(g, n)[:, c - c0, :], flat(bdN, c), ident)
                                inc(mm, "n_turned")
                    W("bdtt_ready", 3 * d + 3, r)
                    W("s0_spread", d + 1, r)
                    inc(nc.tensor.transpose(ps[:, 4, 0:P], bdSA[:, :, :].rearrange("p g l -> p (g l)"), ident), "s0_turned")
                    Yv = lambda c: ps[:, 6, c * L:(c + 1) * L] if c < 8 else ps[:, 7, (c - 8) * L:(c - 7) * L]
                    for j, (c, first, lastc) in enumerate(steps_of(d)):
                        hs = c < 8 or not first
                        q = j % 2
                        k = 10 * d + j + 1
                        if j == 0:
                            W("s0_ready", d + 1, r)
                        else:
                            W("state_ready", k - 1, r)
                        mm = nc.tensor.matmul(ps[:, 4, P:P + L], flat(bdAk, c), cV[:, c, :], start=True, stop=not hs)
                        if hs:
                            mm = nc.tensor.matmul(ps[:, 4, P:P + L], flat(bdKW, c), Sc[:, q, :], start=False, stop=True)
                        inc(mm, "r_sums")
                        W("nr_ready", k, r)
                        inc(nc.tensor.matmul(ps[:, 5, 0:L], flat(bdTT, c), nR[:, :], start=True, stop=True), "sa_sums")
                        W("sa_ready", 2 * k, r)
                        nc.tensor.matmul(ps[:, 5, P:P + L], flat(bdBn, c), cSA[:, :], start=True, stop=False)
                        if hs:
                            nc.tensor.matmul(ps[:, 5, P:P + L], ident, Sc[:, q, :], start=False, stop=False)
                        inc(nc.tensor.matmul(ps[:, 5, P:P + L], flat(bdKn, c), cV[:, c, :], start=False, stop=True), "state_sums")
                        nc.tensor.matmul(Yv(c), flat(bdV, c), RkT[:, c, :], start=True, stop=False)
                        if hs:
                            nc.tensor.matmul(Yv(c), bdS[:, q].rearrange("p g l -> p (g l)"), KR[:, c, 1, :], start=False, stop=False)
                        inc(nc.tensor.matmul(Yv(c), bdSA[:, :, :].rearrange("p g l -> p (g l)"), RbT[:, c, :], start=False, stop=True), "y_sums")
                    W("state_ready", 10 * d + 10, r)
                    inc(nc.tensor.transpose(ps[:, 4, 0:P], bdS[:, 0].rearrange("p g l -> p (g l)"), ident), "final_turned")
                W("y_taken", 2, r)
                W("final_taken", 2, r)
                W("bonus_products", 1, r)
                inc(sums(blockones, t1[:, :], 4), "bonus_sums")
                inc(sums(blockones, ysum[:, :], 6), "mean_sums")
                W("bonus_ready", 1, r)
                inc(sums(g2[:, 2, 0, :], lora[:, 2, :], 4), "gate_sums")
                W("y_squares", 1, r)
                inc(sums(blockones, t2[:, :], 6), "var_sums")
                pe.wait_ge(signal("var_sums").sem, signal("var_sums").at(1, r))
                pe.sem_inc(signal("lw_free").sem, 1)
                W("round_done", 1, r)
                for n in cnt:
                    assert True
            S["pe_cnt"] = dict(cnt)

        @block.scalar
        def _(act):
            W = lambda name, n, r: act.wait_ge(signal(name).sem, signal(name).at(n, r))
            cnt = {}

            def inc(ins, name):
                ins.then_inc(signal(name).sem, 1)
                cnt[name] = cnt.get(name, 0) + 1
            act.wait_ge(signal("bdk_zeroed").sem, 1)
            with act.Fori(0, PAIRS) as r:
                cnt.clear()
                A = nc.scalar.activation
                for i in range(3):
                    W("projected", i + 1, r)
                    W("raw_free", 1, r)
                    inc(A(as_halves(raw[:, i, :]), half_view(ps, 2 * (i % 2)), ACT.Copy), "raw_ready")
                W("mixed", 3, r)
                for h in range(2):
                    q = slice(L * h, L * h + L)
                    inc(A(bdK[q, :, h, :], chunks(mix[q, 2, :]), ACT.Copy), "v_spread")
                W("kk_raw", 1, r)
                inc(A(t1[:, :], kk[:, :], ACT.Square), "kk_squares")
                W("kk_max", 1, r)
                inc(A(t2[:, :], t2[:, :], ACT.Sqrt), "kk_root")
                for g, (c0, n) in enumerate(GROUPS):
                    W("v_turned", g + 1, r)
                    inc(A(bdV[:, c0:c0 + n].rearrange("p c g l -> p c (g l)"), bank(4 + g, n, P), ACT.Copy), "bdv_ready")
                for d in range(2):
                    W("lora_sums", d + 1, r)
                    if d == 0:
                        W("kk_ready", 1, r)
                    W("derived", 1, r)
                    inc(A(as_halves(t1[:, :]), half_view(ps, 4), ACT.Tanh, scale=0.5, bias=dp[:, 3 + d:4 + d]), "lora_taken")
                    if d:
                        W("bd_factors", 3, r)
                    inc(A(as_halves(t2[:, :]), half_view(ps, 6), ACT.Tanh, scale=0.5, bias=dp[:, 5 + d:6 + d]), "lora_taken")
                    W("logs", d + 1, r)
                    inc(A(etot[:, :], tot[:, :], ACT.Exp), "exps")
                    inc(A(t6, t5[:, :], ACT.Exp), "exps")
                    inc(A(t7, t4[:, :], ACT.Exp), "exps")
                    inc(A(t8, t4[:, :], ACT.Exp, scale=-1.0), "exps")
                    for g, (c0, n) in enumerate(GROUPS):
                        for m, out in enumerate((bdBn, bdKn)):
                            W("rows_turned", 6 * d + 2 * g + m + 1, r)
                            inc(A(out[:, c0:c0 + n].rearrange("p c g l -> p c (g l)"), bank(7, n, P), ACT.Copy), "rows_taken")
                    for i in range(LEVELS - 1):
                        for g, (c0, n) in enumerate(GROUPS):
                            W("bdn_ready", 15 * d + 3 * i + g + 1, r)
                            for h in range(2):
                                q = slice(L * h, L * h + L)
                                inc(A(cN[q, c0:c0 + n, :], bdN[q, c0:c0 + n, h, :], ACT.Copy), "cn_ready")
                        for g, (c0, n) in enumerate(GROUPS):
                            W("n_turned", 12 * d + 3 * i + g + 1, r)
                            inc(A(bdNT[:, c0:c0 + n].rearrange("p c g l -> p c (g l)"), tr_view(g, n), ACT.Copy), "bdnt_ready")
                    for j in range(10):
                        k = 10 * d + j + 1
                        W("r_sums", k, r)
                        inc(A(nR[:, :], ps[:, 4, P:P + L], ACT.Copy, scale=-1.0), "nr_ready")
                W("y_squares_in", 1, r)
                inc(A(t2[:, :], t4[:, :], ACT.Square), "y_squares")
                W("var_sums", 1, r)
                inc(A(as_halves(t5[:, :]), half_view(ps, 6), ACT.Sqrt, scale=1.0 / L, bias=C["eps"][:, 1:2]), "ln_root")
            S["act_cnt"] = dict(cnt)

        @block.vector
        def _(dve):
            W = lambda name, n, r: dve.wait_ge(signal(name).sem, signal(name).at(n, r))
            V = nc.vector
            dve.sem_inc(signal("raw_free").sem, 1)
            dve.sem_inc(signal("s0_free").sem, 2)
            cnt = {}
            with dve.Fori(0, PAIRS) as r:
                cnt.clear()

                def did(ins, name):
                    cnt[name] = cnt.get(name, 0) + 1
                    ins.then_inc(signal(name).sem, 1)
                    dve.wait_ge(signal(name).sem, signal(name).at(cnt[name], r))
                link = lambda ins: did(ins, "vector_line")

                def raised(name, k=1):
                    dve.sem_inc(signal(name).sem, k)
                    cnt[name] = cnt.get(name, 0) + k
                link(V.tensor_copy(pp[:, :], S["ptab"][:, 1, 0:120].rearrange("p (n e) -> p n e", e=PAIRS)[:, :, bass.ds(r, 1)].rearrange("p n e -> p (n e)")))
                link(V.tensor_tensor(dp[:, 0:3], pp[:, 0:3], pp[:, 3:6], ALU.add))
                link(V.tensor_scalar(dp[:, 0:3], dp[:, 0:3], -1.0, 1.0, ALU.mult, ALU.add))
                link(V.tensor_scalar(dp[:, 3:7], pp[:, 9:13], 0.5, None, ALU.mult))
                link(V.tensor_scalar(dp[:, 7:8], pp[:, 7:8], 0.5, None, ALU.mult))
                did(V.tensor_scalar(dp[:, 8:9], pp[:, 7:8], -0.5, 1.0, ALU.mult, ALU.add), "derived")
                for i in range(3):
                    W("raw_ready", i + 1, r)
                    mix_neighbours(nc, link, mix[:, i, :], raw[:, i, :], dp[:, i:i + 1], pp[:, i:i + 1], pp[:, 3 + i:4 + i])
                    raised("mixed")
                rT, kT, vT = mix[:, 0, :], mix[:, 1, :], mix[:, 2, :]
                did(V.tensor_scalar(kk[:, :], kT, pp[:, 6:7], None, ALU.mult), "kk_raw")
                W("kk_sums", 1, r)
                did(V.tensor_scalar(as_halves(t2[:, :]), half_view(ps, 4), 1e-24, None, ALU.max), "kk_max")
                W("kk_root", 1, r)
                link(V.reciprocal(t2[:, :], t2[:, :]))
                did(V.tensor_tensor(kk[:, :], kk[:, :], t2[:, :], ALU.mult), "kk_ready")
                W("bdv_ready", 3, r)
                link(V.tensor_tensor(cV[:, :, :], bdV[:, :, 0, :], bdV[:, :, 1, :], ALU.add))
                for d in range(2):
                    mT, mI, mN = (1, 1, 2) if d == 0 else (2, 3, 1)
                    W("lora_taken", 2 * d + 2, r)
                    link(V.tensor_scalar(t1[:, :], t1[:, :], -0.5 * DECAY_SCALE, -0.5 * DECAY_SCALE, ALU.mult, ALU.add))
                    link(V.tensor_scalar(t3[:, :], t2[:, :], dp[:, 7:8], dp[:, 8:9], ALU.mult, ALU.add))
                    link(V.tensor_tensor(t3[:, :], t3[:, :], kT, ALU.mult))
                    if d == 0:
                        link(V.tensor_copy(kds[:, :], t3[:, :]))
                    else:
                        link(V.tensor_tensor(kds[:, :], kds[:, :], t3[:, :], ALU.add))
                    link(V.tensor_scalar(t2[:, :], t2[:, :], 0.5, 0.5, ALU.mult, ALU.add))
                    link(V.tensor_tensor(t2[:, :], t2[:, :], kk[:, :], ALU.mult))
                    link(V.tensor_tensor_scan(t4[:, :], C["ns"][:, :], t1[:, :], 0.0, ALU.mult, ALU.add))
                    link(V.tensor_copy(tot[:, :].rearrange("p (c o) -> p c o", o=1), chunks(t4[:, :])[:, :, L - 1:L]))
                    if d == 0:
                        did(V.tensor_tensor(t5[:, :], t4[:, :], t1[:, :], ALU.subtract), "logs")
                    else:
                        link(V.tensor_tensor(chunks(t5[:, :]), bcast(tot[:, :], L, 2), chunks(t4[:, :]), ALU.subtract))
                        did(V.tensor_tensor(t4[:, :], t5[:, :], t1[:, :], ALU.add), "logs")
                    W("exps", 4 * d + 4, r)
                    did(V.tensor_tensor(KR[:, :, 0, :], chunks(kk[:, :]), chunks(t6), ALU.mult), "factors")
                    did(V.tensor_tensor(KR[:, :, 1, :], chunks(rT), chunks(t7), ALU.mult), "factors")
                    did(V.tensor_tensor(cB[:, :, :], chunks(t2[:, :]), chunks(t8), ALU.mult), "factors")
                    did(V.tensor_tensor(t3[:, :], t3[:, :], t8, ALU.mult), "factors")
                    if d:
                        raised("raw_free")
                    for g, (c0, n) in enumerate(GROUPS):
                        cs = slice(c0, c0 + n)
                        W("grams", 3 * d + g + 1, r)
                        G1, G2, G3 = bank(4, n, P), bank(5, n, P), bank(6, n, L)
                        link(V.tensor_tensor(bdNT[:, cs], bcast(G1[:, :, 0:L], 2, 2), bcast(C["bd"][:, 2 + mT], n, 1), ALU.mult))
                        link(V.tensor_tensor(TTc[:, cs], G1[:, :, 0:L], bcast(C["cm"][:, 2 * d], n, 1), ALU.mult))
                        link(V.tensor_tensor(TTc[:, cs], TTc[:, cs], bcast(C["ci"][:, :], n, 1), ALU.add))
                        link(V.tensor_tensor(RbT[:, cs], G1[:, :, L:P], bcast(C["cm"][:, mI], n, 1), ALU.mult))
                        link(V.tensor_tensor(bdAk[:, cs], bcast(G2[:, :, 0:L], 2, 2), bcast(C["bd"][:, mT], n, 1), ALU.mult))
                        link(V.tensor_tensor(RkT[:, cs], G2[:, :, L:P], bcast(C["cm"][:, mI], n, 1), ALU.mult))
                        did(V.tensor_tensor(cN[:, cs], G3, bcast(C["cm"][:, 2 - 2 * d], n, 1), ALU.mult), "grams_taken")
                    for i in range(LEVELS):
                        for g, (c0, n) in enumerate(GROUPS):
                            W("squared", 15 * d + 3 * i + g + 1, r)
                            did(V.tensor_tensor(bdN[:, c0:c0 + n], bcast(sq_view(g, n), 2, 2), bcast(blk, n, 1), ALU.mult), "bdn_ready")
                        for g, (c0, n) in enumerate(GROUPS):
                            W("tt_sums", 15 * d + 3 * i + g + 1, r)
                            did(V.tensor_tensor(TTc[:, c0:c0 + n], TTc[:, c0:c0 + n], tt_view(g, n), ALU.add), "tt_ready")
                    for g, (c0, n) in enumerate(GROUPS):
                        did(V.tensor_tensor(bdTT[:, c0:c0 + n], bcast(TTc[:, c0:c0 + n], 2, 2), bcast(blk, n, 1), ALU.mult), "bdtt_ready")
                    dve.wait_ge(signal(f"s0_in{d}").sem, r * 16 + 16)
                    did(V.tensor_tensor(bdSA[:, :, :], bcast(s0[:, d, :], 2, 1), blk, ALU.mult), "s0_spread")
                    raised("s0_free")
                    W("s0_turned", d + 1, r)
                    link(V.tensor_copy(bdS[:, 0].rearrange("p g l -> p (g l)"), ps[:, 4, 0:P]))
                    did(V.tensor_tensor(Sc[:, 0, :], bdS[:, 0, 0, :], bdS[:, 0, 1, :], ALU.add), "s0_ready")
                    for j, (c, first, lastc) in enumerate(steps_of(d)):
                        k = 10 * d + j + 1
                        q = (j + 1) % 2
                        W("sa_sums", k, r)
                        if j:
                            W("y_sums", k - 1, r)
                        did(V.tensor_copy(cSA[:, :], ps[:, 5, 0:L]), "sa_ready")
                        did(V.tensor_tensor(bdSA[:, :, :], bcast(ps[:, 5, 0:L], 2, 1), blk, ALU.mult), "sa_ready")
                        W("state_sums", k, r)
                        link(V.tensor_scalar(Sc[:, q, :], ps[:, 5, P:P + L], etot[:, c:c + 1], None, ALU.mult))
                        did(V.scalar_tensor_tensor(out=bdS[:, q], in0=bcast(ps[:, 5, P:P + L], 2, 1), scalar=etot[:, c:c + 1],
                                                   in1=blk, op0=ALU.mult, op1=ALU.mult), "state_ready")
                    W("y_sums", 10 * d + 10, r)
                    if d == 0:
                        link(V.tensor_copy(ysum[:, 0:NS], ps[:, 6, :]))
                        did(V.tensor_copy(ysum[:, NS:T], ps[:, 7, 0:NP]), "y_taken")
                    else:
                        link(V.tensor_tensor(ysum[:, 0:NS], ysum[:, 0:NS], ps[:, 6, :], ALU.add))
                        did(V.tensor_tensor(ysum[:, NS:T], ysum[:, NS:T], ps[:, 7, 0:NP], ALU.add), "y_taken")
                    W("final_turned", d + 1, r)
                    link(V.tensor_copy(bdSA[:, :, :].rearrange("p g l -> p (g l)"), ps[:, 4, 0:P]))
                    raised("final_taken")
                    W("final_free", d + 1, r)
                    did(V.tensor_tensor(sout[:, d, :], bdSA[:, 0, :], bdSA[:, 1, :], ALU.add), "final_ready")
                link(V.tensor_tensor(t1[:, :], kds[:, :], rT, ALU.mult))
                did(V.tensor_scalar(t1[:, :], t1[:, :], pp[:, 8:9], None, ALU.mult), "bonus_products")
                W("mean_sums", 1, r)
                did(V.tensor_tensor(as_halves(t3[:, :]), half_view(ps, 4), as_halves(vT), ALU.mult), "bonus_ready")
                did(V.scalar_tensor_tensor(out=as_halves(t4[:, :]), in0=half_view(ps, 6), scalar=-1.0 / L,
                                           in1=as_halves(ysum[:, :]), op0=ALU.mult, op1=ALU.add), "y_squares_in")
                W("ln_root", 1, r)
                link(V.reciprocal(t5[:, :], t5[:, :]))
                link(V.tensor_tensor(t4[:, :], t4[:, :], t5[:, :], ALU.mult))
                link(V.tensor_scalar(t4[:, :], t4[:, :], pp[:, 13:14], pp[:, 14:15], ALU.mult, ALU.add))
                link(V.tensor_tensor(t4[:, :], t4[:, :], t3[:, :], ALU.add))
                W("gate_sums", 1, r)
                W("final_free", 3, r)
                did(V.tensor_tensor(as_halves(outr[:, :]), as_halves(t4[:, :]),
                                    half_view(ps, 4), ALU.mult), "round_done")
            S["dve_cnt"] = dict(cnt)
        S["sig"] = sig


HLEV = (1, 2, 4, 8, 16, 32, 64)
HKINDS = 5


def stage_hgrn(nc, I, O, S, per):
    with ExitStack() as ctx:
        sb = lambda name, shape, dt=F32: ctx.enter_context(nc.sbuf_tensor(name, shape, dt))
        C = S["consts"]
        sig = {}

        def signal(name):
            if name not in sig:
                sig[name] = Signal(ctx, nc, "hg_" + name, per.get("hg_" + name, 0))
            return sig[name]
        w = sb("whg", [P, HKINDS, KT, P])
        halfraw = sb("halfraw", [P, 3, T])
        th = sb("hth", [P, 4, T])
        vT, gh = halfraw[:, 1, :], halfraw[:, 2, :]
        q, sgate = sb("hq", [P, T]), sb("sgate", [P, T])
        key = [sb(f"key{d}", [P, T]) for d in range(2)]
        incl = [sb(f"incl{d}", [P, T]) for d in range(2)]
        excl = [sb(f"excl{d}", [P, T]) for d in range(2)]
        qs = [sb(f"qs{d}", [P, T]) for d in range(2)]
        ks = [sb(f"ks{d}", [P, T]) for d in range(2)]
        att = sb("att", [P, TT, P])
        kn = [sb(f"kn{d}", [P, TT, P]) for d in range(2)]
        vn = sb("vn", [P, TT, P])
        st = [sb(f"hst{d}", [P, TT - 1, P]) for d in range(2)]
        fin = sb("hfin", [P, 2, P])
        o1, rt, outh, osq = sb("o1", [P, T]), sb("hrt", [P, T]), sb("outh", [P, T]), sb("osq", [P, T])
        lbp = sb("lbp", [P, 3, 16])
        hm = sb("hmask", [P, 15, P])
        ps = ctx.enter_context(nc.psum_tensor("psH", [P, 8, 512], F32))
        s_m = ctx.enter_context(nc.semaphore("hg_mask_steps"))
        block = ctx.enter_context(nc.Block())
        wide = lambda b: ps[:, b:b + 2, :].rearrange("p a n -> p (a n)")[:, 0:T]

        def tok(ps_b, c):
            return ps[:, ps_b + c // 4, (c % 4) * P:(c % 4 + 1) * P]

        def seg(ap, m, half):
            return ap.rearrange("p (j a r) -> p j a r", a=2, r=m)[:, :, half, :]

        @block.sync
        def _(sp):
            win = I["w_in"][0].rearrange("(k p) n -> p k n", p=P)
            sp.sem_inc(signal("fin_free").sem, 1)
            with sp.Fori(0, HG_HEADS) as r:
                sp.wait_ge(signal("w_free").sem, r + 1)
                for i in range(HKINDS):
                    sp.dma_start(w[:, i, :, :], win[:, :, bass.ds(HG0 + i * HG_DIM + r * P, P)]).then_inc(signal("w_in").sem, 16)
                sp.wait_ge(signal("s0_free").sem, r + 1)
                for d, c in ((0, 0), (1, TT - 2)):
                    sp.dma_start(st[d][:, c, :], I["state_hgrn"][0, 0, d].rearrange("h k v -> (h k) v")[bass.ds(r * P, P), :])\
                        .then_inc(signal("s0_in").sem, 16)
                sp.wait_ge(signal("fin_ready").sem, r * 2 + 2)
                for d in range(2):
                    sp.dma_start(O["new_state_hgrn"][0, 0, d].rearrange("h k v -> (h k) v")[bass.ds(r * P, P), :], fin[:, d, :])\
                        .then_inc(signal("out").sem, 16)
                sp.wait_ge(signal("round_done").sem, r + 1)
                sp.dma_start(S["outh"][bass.ds(r, 1)].rearrange("o p n -> (o p) n"), outh[:, :]).then_inc(signal("out").sem, 16)
                sp.wait_ge(signal("out").sem, r * 48 + 48)
                sp.sem_inc(signal("fin_free").sem, 1)

        @block.gpsimd
        def _(pool):
            n = [0]

            def link(ins):
                n[0] += 1
                ins.then_inc(s_m, 1)
                pool.wait_ge(s_m, n[0])
            link(nc.gpsimd.memset(hm[:, :, :], 0.0))
            link(nc.gpsimd.tensor_copy(hm[:, 0, :], C["ident"][:, :]))
            for l, m in enumerate(HLEV):
                nj = P // (2 * m)
                for d in range(2):
                    v = seg(hm[:, 1 + 7 * d + l, :], m, 1 - d)
                    link(nc.gpsimd.memset(v, 1.0))
                    link(nc.gpsimd.affine_select(out=v, in_=v, compare_op=ALU.is_ge, fill=0.0, base=-m * d,
                                                 pattern=[[-2 * m, nj], [0, m]], channel_multiplier=1))
                    link(nc.gpsimd.affine_select(out=v, in_=v, compare_op=ALU.is_ge, fill=0.0, base=m - 1 + m * d,
                                                 pattern=[[2 * m, nj], [0, m]], channel_multiplier=-1))
            assert n[0] == 44

        @block.tensor
        def _(pe):
            W = lambda name, n, r: pe.wait_ge(signal(name).sem, signal(name).at(n, r))
            cnt = {}

            def inc(mm, name):
                mm.then_inc(signal(name).sem, 1)
                cnt[name] = cnt.get(name, 0) + 1
            pe.sem_inc(signal("w_free").sem, 1)
            ident = C["ident"][:, :]
            with pe.Fori(0, HG_HEADS) as r:
                cnt.clear()
                pe.wait_ge(signal("w_in").sem, r * 80 + 80)
                for i in range(HKINDS):
                    if i >= 2:
                        W("raw_taken", i - 1, r)
                    for h in range(2):
                        for k in range(KT):
                            mm = nc.tensor.matmul(ps[:, 2 * (i % 2) + h, 0:HALF], w[:, i, k, :],
                                                  S["hT"][:, k, h * HALF:(h + 1) * HALF], start=(k == 0), stop=(k == KT - 1))
                    inc(mm, "projected")
                pe.wait_ge(signal("projected").sem, signal("projected").at(HKINDS, r))
                pe.sem_inc(signal("w_free").sem, 1)
                cnt["w_free"] = 1
                W("raw_taken", 4, r)
                for c in range(TT):
                    mm = nc.tensor.transpose(tok(4, c), halfraw[:, 1, c * P:(c + 1) * P], ident)
                inc(mm, "v_turned")
                W("diag_ready", 1, r)
                for c in range(TT):
                    mm = nc.tensor.matmul(tok(6, c), qs[1][:, c * P:(c + 1) * P], q[:, c * P:(c + 1) * P], start=True, stop=True)
                inc(mm, "grams")
                W("vn_ready", 1, r)
                n = 1
                for l in range(len(HLEV)):
                    for d in range(2):
                        W("scaled", n, r)
                        if n > 1:
                            W("att_taken", n - 1, r)
                        for c in range(TT):
                            mm = nc.tensor.matmul(tok(4 + 2 * (n % 2 == 0), c), ks[d][:, c * P:(c + 1) * P],
                                                  qs[d][:, c * P:(c + 1) * P], start=True, stop=True)
                        inc(mm, "grams")
                        n += 1
                for d in range(2):
                    W("state_factors", d + 1, r)
                    if d == 0:
                        W("att_taken", 15, r)
                    for c in range(TT):
                        mm = nc.tensor.transpose(tok(4 + 2 * d, c), ks[d][:, c * P:(c + 1) * P], ident)
                    inc(mm, "k_turned")
                for d in range(2):
                    W("kn_ready", d + 1, r)
                    for c in range(TT):
                        mm = nc.tensor.matmul(tok(4 + 2 * d, c), kn[d][:, c, :], vn[:, c, :], start=True, stop=True)
                    inc(mm, "kv_sums")
                W("states_ready", 1, r)
                for c in range(TT):
                    mm = nc.tensor.matmul(tok(0, c), vn[:, c, :], att[:, c, :], start=True, stop=(c == TT - 1))
                    if c < TT - 1:
                        for d in range(2):
                            mm = nc.tensor.matmul(tok(0, c), st[d][:, c, :], qs[d][:, c * P:(c + 1) * P], start=False, stop=(d == 1))
                inc(mm, "o_sums")
                W("o_squares", 1, r)
                for h in range(2):
                    mm = nc.tensor.matmul(ps[:, 2 + h, 0:HALF], C["ones"][:, :], osq[:, h * HALF:(h + 1) * HALF], start=True, stop=True)
                inc(mm, "norm_sums")
                W("round_done", 1, r)
            S["hpe_cnt"] = dict(cnt)

        @block.scalar
        def _(act):
            W = lambda name, n, r: act.wait_ge(signal(name).sem, signal(name).at(n, r))
            cnt = {}
            A = nc.scalar.activation

            def inc(ins, name):
                ins.then_inc(signal(name).sem, 1)
                cnt[name] = cnt.get(name, 0) + 1
            act.wait_ge(signal("lb_diff").sem, 1)
            A(lbp[:, 0, :], lbp[:, 0, :], ACT.Tanh, scale=0.5).then_inc(signal("lb_tanh").sem, 1)
            with act.Fori(0, HG_HEADS) as r:
                cnt.clear()
                for i in range(HKINDS):
                    W("projected", i + 1, r)
                    W("raw_free", 1, r)
                    src = half_view(ps, 2 * (i % 2))
                    raw = {0: (0, 0.5), 3: (1, 1.0), 4: (2, 0.5)}.get(i)
                    tan = {0: 0, 1: 1, 2: 2, 4: 3}.get(i)
                    if tan is not None:
                        t = A(as_halves(th[:, tan, :]), src, ACT.Tanh, scale=0.5)
                    if raw is not None:
                        t = A(as_halves(halfraw[:, raw[0], :]), src, ACT.Copy, scale=raw[1])
                    inc(t, "raw_taken")
                W("v_turned", 1, r)
                inc(A(vn[:, :, :].rearrange("p a b -> p (a b)"), wide(4), ACT.Copy), "vn_ready")
                for d in range(2):
                    W("k_turned", d + 1, r)
                    inc(A(kn[d][:, :, :].rearrange("p a b -> p (a b)"), wide(4 + 2 * d), ACT.Copy), "kn_ready")
                W("o_sums", 1, r)
                inc(A(osq[:, :], wide(0), ACT.Square), "o_squares")
                W("norm_sums", 1, r)
                inc(A(as_halves(rt[:, :]), half_view(ps, 2), ACT.Sqrt, scale=1.0 / P, bias=C["eps"][:, 0:1]), "norm_root")
            S["hact_cnt"] = dict(cnt)

        @block.vector
        def _(dve):
            W = lambda name, n, r: dve.wait_ge(signal(name).sem, signal(name).at(n, r))
            V = nc.vector
            cnt = {}
            dve.sem_inc(signal("raw_free").sem, 1)
            dve.sem_inc(signal("s0_free").sem, 1)
            n0 = [0]

            def once(ins):
                n0[0] += 1
                ins.then_inc(signal("setup_line").sem, 1)
                dve.wait_ge(signal("setup_line").sem, n0[0])
            dve.wait_ge(s_m, 44)
            V.tensor_tensor(lbp[:, 0, :], S["ptab"][:, 2, LB0:LB0 + 16], S["ptab"][:, 2, LB1:LB1 + 16], ALU.subtract)\
                .then_inc(signal("lb_diff").sem, 1)
            dve.wait_ge(signal("lb_tanh").sem, 1)
            once(V.tensor_scalar(lbp[:, 1, :], lbp[:, 0, :], 0.25, 0.75, ALU.mult, ALU.add))
            once(V.tensor_scalar(lbp[:, 2, :], lbp[:, 0, :], -0.25, 0.25, ALU.mult, ALU.add))
            with dve.Fori(0, HG_HEADS) as r:
                cnt.clear()

                def did(ins, name):
                    cnt[name] = cnt.get(name, 0) + 1
                    ins.then_inc(signal(name).sem, 1)
                    dve.wait_ge(signal(name).sem, signal(name).at(cnt[name], r))
                link = lambda ins: did(ins, "vector_line")

                def raised(name):
                    dve.sem_inc(signal(name).sem, 1)
                    cnt[name] = cnt.get(name, 0) + 1
                W("raw_taken", HKINDS, r)
                link(V.scalar_tensor_tensor(out=q[:, :], in0=th[:, 0, :], scalar=1.0, in1=halfraw[:, 0, :], op0=ALU.add, op1=ALU.mult))
                link(V.scalar_tensor_tensor(out=sgate[:, :], in0=th[:, 3, :], scalar=1.0, in1=gh, op0=ALU.add, op1=ALU.mult))
                for d in range(2):
                    link(V.tensor_scalar(incl[d][:, :], th[:, 1 + d, :], lbp[:, 2, bass.ds(r + 8 * d, 1)], lbp[:, 1, bass.ds(r + 8 * d, 1)],
                                         ALU.mult, ALU.add))
                    link(V.tensor_scalar(key[d][:, :], incl[d][:, :], -1.0, 1.0, ALU.mult, ALU.add))
                    if d == 0:
                        link(V.memset(excl[d][:, :], 1.0))
                did(V.tensor_tensor(qs[1][:, :], key[0][:, :], key[1][:, :], ALU.add), "diag_ready")
                i32 = lambda ap: ap.bitcast(I32)

                def take(n, mask, b, beside):
                    W("grams", n, r)
                    beside().then_inc(signal("vector_line").sem, 1)
                    cnt["vector_line"] += 1
                    did(V.copy_predicated(att[:, :, :], i32(bcast(hm[:, mask, :], TT, 1)), wide(b).rearrange("p (c t) -> p c t", t=P)), "att_taken")
                    dve.wait_ge(signal("vector_line").sem, signal("vector_line").at(cnt["vector_line"], r))
                take(1, 0, 6, lambda: V.memset(excl[1][:, :], 1.0))
                for l, m in enumerate(HLEV):
                    for d in range(2):
                        n = 1 + 2 * l + d
                        qh, kh = 1 - d, d
                        link(V.tensor_tensor(seg(qs[d][:, :], m, qh), seg(q[:, :], m, qh), seg(incl[d][:, :], m, qh), ALU.mult))
                        if l == 0:
                            link(V.tensor_copy(seg(qs[d][:, :], m, kh), seg(q[:, :], m, kh)))
                            link(V.tensor_copy(ks[d][:, :], key[d][:, :]))
                        did(V.tensor_tensor(seg(ks[d][:, :], m, kh), seg(key[d][:, :], m, kh), seg(excl[d][:, :], m, kh), ALU.mult), "scaled")
                        end = m - 1 if d == 0 else 0
                        tq = seg(incl[d][:, :], m, kh)[:, :, end:end + 1]
                        tk = seg(incl[d][:, :], m, qh)[:, :, end:end + 1]
                        wide_t = lambda a: a.broadcast_to([P, T // (2 * m), m])
                        link(V.tensor_tensor(seg(excl[d][:, :], m, kh), seg(excl[d][:, :], m, kh), wide_t(tk), ALU.mult))
                        take(n + 1, 1 + 7 * d + l, 4 + 2 * (n % 2 == 0),
                             lambda: V.tensor_tensor(seg(incl[d][:, :], m, qh), seg(incl[d][:, :], m, qh), wide_t(tq), ALU.mult))
                for d in range(2):
                    link(V.tensor_tensor(qs[d][:, :], q[:, :], incl[d][:, :], ALU.mult))
                    did(V.tensor_tensor(ks[d][:, :], key[d][:, :], excl[d][:, :], ALU.mult), "state_factors")
                dve.wait_ge(signal("s0_in").sem, r * 32 + 32)
                W("fin_free", 1, r)
                for d in range(2):
                    W("kv_sums", d + 1, r)
                    did(V.tensor_copy(fin[:, d, :], tok(4 + 2 * d, TT - 1)), "fin_ready")
                    for j in range(TT - 2):
                        c, c2 = (j, j + 1) if d == 0 else (TT - 2 - j, TT - 3 - j)
                        e = c * P + (P - 1 if d == 0 else 0)
                        link(V.scalar_tensor_tensor(out=st[d][:, c2, :], in0=st[d][:, c, :], scalar=incl[d][:, e:e + 1],
                                                    in1=tok(4 + 2 * d, c), op0=ALU.mult, op1=ALU.add))
                raised("states_ready")
                W("norm_root", 1, r)
                raised("s0_free")
                raised("raw_free")
                link(V.reciprocal(rt[:, :], rt[:, :]))
                link(V.tensor_tensor(o1[:, :], wide(0), rt[:, :], ALU.mult))
                did(V.scalar_tensor_tensor(out=outh[:, :], in0=o1[:, :], scalar=S["ptab"][:, 2, bass.ds(r + HGN, 1)], in1=sgate[:, :],
                                           op0=ALU.mult, op1=ALU.mult), "round_done")
            S["hdve_cnt"] = dict(cnt)
        S["hsig"] = sig


def stage_merge(nc, I, S):
    with ExitStack() as ctx:
        sb = lambda name, shape, dt=F32: ctx.enter_context(nc.sbuf_tensor(name, shape, dt))
        sg = lambda name: ctx.enter_context(nc.semaphore("mg_" + name))
        SLOTS = 2
        w = [sb(f"wmg{s}", [P, 3 * KT, P]) for s in range(SLOTS)]
        br = sb("branches", [P, 2, PAIRS, T])
        th = [sb(f"gth{i}", [P, T]) for i in range(2)]
        m1, m2 = sb("m1", [P, T]), sb("m2", [P, T])
        ps = ctx.enter_context(nc.psum_tensor("psM", [P, 8, 512], F32))
        s_w = [sg(f"w_in{s}") for s in range(SLOTS)]
        s_wf = [sg(f"w_free{s}") for s in range(SLOTS)]
        s_br, s_gate, s_branch, s_th, s_m, s_mix = map(sg, ("branches_in", "gates", "branch_sums", "tanhs", "products", "merged"))
        block = ctx.enter_context(nc.Block())

        @block.sync
        def _(sp):
            for i, name in enumerate(("outr", "outh")):
                sp.dma_start(br[:, i], S[name].rearrange("n p t -> p n t")).then_inc(s_br, 16)
            win = I["w_in"][0].rearrange("(k p) n -> p k n", p=P)
            with sp.Fori(0, KT // SLOTS) as r:
                for s in range(SLOTS):
                    sp.wait_ge(s_wf[s], r + 1)
                    for g in range(2):
                        sp.dma_start(w[s][:, g * KT:(g + 1) * KT, :], win[:, :, bass.ds((r * SLOTS + s) * P + (GATE0 + g * D), P)])\
                            .then_inc(s_w[s], 16)
                    for g, name in enumerate(("w_br_rwkv", "w_br_hgrn")):
                        src = I[name][0].rearrange("(k p) n -> p k n", p=P)
                        sp.dma_start(w[s][:, 2 * KT + 8 * g:2 * KT + 8 * g + 8, :], src[:, :, bass.ds((r * SLOTS + s) * P, P)])\
                            .then_inc(s_w[s], 16)

        @block.tensor
        def _(pe):
            for s in range(SLOTS):
                pe.sem_inc(s_wf[s], 1)
            pe.wait_ge(s_br, 32)
            with pe.Fori(0, KT // SLOTS) as r:
                for s in range(SLOTS):
                    pe.wait_ge(s_w[s], r * 64 + 64)
                    for g in range(2):
                        pe.wait_ge(s_th, r * 4 + (2 * s + g + 1))
                        for h in range(2):
                            for k in range(KT):
                                mm = nc.tensor.matmul(ps[:, 2 * g + h, 0:HALF], w[s][:, g * KT + k, :],
                                                      S["hT"][:, k, h * HALF:(h + 1) * HALF], start=(k == 0), stop=(k == KT - 1))
                        mm.then_inc(s_gate, 1)
                    for g in range(2):
                        pe.wait_ge(s_m, r * 4 + (2 * s + g + 1))
                        for h in range(2):
                            for k in range(PAIRS):
                                mm = nc.tensor.matmul(ps[:, 4 + 2 * g + h, 0:HALF], w[s][:, 2 * KT + 8 * g + k, :],
                                                      br[:, g, k, h * HALF:(h + 1) * HALF], start=(k == 0), stop=(k == PAIRS - 1))
                        mm.then_inc(s_branch, 1)
                    pe.wait_ge(s_branch, r * 4 + (2 * s + 2))
                    pe.sem_inc(s_wf[s], 1)

        @block.scalar
        def _(act):
            act.sem_inc(s_th, 2)
            with act.Fori(0, KT // SLOTS) as r:
                for s in range(SLOTS):
                    for g in range(2):
                        act.wait_ge(s_gate, r * 4 + (2 * s + g + 1))
                        act.wait_ge(s_m, r * 4 + (2 * s + g + 1))
                        nc.scalar.activation(as_halves(th[g][:, :]), half_view(ps, 2 * g), ACT.Tanh, scale=0.5).then_inc(s_th, 1)

        @block.vector
        def _(dve):
            dve.sem_inc(s_m, 2)
            with dve.Fori(0, KT // SLOTS) as r:
                for s in range(SLOTS):
                    for g, m in enumerate((m1, m2)):
                        dve.wait_ge(s_branch, r * 4 + (2 * s + g + 1))
                        dve.wait_ge(s_th, r * 4 + (2 * s + g + 3))
                        nc.vector.scalar_tensor_tensor(out=as_halves(m[:, :]), in0=as_halves(th[g][:, :]), scalar=1.0,
                                                       in1=half_view(ps, 4 + 2 * g), op0=ALU.add, op1=ALU.mult).then_inc(s_m, 1)
                    dve.wait_ge(s_m, r * 4 + (2 * s + 4))
                    nc.vector.tensor_tensor(S["mergedT"][:, bass.ds(r * SLOTS + s, 1), :].rearrange("p o n -> p (o n)"), m1[:, :], m2[:, :], ALU.add)\
                        .then_inc(s_mix, 1)
                    dve.wait_ge(s_mix, r * SLOTS + (s + 1))


def stage_out_norm(nc, I, S):
    with ExitStack() as ctx:
        sb = lambda name, shape, dt=F32: ctx.enter_context(nc.sbuf_tensor(name, shape, dt))
        sg = lambda name: ctx.enter_context(nc.semaphore("on_" + name))
        w = [sb(f"wout{s}", [P, KT, P]) for s in range(2)]
        xs = [sb(f"xs{s}", [P, T]) for s in range(2)]
        xq = [sb(f"xq{s}", [P, T]) for s in range(2)]
        gth = sb("gth", [P, KT, 2])
        rstd = sb("rstd2", [P, T])
        wr = sb("wr", [P, KT, NE])
        mx, sm, ex = sb("mx", [P, TT]), sb("sm", [P, TT]), sb("ex", [P, TT, NE])
        ps = ctx.enter_context(nc.psum_tensor("psO", [P, 8, 512], F32))
        s_w = [sg(f"w_in{s}") for s in range(2)]
        (s_x, s_r, s_xt, s_xc, s_o, s_x1, s_q, s_ss, s_root, s_v, s_h2, s_ht, s_hc, s_lg, s_lr, s_ex) = map(sg, (
            "x_in", "router_in", "x_turned", "x_copied", "out_sums", "x1_ready", "squares", "square_sums", "root",
            "vector_line", "h2_ready", "h2_turned", "h2_copied", "logits", "logits_ready", "exps"))
        block = ctx.enter_context(nc.Block())
        xrow, x1T, h2T, mT, h2row = S["rows"], S["x1T"], S["hT"], S["mergedT"], S["rows"]
        wide = lambda b: ps[:, b:b + 2, :].rearrange("p a n -> p (a n)")[:, 0:T]

        def tok(b, t):
            return ps[:, b + t // 4, (t % 4) * P:(t % 4 + 1) * P]

        @block.sync
        def _(sp):
            for t in range(TT):
                src = I["x_sample"][0, t * P:(t + 1) * P, :] if t < TT - 1 else I["x_prompt"][0]
                sp.dma_start(xrow[:, t, :], src).then_inc(s_x, 16)
            sp.dma_start(wr[:, :, :], I["moe_router"][0].rearrange("(k p) e -> p k e", p=P)).then_inc(s_r, 16)
            wo = I["w_out"][0].rearrange("(k p) n -> p k n", p=P)
            for j in range(KT):
                if j >= 2:
                    sp.wait_ge(s_o, j - 1)
                sp.dma_start(w[j % 2][:, :, :], wo[:, :, j * P:(j + 1) * P]).then_inc(s_w[j % 2], 16)

        @block.tensor
        def _(pe):
            ident = S["consts"]["ident"][:, :]
            pe.wait_ge(s_x, 16 * TT)
            for j in range(KT):
                if j:
                    pe.wait_ge(s_xc, j)
                for t in range(TT):
                    mm = nc.tensor.transpose(tok(4, t), xrow[:, t, j * P:(j + 1) * P], ident)
                mm.then_inc(s_xt, 1)
                pe.wait_ge(s_w[j % 2], 16 * (j // 2 + 1))
                if j >= 2:
                    pe.wait_ge(s_x1, 2 * (j - 1))
                for cut, b in ((slice(0, NS), 0), (slice(NS, T), 1)):
                    for k in range(KT):
                        mm = nc.tensor.matmul(ps[:, 2 * (j % 2) + b, 0:cut.stop - cut.start], w[j % 2][:, k, :], mT[:, k, cut],
                                              start=(k == 0), stop=(k == KT - 1))
                mm.then_inc(s_o, 1)
                if j >= 1:
                    pe.wait_ge(s_q, j)
                    for h in range(2):
                        mm = nc.tensor.matmul(ps[:, 6 + h, 0:HALF], S["consts"]["ones"][:, :], xq[(j - 1) % 2][:, h * HALF:(h + 1) * HALF],
                                              start=(j == 1), stop=False)
                    mm.then_inc(s_ss, 1)
            pe.wait_ge(s_q, KT)
            for h in range(2):
                mm = nc.tensor.matmul(ps[:, 6 + h, 0:HALF], S["consts"]["ones"][:, :], xq[(KT - 1) % 2][:, h * HALF:(h + 1) * HALF],
                                      start=False, stop=True)
            mm.then_inc(s_ss, 1)
            for j in range(KT):
                b = 2 * (j % 2)
                pe.wait_ge(s_h2, 2 * (j + 1))
                if j >= 2:
                    pe.wait_ge(s_hc, j - 1)
                for t in range(TT):
                    mm = nc.tensor.transpose(tok(b, t), h2T[:, j, t * P:(t + 1) * P], ident)
                mm.then_inc(s_ht, 1)
            pe.wait_ge(s_r, 16)
            for t in range(TT):
                for k in range(KT):
                    mm = nc.tensor.matmul(ps[:, 4, t * NE:(t + 1) * NE], h2T[:, k, t * P:(t + 1) * P], wr[:, k, :],
                                          start=(k == 0), stop=(k == KT - 1))
            mm.then_inc(s_lg, 1)

        @block.scalar
        def _(act):
            A = nc.scalar.activation
            for j in range(KT):
                act.wait_ge(s_xt, j + 1)
                if j >= 2:
                    act.wait_ge(s_x1, 2 * (j - 1))
                A(xs[j % 2][:, :], wide(4), ACT.Copy).then_inc(s_xc, 1)
                if j >= 1:
                    act.wait_ge(s_x1, 2 * j)
                    if j >= 3:
                        act.wait_ge(s_ss, j - 2)
                    A(xq[(j - 1) % 2][:, :], x1T[:, j - 1, :], ACT.Square).then_inc(s_q, 1)
            act.wait_ge(s_x1, 2 * KT)
            act.wait_ge(s_ss, KT - 2)
            A(xq[(KT - 1) % 2][:, :], x1T[:, KT - 1, :], ACT.Square).then_inc(s_q, 1)
            act.wait_ge(s_ss, KT)
            A(as_halves(rstd[:, :]), half_view(ps, 6), ACT.Sqrt, scale=1.0 / D, bias=S["consts"]["eps"][:, 0:1]).then_inc(s_root, 1)
            for j in range(KT):
                act.wait_ge(s_ht, j + 1)
                A(h2row[:, :, j * P:(j + 1) * P], wide(2 * (j % 2)).rearrange("p (t c) -> p t c", c=P), ACT.Copy).then_inc(s_hc, 1)
            act.wait_ge(s_lr, 1)
            A(ex[:, :, :], ex[:, :, :], ACT.Exp).then_inc(s_ex, 1)

        @block.vector
        def _(dve):
            V = nc.vector
            steps = [0]

            def link(ins):
                steps[0] += 1
                ins.then_inc(s_v, 1)
                dve.wait_ge(s_v, steps[0])
            modT, A2 = S["modT"], S["A2"]
            link(V.tensor_scalar(gth[:, :, :], modT[:, 2 * KT:3 * KT, :], 0.5, None, ALU.mult))
            for j in range(KT):
                dve.wait_ge(s_o, j + 1)
                dve.wait_ge(s_xc, j + 1)
                for s, (cut, b) in enumerate(((slice(0, NS), 0), (slice(NS, T), 1))):
                    V.scalar_tensor_tensor(out=x1T[:, j, cut], in0=ps[:, 2 * (j % 2) + b, 0:cut.stop - cut.start], scalar=gth[:, j, s:s + 1],
                                           in1=xs[j % 2][:, cut], op0=ALU.mult, op1=ALU.add).then_inc(s_x1, 1)
            dve.wait_ge(s_x1, 2 * KT)
            dve.wait_ge(s_root, 1)
            link(V.reciprocal(rstd[:, :], rstd[:, :]))
            for j in range(KT):
                link(V.tensor_tensor(h2T[:, j, :], x1T[:, j, :], rstd[:, :], ALU.mult))
                for s, cut in enumerate((slice(0, NS), slice(NS, T))):
                    V.tensor_scalar(h2T[:, j, cut], h2T[:, j, cut], A2[:, j, s:s + 1], modT[:, 3 * KT + j, s:s + 1],
                                    ALU.mult, ALU.add).then_inc(s_h2, 1)
            dve.wait_ge(s_h2, 2 * KT)
            dve.wait_ge(s_lg, 1)
            aff = S["aff"]
            lg = ps[:, 4, 0:TT * NE].rearrange("p (t e) -> p t e", e=NE)
            link(V.tensor_reduce(mx[:, :], lg, AX_X, ALU.max))
            V.tensor_tensor(ex[:, :, :], lg, bcast(mx[:, :], NE, 2), ALU.subtract).then_inc(s_lr, 1)
            dve.wait_ge(s_lr, 1)
            dve.wait_ge(s_ex, 1)
            link(V.tensor_reduce(sm[:, :], ex[:, :, :], AX_X, ALU.add))
            link(V.reciprocal(sm[:, :], sm[:, :]))
            link(V.tensor_tensor(aff[:, :, :], ex[:, :, :], bcast(sm[:, :], NE, 2), ALU.mult))


def stage_choose(nc, S):
    with ExitStack() as ctx:
        sb = lambda name, shape, dt=F32: ctx.enter_context(nc.sbuf_tensor(name, shape, dt))
        sg = lambda name: ctx.enter_context(nc.semaphore("ch_" + name))
        left, m8 = sb("left", [NE, T]), sb("m8", [NE, 8])
        one, cum = sb("onerow", [NE, T]), sb("cum", [NE, T])
        ps = ctx.enter_context(nc.psum_tensor("psC", [P, 8, 512], F32))
        s_t, s_v, s_s, s_b = map(sg, ("turned", "vector_line", "slots_ready", "slots_turned"))
        block = ctx.enter_context(nc.Block())
        ident = S["consts"]["ident"]

        @block.tensor
        def _(pe):
            for t in range(TT):
                mm = nc.tensor.transpose(ps[0:NE, t // 4, (t % 4) * P:(t % 4 + 1) * P], S["aff"][:, t, :], ident[:, :])
            mm.then_inc(s_t, 1)
            pe.wait_ge(s_s, 1)
            for t in range(TT):
                mm = nc.tensor.transpose(ps[:, 2, t * NE:(t + 1) * NE], cum[:, t * P:(t + 1) * P], ident[0:NE, 0:NE])
            mm.then_inc(s_b, 1)

        @block.vector
        def _(dve):
            V = nc.vector
            steps = [0]

            def link(ins):
                steps[0] += 1
                ins.then_inc(s_v, 1)
                dve.wait_ge(s_v, steps[0])
            dve.wait_ge(s_t, 1)
            link(V.tensor_copy(left[:, :], ps[0:NE, 0:2, :].rearrange("p a n -> p (a n)")[:, 0:T]))
            for cut, cap in ((slice(0, NS), CAP_S), (slice(NS, T), CAP_P)):
                for _i in range(cap // 8):
                    link(V.max(m8[:, :], left[:, cut]))
                    link(V.match_replace(left[:, cut], m8[:, :], left[:, cut], -1.0))
            link(V.tensor_scalar(left[:, :], left[:, :], 0.0, None, ALU.is_lt))
            link(V.memset(one[:, :], 1.0))
            for cut in (slice(0, NS), slice(NS, T)):
                link(V.tensor_tensor_scan(cum[:, cut], one[:, cut], left[:, cut], 0.0, ALU.mult, ALU.add))
            V.tensor_tensor(cum[:, :], cum[:, :], left[:, :], ALU.mult).then_inc(s_s, 1)
            dve.wait_ge(s_b, 1)
            link(V.tensor_copy(S["slot"][:, :, :].rearrange("p t e -> p (t e)"), ps[:, 2, 0:TT * NE]))


def stage_experts(nc, I, S):
    with ExitStack() as ctx:
        sb = lambda name, shape, dt=F32: ctx.enter_context(nc.sbuf_tensor(name, shape, dt))
        sg = lambda name: ctx.enter_context(nc.semaphore("ex_" + name))
        RING = 8
        M = CAP_S + CAP_P
        FT = FF // P
        KC = 2
        NCHUNK = 2 * (KT // KC) + FT
        USES = 2 * NCHUNK // RING
        NPAIR = NE // 2
        spare = [S[n][:, :, :].rearrange("p k t -> p (k t)")[:, i * 2048:(i + 1) * 2048] for n in ("hT", "mergedT") for i in range(5)]
        ring = spare[0:RING]
        xg = sb("xg", [P, KT, 2, M])
        hid = sb("hid", [P, FT, M])
        gt, gu = sb("gtanh", [P, FT, M]), sb("gsilu", [P, FT, M])
        sel, selw = sb("sel", [P, 4, 2, CAP_S]), sb("selw", [P, 4, 2, CAP_S])
        selp, selpw = sb("selp", [P, 2, CAP_P]), sb("selpw", [P, 2, 32])
        selT, selpT = sb("selT", [P, NS]), sb("selpT", [64, NP])
        ys, yp = spare[RING], spare[RING + 1][0:64, :]
        iota = sb("iota", [P, CAP_S])
        gth = sb("gth2", [P, KT, 2])
        ps = ctx.enter_context(nc.psum_tensor("psE", [P, 8, 512], F32))
        s_in = [sg(f"w_in{i}") for i in range(RING)]
        s_free = [sg(f"w_free{i}") for i in range(RING)]
        (s_io, s_sel, s_selT, s_selc, s_gath, s_xg, s_gus, s_tanh, s_hid, s_down, s_y, s_sc, s_add, s_v, s_z) = map(sg, (
            "iota", "selected", "selection_turned", "selection_copied", "gathered", "xg_ready", "gate_up_sums", "gate_tanh",
            "hidden", "down_sums", "y_ready", "scattered", "added", "vector_line", "zeroed"))
        block = ctx.enter_context(nc.Block())
        x1T, rows = S["x1T"], S["rows"]
        PJ = 3
        gj = [list(range(a, min(a + PJ, KT))) for a in range(0, KT, PJ)]
        N_GATH, N_GUS, N_TANH, N_HID, N_DOWN, N_Y, N_SC, N_ADD = len(gj), 2, 4, 2, 2, 8, KT, 2 * KT

        def chunk_list(e):
            return [("gu", k, g) for k in range(KT // KC) for g in range(2)] + [("down", m, 0) for m in range(FT)]

        @block.sync
        def _(sp):
            wg, wu, wd = (I[n][0].rearrange("e a b -> (e a) b") for n in ("moe_w_gate", "moe_w_up", "moe_w_down"))
            with sp.Fori(0, NPAIR) as r:
                n = 0
                for e in range(2):
                    for what, k, g in chunk_list(e):
                        slot, use = n % RING, n // RING
                        sp.wait_ge(s_free[slot], r * USES + (use + 1))
                        if what == "gu":
                            src = (wg, wu)[g][bass.ds(r * (2 * D) + (e * D + k * KC * P), KC * P), :].rearrange("(k p) f -> p k f", p=P)
                            dst = ring[slot].rearrange("p (k f) -> p k f", k=KC)
                        else:
                            src = wd[bass.ds(r * (2 * FF) + (e * FF + k * P), P), :]
                            dst = ring[slot]
                        sp.dma_start(dst, src).then_inc(s_in[slot], 16)
                        n += 1

        @block.gpsimd
        def _(pool):
            nc.gpsimd.iota(iota[:, :], pattern=[[1, CAP_S]], base=1, channel_multiplier=0,
                           allow_small_or_imprecise_dtypes=True).then_inc(s_io, 1)
            nc.gpsimd.memset(selpw[:, :, :], 0.0).then_inc(s_z, 1)
            nc.gpsimd.memset(yp, 0.0).then_inc(s_z, 1)

        @block.tensor
        def _(pe):
            ident = S["consts"]["ident"][:, :]
            for i in range(RING):
                pe.sem_inc(s_free[i], 1)
            with pe.Fori(0, NPAIR) as r:
                pe.wait_ge(s_sel, r + 1)
                for t in range(4):
                    mm = nc.tensor.transpose(ps[:, 6, t * P:(t + 1) * P], selw[:, t].rearrange("p e s -> p (e s)"), ident)
                mm = nc.tensor.transpose(ps[0:64, 7, 0:P], selpw[:, :, :].rearrange("p e s -> p (e s)"), ident)
                mm.then_inc(s_selT, 1)
                for i, js in enumerate(gj):
                    if i >= 2:
                        pe.wait_ge(s_xg, r * N_GATH + (i - 1))
                    for n, j in enumerate(js):
                        o = ps[:, 4 + i % 2, n * 2 * M:(n + 1) * 2 * M].rearrange("p (e s) -> p e s", e=2)
                        for t in range(4):
                            nc.tensor.matmul(o[:, :, 0:CAP_S], rows[:, t, j * P:(j + 1) * P], sel[:, t, :, :], start=(t == 0), stop=(t == 3))
                        mm = nc.tensor.matmul(o[:, :, CAP_S:M], rows[:, 4, j * P:(j + 1) * P], selp[:, :, :], start=True, stop=True)
                    mm.then_inc(s_gath, 1)
                n = 0
                for e in range(2):
                    if e == 0:
                        pe.wait_ge(s_xg, r * N_GATH + N_GATH)
                        pe.wait_ge(s_selc, r * 2 + 2)
                    else:
                        pe.wait_ge(s_hid, r * N_HID + 1)
                    for what, k, g in chunk_list(e):
                        slot, use = n % RING, n // RING
                        if what == "down" and k == 0:
                            pe.wait_ge(s_hid, r * N_HID + (e + 1))
                            if e:
                                pe.wait_ge(s_y, r * N_Y + 4)
                        pe.wait_ge(s_in[slot], r * (16 * USES) + 16 * (use + 1))
                        if what == "gu":
                            for kk in range(KC):
                                kt = k * KC + kk
                                for m in range(FT):
                                    mm = nc.tensor.matmul(ps[:, 2 * g + m // 4, (m % 4) * M:(m % 4 + 1) * M],
                                                          ring[slot][:, kk * FF + m * P:kk * FF + (m + 1) * P], xg[:, kt, e, :],
                                                          start=(kt == 0 and m % 4 == 0), stop=(kt == KT - 1), skip_group_check=True)
                            if g == 1 and k == KT // KC - 1:
                                mm.then_inc(s_gus, 1)
                                pe.wait_ge(s_gus, r * N_GUS + (e + 1))
                                pe.sem_inc(s_free[slot], 1)
                            else:
                                mm.then_inc(s_free[slot], 1)
                        else:
                            for c in range(4):
                                mm = nc.tensor.matmul(ps[0:M, 4 + c, :], hid[:, k, :], ring[slot][:, c * 512:(c + 1) * 512],
                                                      start=(k == 0), stop=(k == FT - 1), skip_group_check=True)
                            if k == FT - 1:
                                mm.then_inc(s_down, 1)
                                pe.wait_ge(s_down, r * N_DOWN + (e + 1))
                                pe.sem_inc(s_free[slot], 1)
                            else:
                                mm.then_inc(s_free[slot], 1)
                        n += 1
                pe.wait_ge(s_y, r * N_Y + N_Y)
                for j in range(KT):
                    b = 4 + 2 * (j % 2)
                    if j >= 2:
                        pe.wait_ge(s_add, r * N_ADD + 2 * (j - 1))
                    nc.tensor.matmul(ps[:, b, :], ys[:, j * P:(j + 1) * P], selT[:, :], start=True, stop=True)
                    nc.tensor.matmul(ps[:, b + 1, 0:P], yp[:, j * P:(j + 1) * P], selpT[:, :], start=True, stop=True).then_inc(s_sc, 1)
                pe.wait_ge(s_add, r * N_ADD + N_ADD)

        @block.scalar
        def _(act):
            A = nc.scalar.activation
            with act.Fori(0, NPAIR) as r:
                act.wait_ge(s_selT, r + 1)
                A(selT[:, :], ps[:, 6, :], ACT.Copy).then_inc(s_selc, 1)
                A(selpT[:, :], ps[0:64, 7, 0:P], ACT.Copy).then_inc(s_selc, 1)
                for i, js in enumerate(gj):
                    act.wait_ge(s_gath, r * N_GATH + (i + 1))
                    A(xg[:, js[0]:js[-1] + 1, :, :].rearrange("p j e s -> p (j e s)"), ps[:, 4 + i % 2, 0:len(js) * 2 * M], ACT.Copy).then_inc(s_xg, 1)
                for e in range(2):
                    act.wait_ge(s_gus, r * N_GUS + (e + 1))
                    if e:
                        act.wait_ge(s_hid, r * N_HID + 1)
                    for h in range(2):
                        A(gt[:, 4 * h:4 * h + 4, :].rearrange("p m s -> p (m s)"), ps[:, h, 0:4 * M], ACT.Tanh, scale=0.5).then_inc(s_tanh, 1)
                    act.wait_ge(s_down, r * N_DOWN + (e + 1))
                    for c in range(2, 4):
                        A(ys[64 * e:64 * e + 64, c * 512:(c + 1) * 512], ps[0:64, 4 + c, :], ACT.Copy)
                        A(yp[32 * e:32 * e + CAP_P, c * 512:(c + 1) * 512], ps[64:M, 4 + c, :], ACT.Copy).then_inc(s_y, 1)

        @block.vector
        def _(dve):
            V = nc.vector
            dve.wait_ge(s_io, 1)
            dve.wait_ge(s_z, 2)
            V.tensor_scalar(gth[:, :, :], S["modT"][:, 5 * KT:6 * KT, :], 0.5, None, ALU.mult).then_inc(s_v, 1)
            dve.wait_ge(s_v, 1)
            with dve.Fori(0, NPAIR) as r:
                for e in range(2):
                    for t in range(TT):
                        out, outw, cap = (sel[:, t, e, :], selw[:, t, e, :], CAP_S) if t < 4 else (selp[:, e, :], selpw[:, e, 0:CAP_P], CAP_P)
                        place, weight = (S[x][:, t, bass.ds(r * 2 + e, 1)] for x in ("slot", "aff"))
                        V.tensor_scalar(out, iota[:, 0:cap], place, None, ALU.is_equal)
                        last = V.tensor_scalar(outw, iota[:, 0:cap], place, weight, ALU.is_equal, ALU.mult)
                last.then_inc(s_sel, 1)
                for e in range(2):
                    dve.wait_ge(s_tanh, r * N_TANH + (2 * e + 2))
                    for h in range(2):
                        ms = slice(4 * h, 4 * h + 4)
                        fl = lambda a: a[:, ms, :].rearrange("p m s -> p (m s)")
                        last = V.scalar_tensor_tensor(out=fl(gu), in0=fl(gt), scalar=1.0, in1=ps[:, h, 0:4 * M], op0=ALU.add, op1=ALU.mult)
                    last.then_inc(s_v, 1)
                    dve.wait_ge(s_v, r * 2 + (e + 2))
                    for h in range(2):
                        ms = slice(4 * h, 4 * h + 4)
                        fl = lambda a: a[:, ms, :].rearrange("p m s -> p (m s)")
                        last = V.tensor_tensor(fl(hid), fl(gu), ps[:, 2 + h, 0:4 * M], ALU.mult)
                    last.then_inc(s_hid, 1)
                    dve.wait_ge(s_down, r * N_DOWN + (e + 1))
                    for c in range(2):
                        V.tensor_copy(ys[64 * e:64 * e + 64, c * 512:(c + 1) * 512], ps[0:64, 4 + c, :])
                        V.tensor_copy(yp[32 * e:32 * e + CAP_P, c * 512:(c + 1) * 512], ps[64:M, 4 + c, :]).then_inc(s_y, 1)
                for j in range(KT):
                    b = 4 + 2 * (j % 2)
                    dve.wait_ge(s_sc, r * N_SC + (j + 1))
                    for s, (cut, bb) in enumerate(((slice(0, NS), b), (slice(NS, T), b + 1))):
                        V.scalar_tensor_tensor(out=x1T[:, j, cut], in0=ps[:, bb, 0:cut.stop - cut.start], scalar=gth[:, j, s:s + 1],
                                               in1=x1T[:, j, cut], op0=ALU.mult, op1=ALU.add).then_inc(s_add, 1)
                dve.wait_ge(s_add, r * N_ADD + N_ADD)


def stage_final(nc, I, O, S):
    with ExitStack() as ctx:
        sb = lambda name, shape, dt=F32: ctx.enter_context(nc.sbuf_tensor(name, shape, dt))
        sg = lambda name: ctx.enter_context(nc.semaphore("fi_" + name))
        g, junk = (S["mergedT"][:, :, :].rearrange("p k t -> p (k t)")[:, i * D:(i + 1) * D] for i in range(2))
        yv = S["hT"][:, :, :].rearrange("p k t -> p (k t)").rearrange("p (t n) -> p t n", n=D)
        ssq, rs = sb("ssqf", [P, TT]), sb("rsf", [P, TT])
        ps = ctx.enter_context(nc.psum_tensor("psF", [P, 8, 512], F32))
        s_g, s_t, s_c, s_ss, s_root, s_r, s_y, s_out = map(sg, ("g_in", "turned", "copied", "ssq", "root", "rstd", "y_ready", "y_out"))
        block = ctx.enter_context(nc.Block())
        rows = S["rows"]

        @block.sync
        def _(sp):
            sp.dma_start(g, I["final_norm_g"].partition_broadcast(P)).then_inc(s_g, 16)
            for t in range(TT):
                dst = O["y_sample"][0, t * P:(t + 1) * P, :] if t < TT - 1 else O["y_prompt"][0]
                sp.wait_ge(s_y, t + 1)
                sp.dma_start(dst, yv[:, t, :]).then_inc(s_out, 16)
            sp.wait_ge(s_out, 16 * TT)

        @block.tensor
        def _(pe):
            for i in range(4 * TT):
                t, q = divmod(i, 4)
                if i >= 8:
                    pe.wait_ge(s_c, i - 7)
                for n in range(4):
                    mm = nc.tensor.transpose(ps[:, i % 8, n * P:(n + 1) * P], S["x1T"][:, 4 * q + n, t * P:(t + 1) * P],
                                             S["consts"]["ident"][:, :])
                mm.then_inc(s_t, 1)

        @block.scalar
        def _(act):
            A = nc.scalar.activation
            for t in range(TT):
                act.wait_ge(s_c, 4 * t + 4)
                if t:
                    act.wait_ge(s_ss, t)
                A(junk, rows[:, t, :], ACT.Square, accum_out=ssq[:, t:t + 1]).then_inc(s_ss, 1)
            act.wait_ge(s_ss, TT)
            A(rs[:, :], ssq[:, :], ACT.Sqrt, scale=1.0 / D, bias=S["consts"]["eps"][:, 0:1]).then_inc(s_root, 1)

        @block.vector
        def _(dve):
            V = nc.vector
            for i in range(4 * TT):
                t, q = divmod(i, 4)
                dve.wait_ge(s_t, i + 1)
                V.tensor_copy(rows[:, t, q * 512:(q + 1) * 512], ps[:, i % 8, :]).then_inc(s_c, 1)
            dve.wait_ge(s_root, 1)
            dve.wait_ge(s_g, 16)
            V.reciprocal(rs[:, :], rs[:, :]).then_inc(s_r, 1)
            dve.wait_ge(s_r, 1)
            for t in range(TT):
                V.scalar_tensor_tensor(out=yv[:, t, :], in0=rows[:, t, :], scalar=rs[:, t:t + 1], in1=g,
                                       op0=ALU.mult, op1=ALU.mult).then_inc(s_y, 1)


def build_layer(nc, I, O, per=None):
    per = per or PER
    with ExitStack() as ctx:
        sb = lambda name, shape, dt=F32: ctx.enter_context(nc.sbuf_tensor(name, shape, dt))
        S = {"consts": {"ident": sb("ident", [P, P]), "bd": sb("bdmask", [P, 5, 2, L]), "cm": sb("cmask", [P, 4, L]),
                        "ci": sb("cident", [P, L]), "ns": sb("nstart", [P, T]), "ones": sb("ones", [P, P]), "eps": sb("epsv", [P, 2])},
             "ptab": sb("ptab", [P, 3, P]), "modT": sb("modT", [P, 96, 2]),
             "A1": sb("A1", [P, KT, 2]), "A2": sb("A2", [P, KT, 2]), "aff": sb("aff", [P, TT, NE]), "slot": sb("slot", [P, TT, NE]),
             "outr": nc.dram_tensor("outr_scratch", (PAIRS, P, T), F32, kind="Internal").ap(),
             "outh": nc.dram_tensor("outh_scratch", (HG_HEADS, P, T), F32, kind="Internal").ap()}
        with nc.sbuf_tensor("hT", [P, KT, T], F32) as hT:
            S["hT"] = hT
            stage_modulation(nc, I, S)
            stage_masks(nc, S)
            with nc.sbuf_tensor("lora", [P, 3, T], F32) as lora, nc.sbuf_tensor("lw", [P, 3, 2, P], F32) as lw:
                S["lora"], S["lw"] = lora, lw
                stage_lora(nc, I, S)
                with cleared_semaphores(nc):
                    stage_rwkv(nc, I, O, S, per)
            with cleared_semaphores(nc):
                stage_hgrn(nc, I, O, S, per)
            with nc.sbuf_tensor("mergedT", [P, KT, T], F32) as mergedT:
                S["mergedT"] = mergedT
                stage_merge(nc, I, S)
                with nc.sbuf_tensor("x1a", [P, KT, T], F32) as x1T, nc.sbuf_tensor("rows_a", [P, TT, D], F32) as rows:
                    S["x1T"], S["rows"] = x1T, rows
                    stage_out_norm(nc, I, S)
                    stage_choose(nc, S)
                    stage_experts(nc, I, S)
                    stage_final(nc, I, O, S)
        return S


PER = {'bd_factors': 6,
 'bdn_ready': 30,
 'bdnt_ready': 24,
 'bdtt_ready': 6,
 'bdv_ready': 3,
 'bonus_products': 1,
 'bonus_ready': 1,
 'bonus_sums': 1,
 'cn_ready': 48,
 'derived': 1,
 'exps': 8,
 'factors': 8,
 'final_free': 3,
 'final_ready': 2,
 'final_taken': 2,
 'final_turned': 2,
 'gate_sums': 1,
 'grams': 6,
 'grams_taken': 6,
 'hg_att_taken': 15,
 'hg_diag_ready': 1,
 'hg_fin_free': 1,
 'hg_fin_ready': 2,
 'hg_grams': 15,
 'hg_k_turned': 2,
 'hg_kn_ready': 2,
 'hg_kv_sums': 2,
 'hg_norm_root': 1,
 'hg_norm_sums': 1,
 'hg_o_squares': 1,
 'hg_o_sums': 1,
 'hg_projected': 5,
 'hg_raw_free': 1,
 'hg_raw_taken': 5,
 'hg_round_done': 1,
 'hg_s0_free': 1,
 'hg_scaled': 14,
 'hg_state_factors': 2,
 'hg_states_ready': 1,
 'hg_v_turned': 1,
 'hg_vector_line': 64,
 'hg_vn_ready': 1,
 'hg_w_free': 1,
 'kk_max': 1,
 'kk_raw': 1,
 'kk_ready': 1,
 'kk_root': 1,
 'kk_squares': 1,
 'kk_sums': 1,
 'ln_root': 1,
 'logs': 2,
 'lora_sums': 2,
 'lora_taken': 4,
 'lw_free': 1,
 'mean_sums': 1,
 'mixed': 3,
 'n_turned': 24,
 'nr_ready': 20,
 'projected': 3,
 'r_sums': 20,
 'raw_free': 1,
 'raw_ready': 3,
 'round_done': 1,
 'rows_taken': 12,
 'rows_turned': 12,
 's0_free': 2,
 's0_ready': 2,
 's0_spread': 2,
 's0_turned': 2,
 'sa_ready': 40,
 'sa_sums': 20,
 'squared': 30,
 'state_ready': 20,
 'state_sums': 20,
 'tt_ready': 30,
 'tt_sums': 30,
 'v_spread': 2,
 'v_turned': 3,
 'var_sums': 1,
 'vector_line': 106,
 'w_free': 1,
 'y_squares': 1,
 'y_squares_in': 1,
 'y_sums': 20,
 'y_taken': 2}


_INS = ["x_prompt", "x_sample", "c", "state_rwkv", "state_hgrn", "c_ctx", "norm1_g", "norm2_g", "final_norm_g",
        "ada_w", "ada_b", "w_in", "rw_mu", "rw_w0", "rw_w2", "rw_a0", "rw_a2", "rw_g2", "rw_k_k", "rw_k_a", "rw_r_k",
        "rw_ln_w", "rw_ln_b", "hg_lb", "hg_norm_g", "w_br_rwkv", "w_br_hgrn", "w_out", "moe_router",
        "moe_w_gate", "moe_w_up", "moe_w_down"]
_OUTS = [("y_prompt", (1, NP, D)), ("y_sample", (1, NS, D)), ("new_state_rwkv", (1, 1, 2, RW_HEADS, 64, 64)),
         ("new_state_hgrn", (1, 1, 2, HG_HEADS, P, P))]


def kernel(**inputs):
    import numpy as _np
    import concourse.bacc as _bacc
    from concourse.bass_utils import run_bass_kernel_spmd as _run

    nc = _bacc.Bacc("TRN2", target_bir_lowering=False, num_devices=1)
    arrays, I, O = {}, {}, {}
    for name in _INS:
        a = _np.ascontiguousarray(inputs[name])
        arrays[f"in_{name}"] = a
        I[name] = nc.dram_tensor(f"in_{name}", a.shape, F32, kind="ExternalInput").ap()
    for name, shape in _OUTS:
        O[name] = nc.dram_tensor(f"out_{name}", shape, F32, kind="ExternalOutput").ap()
    build_layer(nc, I, O)
    r = _run(nc, [arrays], core_ids=[0])
    return tuple(r.results[0][f"out_{name}"] for name, _ in _OUTS)
```

```python
from contextlib import ExitStack, contextmanager
import math

import concourse.bass as bass
from concourse import mybir

P = 128
D = 2048
KT = D // P
NS, NP = 512, 128
T = NS + NP
TT = T // P
GRID_W = 64
RW_HEADS, RW_DIM = 16, 1024
PAIRS = RW_HEADS // 2
L = 64
NCH = T // L
HG_HEADS = 8
RW_COLS = 3456
HG0 = RW_COLS
HG_DIM = 1024
GATE0 = RW_COLS + 5 * HG_DIM
NE, FF = 16, 1024
CAP_S, CAP_P = 2 * NS // NE, 2 * NP // NE
EPS = 1e-6
LN_EPS = 64e-5
DECAY_SCALE = math.exp(-0.5)

F32 = mybir.dt.float32
I32 = mybir.dt.int32
ALU = mybir.AluOpType
ACT = mybir.ActivationFunctionType
AX_X = mybir.AxisListType.X

ADA_B, C_S, C_P = 0, 96, 112
MU0, MU1, K_K, K_A, R_K, W0, A0, LN_W, LN_B, MUL0, MUL1 = 0, 24, 48, 56, 64, 72, 88, 104, 112, 120, 123
G1, G2, LB0, LB1, HGN = 0, 16, 32, 48, 64


@contextmanager
def cleared_semaphores(nc):
    before = nc.snapshot_sems()
    yield
    nc.clear_and_free_semaphores(nc.allocated_since(before))
    nc.all_engine_barrier()


class Signal:

    def __init__(self, ctx, nc, name, per=0):
        self.sem, self.name, self.per = nc.alloc_semaphore(name), name, per

    def at(self, n, rnd=None):
        assert n > 0, self.name
        return n if rnd is None else rnd * self.per + n


def bcast(ap, n, axis):
    v = ap.unsqueeze(axis)
    shape = list(v.shape)
    shape[axis] = n
    return v.broadcast_to(shape)


def stage_modulation(nc, I, S):
    with ExitStack() as ctx:
        sb = lambda name, shape, dt=F32: ctx.enter_context(nc.sbuf_tensor(name, shape, dt))
        sg = lambda name: ctx.enter_context(nc.semaphore(name))
        RING, CT = 3, 4
        NBLK = 6 * D // (CT * P)
        rows = sb("rows", [P, 3, P])
        xt = sb("xt", [P, TT, D])
        junk = sb("junk", [P, D])
        ssq = sb("ssq", [P, TT])
        std = sb("std", [P, TT])
        rstd = sb("rstd", [P, TT])
        th = sb("th", [P, 2 * KT])
        cond = sb("cond", [P, KT, 2])
        eps = sb("eps", [P, 1])
        ring = [sb(f"ada{i}", [P, KT, CT * P]) for i in range(RING)]
        modrow = [S["hT"][0:2, :, :].rearrange("p k t -> p (k t)"), junk[0:2, :]]
        ps = ctx.enter_context(nc.psum_tensor("psA", [P, 8, 512], F32))
        s_par, s_x, s_id, s_const = sg("params_in"), sg("x_in"), sg("ident_made"), sg("consts_made")
        s_ada = [sg(f"ada_in{i}") for i in range(RING)]
        s_adaf = [sg(f"ada_free{i}") for i in range(RING)]
        s_modc = [sg(f"mod_copied{i}") for i in range(RING)]
        s_ptr, s_ptab, s_th, s_cond = sg("param_rows_turned"), sg("param_tables"), sg("cond_tanh"), sg("cond_ready")
        s_mod, s_modT, s_ssq, s_std, s_xn = sg("mod_sums"), sg("mod_ready"), sg("ssq_ready"), sg("std_ready"), sg("x_normed")
        s_xT, s_h, s_hd, s_v = sg("x_turned"), sg("h_ready"), sg("h_bank_free"), sg("vector_line")
        block = ctx.enter_context(nc.Block())
        mod = ps[:, 3, 0:192].rearrange("p (n s) -> p n s", s=2)

        @block.sync
        def _(sp):
            def rowv(name, r):
                a = I[name]
                if name == "rw_r_k":
                    a = a.rearrange("o (n h) k -> (o n) (h k)", h=2)
                else:
                    letters = "abc"[:len(a.shape) - 1]
                    a = a.rearrange(" ".join(letters) + " (n p) -> (" + " ".join(letters) + " n) p", p=P)
                return a if r is None else a[r[0]:r[1], :]
            table = [(0, ADA_B, "ada_b", None), (0, C_S, "c", None),
                     (1, K_K, "rw_k_k", None), (1, K_A, "rw_k_a", None), (1, R_K, "rw_r_k", None),
                     (1, W0, "rw_w0", None), (1, A0, "rw_a0", None), (1, LN_W, "rw_ln_w", None),
                     (1, LN_B, "rw_ln_b", None),
                     (1, MU0, "rw_mu", (0, 24)), (1, MUL0, "rw_mu", (24, 27)), (1, MU1, "rw_mu", (27, 51)),
                     (1, MUL1, "rw_mu", (51, 54)),
                     (2, G1, "norm1_g", None), (2, G2, "norm2_g", None), (2, LB0, "hg_lb", None),
                     (2, HGN, "hg_norm_g", None)]
            n = 0
            for t, r, name, cut in table:
                v = rowv(name, cut)
                sp.dma_start(rows[r:r + v.shape[0], t, :], v).then_inc(s_par, 16)
                n += 1
            sp.dma_start(rows[C_P:C_P + KT, 0, :], I["c_ctx"].rearrange("(n p) -> n p", p=P)).then_inc(s_par, 16)
            assert n + 1 == 18
            for t in range(TT):
                src = I["x_sample"][0, t * P:(t + 1) * P, :] if t < TT - 1 else I["x_prompt"][0]
                sp.dma_start(xt[:, t, :], src).then_inc(s_x, 16)
            w = I["ada_w"][0].rearrange("(k p) n -> p k n", p=P)
            for r in range(RING):
                sp.dma_start(ring[r][:, :, :], w[:, :, r * CT * P:(r + 1) * CT * P]).then_inc(s_ada[r], 16)
            with sp.Fori(1, NBLK // RING) as i:
                for r in range(RING):
                    sp.wait_ge(s_adaf[r], i)
                    sp.dma_start(ring[r][:, :, :], w[:, :, bass.ds((i * RING + r) * (CT * P), CT * P)]).then_inc(s_ada[r], 16)

        @block.gpsimd
        def _(pool):
            C = S["consts"]
            steps = [0]

            def link(ins):
                steps[0] += 1
                ins.then_inc(s_id, 1)
                pool.wait_ge(s_id, steps[0])
            link(nc.gpsimd.memset(C["ident"][:, :], 0.0))
            link(nc.gpsimd.affine_select(out=C["ident"][:, :], in_=C["ident"][:, :], compare_op=ALU.not_equal, fill=1.0,
                                         base=0, pattern=[[-1, P]], channel_multiplier=1))
            nc.gpsimd.memset(eps[:, :], EPS).then_inc(s_const, 1)

        @block.tensor
        def _(pe):
            ident = S["consts"]["ident"]
            pe.wait_ge(s_id, 2)
            pe.wait_ge(s_par, 18 * 16)
            for t, n in enumerate((128, 126, 72)):
                mm = nc.tensor.transpose(ps[:, 4 + t, 0:n], rows[0:n, t, :], ident[0:n, 0:n])
            mm.then_inc(s_ptr, 1)
            pe.wait_ge(s_cond, 1)
            with pe.Fori(0, NBLK // RING) as i:
                for r in range(RING):
                    pe.wait_ge(s_ada[r], i * 16 + 16)
                    pe.wait_ge(s_modc[r], i + 1)
                    for k in range(KT):
                        mm = nc.tensor.matmul(ps[0:2, r, :], cond[:, k, :], ring[r][:, k, :], start=(k == 0), stop=(k == KT - 1))
                    mm.then_inc(s_adaf[r], 1)
            for r in range(RING):
                pe.wait_ge(s_modc[r], NBLK // RING + 1)
            for n in range(NBLK * CT):
                mm = nc.tensor.transpose(ps[:, 3, 2 * n:2 * n + 2], modrow[n // (5 * KT)][:, n % (5 * KT) * P:(n % (5 * KT) + 1) * P],
                                         ident[0:2, 0:2])
            mm.then_inc(s_mod, 1)
            pe.wait_ge(s_xn, TT)
            for j in range(KT):
                b = 4 + 2 * (j % 2)
                if j >= 2:
                    pe.wait_ge(s_h, 2 * (j - 1))
                for t in range(TT):
                    bank = ps[:, b, t * P:(t + 1) * P] if t < TT - 1 else ps[:, b + 1, 0:P]
                    mm = nc.tensor.transpose(bank, xt[:, t, j * P:(j + 1) * P], ident[:, :])
                mm.then_inc(s_xT, 1)

        @block.scalar
        def _(act):
            act.wait_ge(s_const, 1)
            act.wait_ge(s_ptab, 3)
            nc.scalar.activation(th[:, :], S["ptab"][:, 0, C_S:C_S + 2 * KT], ACT.Tanh, scale=0.5).then_inc(s_th, 1)
            for t in range(TT):
                act.wait_ge(s_x, 16 * TT)
                if t:
                    act.wait_ge(s_ssq, t)
                nc.scalar.activation(junk[:, :], xt[:, t, :], ACT.Square, accum_out=ssq[:, t:t + 1]).then_inc(s_ssq, 1)
            for r in range(RING):
                act.sem_inc(s_modc[r], 1)
            act.wait_ge(s_ssq, TT)
            nc.scalar.activation(std[:, :], ssq[:, :], ACT.Sqrt, scale=1.0 / D, bias=eps[:, 0:1]).then_inc(s_std, 1)
            inner = 5 * D // (CT * P) // RING
            with act.Fori(0, inner) as i:
                for r in range(RING):
                    act.wait_ge(s_adaf[r], i + 1)
                    nc.scalar.activation(modrow[0][:, bass.ds((i * RING + r) * (CT * P), CT * P)], ps[0:2, r, :], ACT.Copy)\
                        .then_inc(s_modc[r], 1)
            for n in range(inner * RING, NBLK):
                place, col = divmod(n * CT * P, 5 * D)
                act.wait_ge(s_adaf[n % RING], n // RING + 1)
                nc.scalar.activation(modrow[place][:, col:col + CT * P], ps[0:2, n % RING, :], ACT.Copy).then_inc(s_modc[n % RING], 1)

        @block.vector
        def _(dve):
            steps = [0]

            def link(ins):
                steps[0] += 1
                ins.then_inc(s_v, 1)
                dve.wait_ge(s_v, steps[0])
            ptab, modT, A1, A2 = S["ptab"], S["modT"], S["A1"], S["A2"]
            dve.wait_ge(s_ptr, 1)
            for t, n in enumerate((128, 126, 72)):
                nc.vector.tensor_copy(ptab[:, t, 0:n], ps[:, 4 + t, 0:n]).then_inc(s_ptab, 1)
            dve.wait_ge(s_ptab, 3)
            dve.wait_ge(s_th, 1)
            link(nc.vector.tensor_scalar(th[:, :], th[:, :], 0.5, 0.5, ALU.mult, ALU.add))
            nc.vector.tensor_tensor(cond[:, :, :].rearrange("p k s -> p s k"), th[:, :].rearrange("p (s k) -> p s k", s=2),
                                    ptab[:, 0, C_S:C_S + 2 * KT].rearrange("p (s k) -> p s k", s=2), ALU.mult).then_inc(s_cond, 1)
            dve.wait_ge(s_std, 1)
            link(nc.vector.reciprocal(rstd[:, :], std[:, :]))
            for t in range(TT):
                nc.vector.tensor_scalar(xt[:, t, :], xt[:, t, :], rstd[:, t:t + 1], None, ALU.mult).then_inc(s_xn, 1)
            dve.wait_ge(s_mod, 1)
            link(nc.vector.tensor_tensor(modT[:, :, :], mod, bcast(ptab[:, 0, 0:96], 2, 2), ALU.add))
            for A, c, g in ((A1, KT, G1), (A2, 4 * KT, G2)):
                link(nc.vector.scalar_tensor_tensor(out=A[:, :, :], in0=modT[:, c:c + KT, :], scalar=1.0,
                                                    in1=bcast(ptab[:, 2, g:g + KT], 2, 2), op0=ALU.add, op1=ALU.mult))
            for j in range(KT):
                dve.wait_ge(s_xT, j + 1)
                b = 4 + 2 * (j % 2)
                nc.vector.tensor_scalar(S["hT"][:, j, 0:NS], ps[:, b, :], A1[:, j, 0:1], modT[:, j, 0:1],
                                        ALU.mult, ALU.add).then_inc(s_h, 1)
                nc.vector.tensor_scalar(S["hT"][:, j, NS:T], ps[:, b + 1, 0:NP], A1[:, j, 1:2], modT[:, j, 1:2],
                                        ALU.mult, ALU.add).then_inc(s_h, 1)
            dve.wait_ge(s_h, 2 * KT)


GROUPS = ((0, 4), (4, 4), (8, 2))
HALF = T // 2
LEVELS = 5


def half_view(ps, b):
    return ps[:, b:b + 2, 0:HALF]


def as_halves(ap):
    return ap.rearrange("p (a n) -> p a n", a=2)


def chunks(ap):
    return ap.rearrange("p (c l) -> p c l", l=L)


def stage_masks(nc, S):
    with ExitStack() as ctx:
        s_m = ctx.enter_context(nc.semaphore("mask_steps"))
        block = ctx.enter_context(nc.Block())
        C = S["consts"]

        @block.gpsimd
        def _(pool):
            n = [0]

            def link(ins):
                n[0] += 1
                ins.then_inc(s_m, 1)
                pool.wait_ge(s_m, n[0])

            def sel(ap, op, base, pattern, cm):
                link(nc.gpsimd.affine_select(out=ap, in_=ap, compare_op=op, fill=0.0, base=base, pattern=pattern,
                                             channel_multiplier=cm))
            bd = C["bd"]
            link(nc.gpsimd.memset(bd[:, :, :, :], 1.0))
            link(nc.gpsimd.memset(bd[:, 3:5, :, :], -1.0))
            for m in range(5):
                sel(bd[:, m], ALU.is_ge, 0, [[-L, 2], [0, L]], 1)
                sel(bd[:, m], ALU.is_ge, L - 1, [[L, 2], [0, L]], -1)
            sel(bd[:, 1], ALU.is_gt, 0, [[L, 2], [1, L]], -1)
            sel(bd[:, 2], ALU.is_gt, 0, [[-L, 2], [-1, L]], 1)
            sel(bd[:, 3], ALU.is_gt, 0, [[L, 2], [1, L]], -1)
            sel(bd[:, 4], ALU.is_gt, 0, [[-L, 2], [-1, L]], 1)
            cm = C["cm"]
            link(nc.gpsimd.memset(cm[:, :, :], 1.0))
            link(nc.gpsimd.memset(cm[:, 0, :], -1.0))
            link(nc.gpsimd.memset(cm[:, 2, :], -1.0))
            for h in range(2):
                q = slice(L * h, L * h + L)
                sel(cm[q, 0, :], ALU.is_gt, 0, [[1, L]], -1)
                sel(cm[q, 1, :], ALU.is_ge, 0, [[1, L]], -1)
                sel(cm[q, 2, :], ALU.is_gt, 0, [[-1, L]], 1)
                sel(cm[q, 3, :], ALU.is_ge, 0, [[-1, L]], 1)
            link(nc.gpsimd.memset(C["ci"][:, :], 0.0))
            for h in range(2):
                link(nc.gpsimd.affine_select(out=C["ci"][L * h:L * h + L, :], in_=C["ci"][L * h:L * h + L, :],
                                             compare_op=ALU.not_equal, fill=1.0, base=0, pattern=[[-1, L]],
                                             channel_multiplier=1))
            link(nc.gpsimd.memset(C["ns"][:, :], 1.0))
            link(nc.gpsimd.memset(chunks(C["ns"][:, :])[:, :, 0:1], 0.0))
            link(nc.gpsimd.memset(C["ones"][:, :], 1.0))
            link(nc.gpsimd.memset(C["eps"][:, 0:1], EPS))
            link(nc.gpsimd.memset(C["eps"][:, 1:2], LN_EPS))


def mix_neighbours(nc, link, out, raw, c, mu0, mu1):
    link(nc.vector.tensor_scalar(out, raw, c, None, ALU.mult))
    for cut, w in ((slice(0, NS), GRID_W), (slice(NS, T), NP)):
        o, r = (a[:, cut].rearrange("p (n w) -> p n w", w=w) for a in (out, raw))
        link(nc.vector.scalar_tensor_tensor(out=o[:, :, 1:w], in0=r[:, :, 0:w - 1], scalar=mu0, in1=o[:, :, 1:w],
                                            op0=ALU.mult, op1=ALU.add))
        link(nc.vector.scalar_tensor_tensor(out=o[:, :, 0:w - 1], in0=r[:, :, 1:w], scalar=mu1, in1=o[:, :, 0:w - 1],
                                            op0=ALU.mult, op1=ALU.add))


def stage_lora(nc, I, S):
    with ExitStack() as ctx:
        sb = lambda name, shape, dt=F32: ctx.enter_context(nc.sbuf_tensor(name, shape, dt))
        sg = lambda name: ctx.enter_context(nc.semaphore(name))
        w = sb("wlora", [P, KT, 3 * P])
        raw = sb("rawlora", [P, 3, T])
        cl = sb("clora", [P, 3])
        ps = ctx.enter_context(nc.psum_tensor("psL", [P, 8, 512], F32))
        s_w, s_p, s_raw, s_v, s_mix, s_th, s_z, s_out = map(sg, (
            "lora_w_in", "lora_projected", "lora_raw", "lora_vec", "lora_mixed", "lora_tanh", "lora_zeroed", "lora_rows"))
        block = ctx.enter_context(nc.Block())
        lora = S["lora"]

        @block.sync
        def _(sp):
            sp.dma_start(w[:, :, :], I["w_in"][0].rearrange("(k p) n -> p k n", p=P)[:, :, 3 * RW_DIM:RW_COLS]).then_inc(s_w, 16)

        @block.gpsimd
        def _(pool):
            nc.gpsimd.memset(S["lw"][:, :, :, :], 0.0).then_inc(s_z, 1)
            pool.wait_ge(s_z, 1)

        @block.tensor
        def _(pe):
            pe.wait_ge(s_w, 16)
            for i in range(3):
                for h in range(2):
                    for k in range(KT):
                        mm = nc.tensor.matmul(ps[:, 2 * i + h, 0:HALF], w[:, k, i * P:(i + 1) * P],
                                              S["hT"][:, k, h * HALF:(h + 1) * HALF], start=(k == 0), stop=(k == KT - 1))
                mm.then_inc(s_p, 1)

        @block.scalar
        def _(act):
            for i in range(3):
                act.wait_ge(s_p, i + 1)
                nc.scalar.activation(as_halves(raw[:, i, :]), half_view(ps, 2 * i), ACT.Copy).then_inc(s_raw, 1)
            act.wait_ge(s_mix, 1)
            nc.scalar.activation(lora[:, 0, :], lora[:, 0, :], ACT.Tanh).then_inc(s_th, 1)
            nc.scalar.activation(lora[:, 2, :], lora[:, 2, :], ACT.Tanh, scale=0.5).then_inc(s_th, 1)

        @block.vector
        def _(dve):
            steps = [0]

            def link(ins):
                steps[0] += 1
                ins.then_inc(s_v, 1)
                dve.wait_ge(s_v, steps[0])
            t1 = S["ptab"][:, 1, :]
            link(nc.vector.tensor_tensor(cl[:, :], t1[:, MUL0:MUL0 + 3], t1[:, MUL1:MUL1 + 3], ALU.add))
            link(nc.vector.tensor_scalar(cl[:, :], cl[:, :], -1.0, 1.0, ALU.mult, ALU.add))
            for i in range(3):
                dve.wait_ge(s_raw, i + 1)
                mix_neighbours(nc, link, lora[:, i, :], raw[:, i, :], cl[:, i:i + 1], t1[:, MUL0 + i:MUL0 + i + 1],
                               t1[:, MUL1 + i:MUL1 + i + 1])
            dve.sem_inc(s_mix, 1)
            dve.wait_ge(s_th, 2)
            link(nc.vector.tensor_scalar(lora[:, 2, :], lora[:, 2, :], 0.5, 0.5, ALU.mult, ALU.add))


def stage_rwkv(nc, I, O, S, per):
    with ExitStack() as ctx:
        sb = lambda name, shape, dt=F32: ctx.enter_context(nc.sbuf_tensor(name, shape, dt))
        C = S["consts"]
        sig = {}

        def signal(name):
            if name not in sig:
                sig[name] = Signal(ctx, nc, "rw_" + name, per.get(name, 0))
            return sig[name]
        w = sb("wrkv", [P, 3, KT, P])
        raw = sb("raw", [P, 3, T])
        mix = sb("mix", [P, 3, T])
        kk, kds, ysum = sb("kk", [P, T]), sb("kds", [P, T]), sb("ysum", [P, T])
        t1, t2, t3, t4, t5 = (sb(f"t{i}", [P, T]) for i in range(1, 6))
        outr = sb("outr", [P, T])
        t6, t7, t8 = (raw[:, i, :] for i in range(3))
        pp, dp, tot, etot = sb("pp", [P, 15]), sb("dp", [P, 9]), sb("tot", [P, NCH]), sb("etot", [P, NCH])
        KR = sb("KR", [P, NCH, 2, L])
        cB = sb("cB", [P, NCH, L])
        bdB, bdK, bdKW, bdBn, bdKn, bdV = (sb(n, [P, NCH, 2, L]) for n in ("bdB", "bdK", "bdKW", "bdBn", "bdKn", "bdV"))
        cV, RbT, RkT, TTc, cN = (sb(n, [P, NCH, L]) for n in ("cV", "RbT", "RkT", "TTc", "cN"))
        bdAk, bdTT, bdNT = (sb(n, [P, NCH, 2, L]) for n in ("bdAk", "bdTT", "bdNT"))
        bdN = bdTT
        Sc, bdS, nR, cSA, bdSA = (sb("Sc", [P, 2, L]), sb("bdS", [P, 2, 2, L]), sb("nR", [P, L]), sb("cSA", [P, L]),
                                  sb("bdSA", [P, 2, L]))
        s0 = sb("s0", [P, 2, L])
        sout = sb("sout", [P, 2, L])
        ps = ctx.enter_context(nc.psum_tensor("psR", [P, 8, 512], F32))
        block = ctx.enter_context(nc.Block())
        g2 = S["lw"]
        lora = S["lora"]
        ident = C["ident"][:, :]
        blk = C["bd"][:, 0]
        blockones = blk.rearrange("p g l -> p (g l)")

        def bank(b, n, width):
            return ps[:, b, 0:n * width].rearrange("p (c l) -> p c l", l=width)
        GB = (4, 5, 6)

        def sq_view(g, n):
            return ps[:, GB[g], 0:n * L].rearrange("p (c l) -> p c l", l=L)

        def tt_view(g, n):
            return ps[:, GB[g], n * L:2 * n * L].rearrange("p (c l) -> p c l", l=L)

        def tr_view(g, n):
            return ps[:, 7, 0:n * P].rearrange("p (c l) -> p c l", l=P)

        def chain():
            return lambda d: [(c, c == 0, c == 7) if d == 0 else (7 - c, c == 0, c == 7) for c in range(8)] + \
                [(8 + e if d == 0 else 9 - e, e == 0, e == 1) for e in range(2)]
        steps_of = chain()

        @block.sync
        def _(sp):
            win = I["w_in"][0].rearrange("(k p) n -> p k n", p=P)
            rw = lambda n: signal(n)
            sp.sem_inc(rw("final_free").sem, 3)
            with sp.Fori(0, PAIRS) as r:
                sp.wait_ge(rw("w_free").sem, r * rw("w_free").per + 1)
                for i in range(3):
                    sp.dma_start(w[:, i, :, :], win[:, :, bass.ds(i * RW_DIM + r * P, P)]).then_inc(rw("w_in").sem, 16)
                sp.wait_ge(rw("lw_free").sem, r * rw("lw_free").per + 1)
                for j, name in enumerate(("rw_w2", "rw_a2")):
                    for d in range(2):
                        sp.dma_start(g2[L * d:L * d + L, j, d, :], I[name][0, d][:, bass.ds(r * P, P)]).then_inc(rw("lw_in").sem, 16)
                sp.dma_start(g2[:, 2, 0, :], I["rw_g2"][0][:, bass.ds(r * P, P)]).then_inc(rw("lw_in").sem, 16)
                for d in range(2):
                    sp.wait_ge(rw("s0_free").sem, r * 2 + d + 1)
                    sp.dma_start(s0[:, d, :], I["state_rwkv"][0, 0, d].rearrange("h v k -> (h v) k")[bass.ds(r * P, P), :])\
                        .then_inc(rw(f"s0_in{d}").sem, 16)
                for d in range(2):
                    sp.wait_ge(rw("final_ready").sem, r * 2 + d + 1)
                    sp.dma_start(O["new_state_rwkv"][0, 0, d].rearrange("h v k -> (h v) k")[bass.ds(r * P, P), :], sout[:, d, :])\
                        .then_inc(rw("final_out").sem, 16)
                    sp.wait_ge(rw("final_out").sem, r * 48 + 16 * (d + 1))
                    sp.sem_inc(rw("final_free").sem, 1)
                sp.wait_ge(rw("round_done").sem, r + 1)
                sp.dma_start(S["outr"][bass.ds(r, 1)].rearrange("o p n -> (o p) n"), outr[:, :]).then_inc(rw("final_out").sem, 16)
                sp.wait_ge(rw("final_out").sem, r * 48 + 48)
                sp.sem_inc(rw("final_free").sem, 1)

        @block.gpsimd
        def _(pool):
            nc.gpsimd.memset(bdK[:, :, :, :], 0.0).then_inc(signal("bdk_zeroed").sem, 1)
            with pool.Fori(0, PAIRS) as r:
                for d in range(2):
                    def bd(out, src, need):
                        pool.wait_ge(signal("factors").sem, signal("factors").at(4 * d + need, r))
                        nc.gpsimd.tensor_tensor(out[:, :, :, :], bcast(src, 2, 2), bcast(blk, NCH, 1), ALU.mult)\
                            .then_inc(signal("bd_factors").sem, 1)
                    bd(bdKW, KR[:, :, 0, :], 1)
                    bd(bdB, cB[:, :, :], 3)
                    bd(bdK, chunks(t3[:, :]), 4)

        @block.tensor
        def _(pe):
            W = lambda name, n, r: pe.wait_ge(signal(name).sem, signal(name).at(n, r))
            cnt = {}

            def inc(mm, name):
                mm.then_inc(signal(name).sem, 1)
                cnt[name] = cnt.get(name, 0) + 1
            pe.sem_inc(signal("w_free").sem, 1)
            pe.sem_inc(signal("lw_free").sem, 1)
            with pe.Fori(0, PAIRS) as r:
                cnt.clear()

                def sums(lhsT, rhs, b):
                    for h in range(2):
                        mm = nc.tensor.matmul(ps[:, b + h, 0:HALF], lhsT, rhs[:, h * HALF:(h + 1) * HALF], start=True, stop=True)
                    return mm
                pe.wait_ge(signal("w_in").sem, r * 48 + 48)
                for i in range(3):
                    if i == 2:
                        W("raw_ready", 1, r)
                    for h in range(2):
                        for k in range(KT):
                            mm = nc.tensor.matmul(ps[:, 2 * (i % 2) + h, 0:HALF], w[:, i, k, :],
                                                  S["hT"][:, k, h * HALF:(h + 1) * HALF], start=(k == 0), stop=(k == KT - 1))
                    if i == 2:
                        mm.then_inc(signal("projected").sem, 1)
                    else:
                        mm.then_inc(signal("projected").sem, 1)
                cnt["projected"] = 3
                pe.wait_ge(signal("projected").sem, signal("projected").at(3, r))
                pe.sem_inc(signal("w_free").sem, 1)
                cnt["w_free"] = 1
                W("kk_squares", 1, r)
                inc(sums(blockones, t1[:, :], 4), "kk_sums")
                W("v_spread", 2, r)
                W("kk_max", 1, r)
                for g, (c0, n) in enumerate(GROUPS):
                    for c in range(c0, c0 + n):
                        mm = nc.tensor.transpose(ps[:, 4 + g, (c - c0) * P:(c - c0 + 1) * P], bdK[:, c].rearrange("p g l -> p (g l)"), ident)
                    inc(mm, "v_turned")
                W("bdv_ready", 3, r)
                pe.wait_ge(signal("lw_in").sem, r * 80 + 80)
                for d in range(2):
                    if d:
                        W("y_taken", 1, r)
                        W("final_taken", 1, r)
                    sums(g2[:, 0, d, :], lora[:, 0, :], 4)
                    inc(sums(g2[:, 1, d, :], lora[:, 1, :], 6), "lora_sums")
                    W("lora_taken", 2 * d + 2, r)
                    W("bd_factors", 3 * d + 3, r)
                    flat = lambda a, c: a[:, c].rearrange("p g l -> p (g l)")
                    for g, (c0, n) in enumerate(GROUPS):
                        if g:
                            W("grams_taken", 3 * d + g, r)
                        for b, lhs in ((4, bdB), (5, bdK)):
                            for c in range(c0, c0 + n):
                                nc.tensor.matmul(ps[:, b, (c - c0) * P:(c - c0 + 1) * P], flat(lhs, c), flat(KR, c), start=True, stop=True)
                        for c in range(c0, c0 + n):
                            mm = nc.tensor.matmul(ps[:, 6, (c - c0) * L:(c - c0 + 1) * L], flat(bdKW, c), cB[:, c, :], start=True, stop=True)
                        inc(mm, "grams")
                        for b, src in ((7, bdB), (7, bdK)):
                            k = 6 * d + 2 * g + (src is bdK)
                            if k:
                                W("rows_taken", k, r)
                            for c in range(c0, c0 + n):
                                mm = nc.tensor.transpose(ps[:, b, (c - c0) * P:(c - c0 + 1) * P], flat(src, c), ident)
                            inc(mm, "rows_turned")
                    W("grams_taken", 3 * d + 3, r)
                    W("rows_taken", 6 * d + 6, r)
                    for i in range(LEVELS):
                        last = i == LEVELS - 1
                        for g, (c0, n) in enumerate(GROUPS):
                            if i:
                                W("bdnt_ready", 4 * 3 * d + 3 * (i - 1) + g + 1, r)
                                W("cn_ready", 2 * (12 * d + 3 * (i - 1) + g + 1), r)
                                W("tt_ready", 15 * d + 3 * (i - 1) + g + 1, r)
                            for c in range(c0, c0 + n):
                                mm = nc.tensor.matmul(sq_view(g, n)[:, c - c0, :], flat(bdNT, c), cN[:, c, :], start=True, stop=True)
                            inc(mm, "squared")
                        for g, (c0, n) in enumerate(GROUPS):
                            k = 15 * d + 3 * i + g + 1
                            W("bdn_ready", k, r)
                            for c in range(c0, c0 + n):
                                mm = nc.tensor.matmul(tt_view(g, n)[:, c - c0, :], flat(bdN, c), TTc[:, c, :], start=True, stop=True)
                            inc(mm, "tt_sums")
                            if not last:
                                if g:
                                    W("bdnt_ready", 12 * d + 3 * i + g, r)
                                for c in range(c0, c0 + n):
                                    mm = nc.tensor.transpose(tr_view(g, n)[:, c - c0, :], flat(bdN, c), ident)
                                inc(mm, "n_turned")
                    W("bdtt_ready", 3 * d + 3, r)
                    W("s0_spread", d + 1, r)
                    inc(nc.tensor.transpose(ps[:, 4, 0:P], bdSA[:, :, :].rearrange("p g l -> p (g l)"), ident), "s0_turned")
                    Yv = lambda c: ps[:, 6, c * L:(c + 1) * L] if c < 8 else ps[:, 7, (c - 8) * L:(c - 7) * L]
                    for j, (c, first, lastc) in enumerate(steps_of(d)):
                        hs = c < 8 or not first
                        q = j % 2
                        k = 10 * d + j + 1
                        if j == 0:
                            W("s0_ready", d + 1, r)
                        else:
                            W("state_ready", k - 1, r)
                        mm = nc.tensor.matmul(ps[:, 4, P:P + L], flat(bdAk, c), cV[:, c, :], start=True, stop=not hs)
                        if hs:
                            mm = nc.tensor.matmul(ps[:, 4, P:P + L], flat(bdKW, c), Sc[:, q, :], start=False, stop=True)
                        inc(mm, "r_sums")
                        W("nr_ready", k, r)
                        inc(nc.tensor.matmul(ps[:, 5, 0:L], flat(bdTT, c), nR[:, :], start=True, stop=True), "sa_sums")
                        W("sa_ready", 2 * k, r)
                        nc.tensor.matmul(ps[:, 5, P:P + L], flat(bdBn, c), cSA[:, :], start=True, stop=False)
                        if hs:
                            nc.tensor.matmul(ps[:, 5, P:P + L], ident, Sc[:, q, :], start=False, stop=False)
                        inc(nc.tensor.matmul(ps[:, 5, P:P + L], flat(bdKn, c), cV[:, c, :], start=False, stop=True), "state_sums")
                        nc.tensor.matmul(Yv(c), flat(bdV, c), RkT[:, c, :], start=True, stop=False)
                        if hs:
                            nc.tensor.matmul(Yv(c), bdS[:, q].rearrange("p g l -> p (g l)"), KR[:, c, 1, :], start=False, stop=False)
                        inc(nc.tensor.matmul(Yv(c), bdSA[:, :, :].rearrange("p g l -> p (g l)"), RbT[:, c, :], start=False, stop=True), "y_sums")
                    W("state_ready", 10 * d + 10, r)
                    inc(nc.tensor.transpose(ps[:, 4, 0:P], bdS[:, 0].rearrange("p g l -> p (g l)"), ident), "final_turned")
                W("y_taken", 2, r)
                W("final_taken", 2, r)
                W("bonus_products", 1, r)
                inc(sums(blockones, t1[:, :], 4), "bonus_sums")
                inc(sums(blockones, ysum[:, :], 6), "mean_sums")
                W("bonus_ready", 1, r)
                inc(sums(g2[:, 2, 0, :], lora[:, 2, :], 4), "gate_sums")
                W("y_squares", 1, r)
                inc(sums(blockones, t2[:, :], 6), "var_sums")
                pe.wait_ge(signal("var_sums").sem, signal("var_sums").at(1, r))
                pe.sem_inc(signal("lw_free").sem, 1)
                W("round_done", 1, r)
                for n in cnt:
                    assert True
            S["pe_cnt"] = dict(cnt)

        @block.scalar
        def _(act):
            W = lambda name, n, r: act.wait_ge(signal(name).sem, signal(name).at(n, r))
            cnt = {}

            def inc(ins, name):
                ins.then_inc(signal(name).sem, 1)
                cnt[name] = cnt.get(name, 0) + 1
            act.wait_ge(signal("bdk_zeroed").sem, 1)
            with act.Fori(0, PAIRS) as r:
                cnt.clear()
                A = nc.scalar.activation
                for i in range(3):
                    W("projected", i + 1, r)
                    W("raw_free", 1, r)
                    inc(A(as_halves(raw[:, i, :]), half_view(ps, 2 * (i % 2)), ACT.Copy), "raw_ready")
                W("mixed", 3, r)
                for h in range(2):
                    q = slice(L * h, L * h + L)
                    inc(A(bdK[q, :, h, :], chunks(mix[q, 2, :]), ACT.Copy), "v_spread")
                W("kk_raw", 1, r)
                inc(A(t1[:, :], kk[:, :], ACT.Square), "kk_squares")
                W("kk_max", 1, r)
                inc(A(t2[:, :], t2[:, :], ACT.Sqrt), "kk_root")
                for g, (c0, n) in enumerate(GROUPS):
                    W("v_turned", g + 1, r)
                    inc(A(bdV[:, c0:c0 + n].rearrange("p c g l -> p c (g l)"), bank(4 + g, n, P), ACT.Copy), "bdv_ready")
                for d in range(2):
                    W("lora_sums", d + 1, r)
                    if d == 0:
                        W("kk_ready", 1, r)
                    W("derived", 1, r)
                    inc(A(as_halves(t1[:, :]), half_view(ps, 4), ACT.Tanh, scale=0.5, bias=dp[:, 3 + d:4 + d]), "lora_taken")
                    if d:
                        W("bd_factors", 3, r)
                    inc(A(as_halves(t2[:, :]), half_view(ps, 6), ACT.Tanh, scale=0.5, bias=dp[:, 5 + d:6 + d]), "lora_taken")
                    W("logs", d + 1, r)
                    inc(A(etot[:, :], tot[:, :], ACT.Exp), "exps")
                    inc(A(t6, t5[:, :], ACT.Exp), "exps")
                    inc(A(t7, t4[:, :], ACT.Exp), "exps")
                    inc(A(t8, t4[:, :], ACT.Exp, scale=-1.0), "exps")
                    for g, (c0, n) in enumerate(GROUPS):
                        for m, out in enumerate((bdBn, bdKn)):
                            W("rows_turned", 6 * d + 2 * g + m + 1, r)
                            inc(A(out[:, c0:c0 + n].rearrange("p c g l -> p c (g l)"), bank(7, n, P), ACT.Copy), "rows_taken")
                    for i in range(LEVELS - 1):
                        for g, (c0, n) in enumerate(GROUPS):
                            W("bdn_ready", 15 * d + 3 * i + g + 1, r)
                            for h in range(2):
                                q = slice(L * h, L * h + L)
                                inc(A(cN[q, c0:c0 + n, :], bdN[q, c0:c0 + n, h, :], ACT.Copy), "cn_ready")
                        for g, (c0, n) in enumerate(GROUPS):
                            W("n_turned", 12 * d + 3 * i + g + 1, r)
                            inc(A(bdNT[:, c0:c0 + n].rearrange("p c g l -> p c (g l)"), tr_view(g, n), ACT.Copy), "bdnt_ready")
                    for j in range(10):
                        k = 10 * d + j + 1
                        W("r_sums", k, r)
                        inc(A(nR[:, :], ps[:, 4, P:P + L], ACT.Copy, scale=-1.0), "nr_ready")
                W("y_squares_in", 1, r)
                inc(A(t2[:, :], t4[:, :], ACT.Square), "y_squares")
                W("var_sums", 1, r)
                inc(A(as_halves(t5[:, :]), half_view(ps, 6), ACT.Sqrt, scale=1.0 / L, bias=C["eps"][:, 1:2]), "ln_root")
            S["act_cnt"] = dict(cnt)

        @block.vector
        def _(dve):
            W = lambda name, n, r: dve.wait_ge(signal(name).sem, signal(name).at(n, r))
            V = nc.vector
            dve.sem_inc(signal("raw_free").sem, 1)
            dve.sem_inc(signal("s0_free").sem, 2)
            cnt = {}
            with dve.Fori(0, PAIRS) as r:
                cnt.clear()

                def did(ins, name):
                    cnt[name] = cnt.get(name, 0) + 1
                    ins.then_inc(signal(name).sem, 1)
                    dve.wait_ge(signal(name).sem, signal(name).at(cnt[name], r))
                link = lambda ins: did(ins, "vector_line")

                def raised(name, k=1):
                    dve.sem_inc(signal(name).sem, k)
                    cnt[name] = cnt.get(name, 0) + k
                link(V.tensor_copy(pp[:, :], S["ptab"][:, 1, 0:120].rearrange("p (n e) -> p n e", e=PAIRS)[:, :, bass.ds(r, 1)].rearrange("p n e -> p (n e)")))
                link(V.tensor_tensor(dp[:, 0:3], pp[:, 0:3], pp[:, 3:6], ALU.add))
                link(V.tensor_scalar(dp[:, 0:3], dp[:, 0:3], -1.0, 1.0, ALU.mult, ALU.add))
                link(V.tensor_scalar(dp[:, 3:7], pp[:, 9:13], 0.5, None, ALU.mult))
                link(V.tensor_scalar(dp[:, 7:8], pp[:, 7:8], 0.5, None, ALU.mult))
                did(V.tensor_scalar(dp[:, 8:9], pp[:, 7:8], -0.5, 1.0, ALU.mult, ALU.add), "derived")
                for i in range(3):
                    W("raw_ready", i + 1, r)
                    mix_neighbours(nc, link, mix[:, i, :], raw[:, i, :], dp[:, i:i + 1], pp[:, i:i + 1], pp[:, 3 + i:4 + i])
                    raised("mixed")
                rT, kT, vT = mix[:, 0, :], mix[:, 1, :], mix[:, 2, :]
                did(V.tensor_scalar(kk[:, :], kT, pp[:, 6:7], None, ALU.mult), "kk_raw")
                W("kk_sums", 1, r)
                did(V.tensor_scalar(as_halves(t2[:, :]), half_view(ps, 4), 1e-24, None, ALU.max), "kk_max")
                W("kk_root", 1, r)
                link(V.reciprocal(t2[:, :], t2[:, :]))
                did(V.tensor_tensor(kk[:, :], kk[:, :], t2[:, :], ALU.mult), "kk_ready")
                W("bdv_ready", 3, r)
                link(V.tensor_tensor(cV[:, :, :], bdV[:, :, 0, :], bdV[:, :, 1, :], ALU.add))
                for d in range(2):
                    mT, mI, mN = (1, 1, 2) if d == 0 else (2, 3, 1)
                    W("lora_taken", 2 * d + 2, r)
                    link(V.tensor_scalar(t1[:, :], t1[:, :], -0.5 * DECAY_SCALE, -0.5 * DECAY_SCALE, ALU.mult, ALU.add))
                    link(V.tensor_scalar(t3[:, :], t2[:, :], dp[:, 7:8], dp[:, 8:9], ALU.mult, ALU.add))
                    link(V.tensor_tensor(t3[:, :], t3[:, :], kT, ALU.mult))
                    if d == 0:
                        link(V.tensor_copy(kds[:, :], t3[:, :]))
                    else:
                        link(V.tensor_tensor(kds[:, :], kds[:, :], t3[:, :], ALU.add))
                    link(V.tensor_scalar(t2[:, :], t2[:, :], 0.5, 0.5, ALU.mult, ALU.add))
                    link(V.tensor_tensor(t2[:, :], t2[:, :], kk[:, :], ALU.mult))
                    link(V.tensor_tensor_scan(t4[:, :], C["ns"][:, :], t1[:, :], 0.0, ALU.mult, ALU.add))
                    link(V.tensor_copy(tot[:, :].rearrange("p (c o) -> p c o", o=1), chunks(t4[:, :])[:, :, L - 1:L]))
                    if d == 0:
                        did(V.tensor_tensor(t5[:, :], t4[:, :], t1[:, :], ALU.subtract), "logs")
                    else:
                        link(V.tensor_tensor(chunks(t5[:, :]), bcast(tot[:, :], L, 2), chunks(t4[:, :]), ALU.subtract))
                        did(V.tensor_tensor(t4[:, :], t5[:, :], t1[:, :], ALU.add), "logs")
                    W("exps", 4 * d + 4, r)
                    did(V.tensor_tensor(KR[:, :, 0, :], chunks(kk[:, :]), chunks(t6), ALU.mult), "factors")
                    did(V.tensor_tensor(KR[:, :, 1, :], chunks(rT), chunks(t7), ALU.mult), "factors")
                    did(V.tensor_tensor(cB[:, :, :], chunks(t2[:, :]), chunks(t8), ALU.mult), "factors")
                    did(V.tensor_tensor(t3[:, :], t3[:, :], t8, ALU.mult), "factors")
                    if d:
                        raised("raw_free")
                    for g, (c0, n) in enumerate(GROUPS):
                        cs = slice(c0, c0 + n)
                        W("grams", 3 * d + g + 1, r)
                        G1, G2, G3 = bank(4, n, P), bank(5, n, P), bank(6, n, L)
                        link(V.tensor_tensor(bdNT[:, cs], bcast(G1[:, :, 0:L], 2, 2), bcast(C["bd"][:, 2 + mT], n, 1), ALU.mult))
                        link(V.tensor_tensor(TTc[:, cs], G1[:, :, 0:L], bcast(C["cm"][:, 2 * d], n, 1), ALU.mult))
                        link(V.tensor_tensor(TTc[:, cs], TTc[:, cs], bcast(C["ci"][:, :], n, 1), ALU.add))
                        link(V.tensor_tensor(RbT[:, cs], G1[:, :, L:P], bcast(C["cm"][:, mI], n, 1), ALU.mult))
                        link(V.tensor_tensor(bdAk[:, cs], bcast(G2[:, :, 0:L], 2, 2), bcast(C["bd"][:, mT], n, 1), ALU.mult))
                        link(V.tensor_tensor(RkT[:, cs], G2[:, :, L:P], bcast(C["cm"][:, mI], n, 1), ALU.mult))
                        did(V.tensor_tensor(cN[:, cs], G3, bcast(C["cm"][:, 2 - 2 * d], n, 1), ALU.mult), "grams_taken")
                    for i in range(LEVELS):
                        for g, (c0, n) in enumerate(GROUPS):
                            W("squared", 15 * d + 3 * i + g + 1, r)
                            did(V.tensor_tensor(bdN[:, c0:c0 + n], bcast(sq_view(g, n), 2, 2), bcast(blk, n, 1), ALU.mult), "bdn_ready")
                        for g, (c0, n) in enumerate(GROUPS):
                            W("tt_sums", 15 * d + 3 * i + g + 1, r)
                            did(V.tensor_tensor(TTc[:, c0:c0 + n], TTc[:, c0:c0 + n], tt_view(g, n), ALU.add), "tt_ready")
                    for g, (c0, n) in enumerate(GROUPS):
                        did(V.tensor_tensor(bdTT[:, c0:c0 + n], bcast(TTc[:, c0:c0 + n], 2, 2), bcast(blk, n, 1), ALU.mult), "bdtt_ready")
                    dve.wait_ge(signal(f"s0_in{d}").sem, r * 16 + 16)
                    did(V.tensor_tensor(bdSA[:, :, :], bcast(s0[:, d, :], 2, 1), blk, ALU.mult), "s0_spread")
                    raised("s0_free")
                    W("s0_turned", d + 1, r)
                    link(V.tensor_copy(bdS[:, 0].rearrange("p g l -> p (g l)"), ps[:, 4, 0:P]))
                    did(V.tensor_tensor(Sc[:, 0, :], bdS[:, 0, 0, :], bdS[:, 0, 1, :], ALU.add), "s0_ready")
                    for j, (c, first, lastc) in enumerate(steps_of(d)):
                        k = 10 * d + j + 1
                        q = (j + 1) % 2
                        W("sa_sums", k, r)
                        if j:
                            W("y_sums", k - 1, r)
                        did(V.tensor_copy(cSA[:, :], ps[:, 5, 0:L]), "sa_ready")
                        did(V.tensor_tensor(bdSA[:, :, :], bcast(ps[:, 5, 0:L], 2, 1), blk, ALU.mult), "sa_ready")
                        W("state_sums", k, r)
                        link(V.tensor_scalar(Sc[:, q, :], ps[:, 5, P:P + L], etot[:, c:c + 1], None, ALU.mult))
                        did(V.scalar_tensor_tensor(out=bdS[:, q], in0=bcast(ps[:, 5, P:P + L], 2, 1), scalar=etot[:, c:c + 1],
                                                   in1=blk, op0=ALU.mult, op1=ALU.mult), "state_ready")
                    W("y_sums", 10 * d + 10, r)
                    if d == 0:
                        link(V.tensor_copy(ysum[:, 0:NS], ps[:, 6, :]))
                        did(V.tensor_copy(ysum[:, NS:T], ps[:, 7, 0:NP]), "y_taken")
                    else:
                        link(V.tensor_tensor(ysum[:, 0:NS], ysum[:, 0:NS], ps[:, 6, :], ALU.add))
                        did(V.tensor_tensor(ysum[:, NS:T], ysum[:, NS:T], ps[:, 7, 0:NP], ALU.add), "y_taken")
                    W("final_turned", d + 1, r)
                    link(V.tensor_copy(bdSA[:, :, :].rearrange("p g l -> p (g l)"), ps[:, 4, 0:P]))
                    raised("final_taken")
                    W("final_free", d + 1, r)
                    did(V.tensor_tensor(sout[:, d, :], bdSA[:, 0, :], bdSA[:, 1, :], ALU.add), "final_ready")
                link(V.tensor_tensor(t1[:, :], kds[:, :], rT, ALU.mult))
                did(V.tensor_scalar(t1[:, :], t1[:, :], pp[:, 8:9], None, ALU.mult), "bonus_products")
                W("mean_sums", 1, r)
                did(V.tensor_tensor(as_halves(t3[:, :]), half_view(ps, 4), as_halves(vT), ALU.mult), "bonus_ready")
                did(V.scalar_tensor_tensor(out=as_halves(t4[:, :]), in0=half_view(ps, 6), scalar=-1.0 / L,
                                           in1=as_halves(ysum[:, :]), op0=ALU.mult, op1=ALU.add), "y_squares_in")
                W("ln_root", 1, r)
                link(V.reciprocal(t5[:, :], t5[:, :]))
                link(V.tensor_tensor(t4[:, :], t4[:, :], t5[:, :], ALU.mult))
                link(V.tensor_scalar(t4[:, :], t4[:, :], pp[:, 13:14], pp[:, 14:15], ALU.mult, ALU.add))
                link(V.tensor_tensor(t4[:, :], t4[:, :], t3[:, :], ALU.add))
                W("gate_sums", 1, r)
                W("final_free", 3, r)
                did(V.tensor_tensor(as_halves(outr[:, :]), as_halves(t4[:, :]),
                                    half_view(ps, 4), ALU.mult), "round_done")
            S["dve_cnt"] = dict(cnt)
        S["sig"] = sig


HLEV = (1, 2, 4, 8, 16, 32, 64)
HKINDS = 5


def stage_hgrn(nc, I, O, S, per):
    with ExitStack() as ctx:
        sb = lambda name, shape, dt=F32: ctx.enter_context(nc.sbuf_tensor(name, shape, dt))
        C = S["consts"]
        sig = {}

        def signal(name):
            if name not in sig:
                sig[name] = Signal(ctx, nc, "hg_" + name, per.get("hg_" + name, 0))
            return sig[name]
        w = sb("whg", [P, HKINDS, KT, P])
        halfraw = sb("halfraw", [P, 3, T])
        th = sb("hth", [P, 4, T])
        vT, gh = halfraw[:, 1, :], halfraw[:, 2, :]
        q, sgate = sb("hq", [P, T]), sb("sgate", [P, T])
        key = [sb(f"key{d}", [P, T]) for d in range(2)]
        incl = [sb(f"incl{d}", [P, T]) for d in range(2)]
        excl = [sb(f"excl{d}", [P, T]) for d in range(2)]
        qs = [sb(f"qs{d}", [P, T]) for d in range(2)]
        ks = [sb(f"ks{d}", [P, T]) for d in range(2)]
        att = sb("att", [P, TT, P])
        kn = [sb(f"kn{d}", [P, TT, P]) for d in range(2)]
        vn = sb("vn", [P, TT, P])
        st = [sb(f"hst{d}", [P, TT - 1, P]) for d in range(2)]
        fin = sb("hfin", [P, 2, P])
        o1, rt, outh, osq = sb("o1", [P, T]), sb("hrt", [P, T]), sb("outh", [P, T]), sb("osq", [P, T])
        lbp = sb("lbp", [P, 3, 16])
        hm = sb("hmask", [P, 15, P])
        ps = ctx.enter_context(nc.psum_tensor("psH", [P, 8, 512], F32))
        s_m = ctx.enter_context(nc.semaphore("hg_mask_steps"))
        block = ctx.enter_context(nc.Block())
        wide = lambda b: ps[:, b:b + 2, :].rearrange("p a n -> p (a n)")[:, 0:T]

        def tok(ps_b, c):
            return ps[:, ps_b + c // 4, (c % 4) * P:(c % 4 + 1) * P]

        def seg(ap, m, half):
            return ap.rearrange("p (j a r) -> p j a r", a=2, r=m)[:, :, half, :]

        @block.sync
        def _(sp):
            win = I["w_in"][0].rearrange("(k p) n -> p k n", p=P)
            sp.sem_inc(signal("fin_free").sem, 1)
            with sp.Fori(0, HG_HEADS) as r:
                sp.wait_ge(signal("w_free").sem, r + 1)
                for i in range(HKINDS):
                    sp.dma_start(w[:, i, :, :], win[:, :, bass.ds(HG0 + i * HG_DIM + r * P, P)]).then_inc(signal("w_in").sem, 16)
                sp.wait_ge(signal("s0_free").sem, r + 1)
                for d, c in ((0, 0), (1, TT - 2)):
                    sp.dma_start(st[d][:, c, :], I["state_hgrn"][0, 0, d].rearrange("h k v -> (h k) v")[bass.ds(r * P, P), :])\
                        .then_inc(signal("s0_in").sem, 16)
                sp.wait_ge(signal("fin_ready").sem, r * 2 + 2)
                for d in range(2):
                    sp.dma_start(O["new_state_hgrn"][0, 0, d].rearrange("h k v -> (h k) v")[bass.ds(r * P, P), :], fin[:, d, :])\
                        .then_inc(signal("out").sem, 16)
                sp.wait_ge(signal("round_done").sem, r + 1)
                sp.dma_start(S["outh"][bass.ds(r, 1)].rearrange("o p n -> (o p) n"), outh[:, :]).then_inc(signal("out").sem, 16)
                sp.wait_ge(signal("out").sem, r * 48 + 48)
                sp.sem_inc(signal("fin_free").sem, 1)

        @block.gpsimd
        def _(pool):
            n = [0]

            def link(ins):
                n[0] += 1
                ins.then_inc(s_m, 1)
                pool.wait_ge(s_m, n[0])
            link(nc.gpsimd.memset(hm[:, :, :], 0.0))
            link(nc.gpsimd.tensor_copy(hm[:, 0, :], C["ident"][:, :]))
            for l, m in enumerate(HLEV):
                nj = P // (2 * m)
                for d in range(2):
                    v = seg(hm[:, 1 + 7 * d + l, :], m, 1 - d)
                    link(nc.gpsimd.memset(v, 1.0))
                    link(nc.gpsimd.affine_select(out=v, in_=v, compare_op=ALU.is_ge, fill=0.0, base=-m * d,
                                                 pattern=[[-2 * m, nj], [0, m]], channel_multiplier=1))
                    link(nc.gpsimd.affine_select(out=v, in_=v, compare_op=ALU.is_ge, fill=0.0, base=m - 1 + m * d,
                                                 pattern=[[2 * m, nj], [0, m]], channel_multiplier=-1))
            assert n[0] == 44

        @block.tensor
        def _(pe):
            W = lambda name, n, r: pe.wait_ge(signal(name).sem, signal(name).at(n, r))
            cnt = {}

            def inc(mm, name):
                mm.then_inc(signal(name).sem, 1)
                cnt[name] = cnt.get(name, 0) + 1
            pe.sem_inc(signal("w_free").sem, 1)
            ident = C["ident"][:, :]
            with pe.Fori(0, HG_HEADS) as r:
                cnt.clear()
                pe.wait_ge(signal("w_in").sem, r * 80 + 80)
                for i in range(HKINDS):
                    if i >= 2:
                        W("raw_taken", i - 1, r)
                    for h in range(2):
                        for k in range(KT):
                            mm = nc.tensor.matmul(ps[:, 2 * (i % 2) + h, 0:HALF], w[:, i, k, :],
                                                  S["hT"][:, k, h * HALF:(h + 1) * HALF], start=(k == 0), stop=(k == KT - 1))
                    inc(mm, "projected")
                pe.wait_ge(signal("projected").sem, signal("projected").at(HKINDS, r))
                pe.sem_inc(signal("w_free").sem, 1)
                cnt["w_free"] = 1
                W("raw_taken", 4, r)
                for c in range(TT):
                    mm = nc.tensor.transpose(tok(4, c), halfraw[:, 1, c * P:(c + 1) * P], ident)
                inc(mm, "v_turned")
                W("diag_ready", 1, r)
                for c in range(TT):
                    mm = nc.tensor.matmul(tok(6, c), qs[1][:, c * P:(c + 1) * P], q[:, c * P:(c + 1) * P], start=True, stop=True)
                inc(mm, "grams")
                W("vn_ready", 1, r)
                n = 1
                for l in range(len(HLEV)):
                    for d in range(2):
                        W("scaled", n, r)
                        if n > 1:
                            W("att_taken", n - 1, r)
                        for c in range(TT):
                            mm = nc.tensor.matmul(tok(4 + 2 * (n % 2 == 0), c), ks[d][:, c * P:(c + 1) * P],
                                                  qs[d][:, c * P:(c + 1) * P], start=True, stop=True)
                        inc(mm, "grams")
                        n += 1
                for d in range(2):
                    W("state_factors", d + 1, r)
                    if d == 0:
                        W("att_taken", 15, r)
                    for c in range(TT):
                        mm = nc.tensor.transpose(tok(4 + 2 * d, c), ks[d][:, c * P:(c + 1) * P], ident)
                    inc(mm, "k_turned")
                for d in range(2):
                    W("kn_ready", d + 1, r)
                    for c in range(TT):
                        mm = nc.tensor.matmul(tok(4 + 2 * d, c), kn[d][:, c, :], vn[:, c, :], start=True, stop=True)
                    inc(mm, "kv_sums")
                W("states_ready", 1, r)
                for c in range(TT):
                    mm = nc.tensor.matmul(tok(0, c), vn[:, c, :], att[:, c, :], start=True, stop=(c == TT - 1))
                    if c < TT - 1:
                        for d in range(2):
                            mm = nc.tensor.matmul(tok(0, c), st[d][:, c, :], qs[d][:, c * P:(c + 1) * P], start=False, stop=(d == 1))
                inc(mm, "o_sums")
                W("o_squares", 1, r)
                for h in range(2):
                    mm = nc.tensor.matmul(ps[:, 2 + h, 0:HALF], C["ones"][:, :], osq[:, h * HALF:(h + 1) * HALF], start=True, stop=True)
                inc(mm, "norm_sums")
                W("round_done", 1, r)
            S["hpe_cnt"] = dict(cnt)

        @block.scalar
        def _(act):
            W = lambda name, n, r: act.wait_ge(signal(name).sem, signal(name).at(n, r))
            cnt = {}
            A = nc.scalar.activation

            def inc(ins, name):
                ins.then_inc(signal(name).sem, 1)
                cnt[name] = cnt.get(name, 0) + 1
            act.wait_ge(signal("lb_diff").sem, 1)
            A(lbp[:, 0, :], lbp[:, 0, :], ACT.Tanh, scale=0.5).then_inc(signal("lb_tanh").sem, 1)
            with act.Fori(0, HG_HEADS) as r:
                cnt.clear()
                for i in range(HKINDS):
                    W("projected", i + 1, r)
                    W("raw_free", 1, r)
                    src = half_view(ps, 2 * (i % 2))
                    raw = {0: (0, 0.5), 3: (1, 1.0), 4: (2, 0.5)}.get(i)
                    tan = {0: 0, 1: 1, 2: 2, 4: 3}.get(i)
                    if tan is not None:
                        t = A(as_halves(th[:, tan, :]), src, ACT.Tanh, scale=0.5)
                    if raw is not None:
                        t = A(as_halves(halfraw[:, raw[0], :]), src, ACT.Copy, scale=raw[1])
                    inc(t, "raw_taken")
                W("v_turned", 1, r)
                inc(A(vn[:, :, :].rearrange("p a b -> p (a b)"), wide(4), ACT.Copy), "vn_ready")
                for d in range(2):
                    W("k_turned", d + 1, r)
                    inc(A(kn[d][:, :, :].rearrange("p a b -> p (a b)"), wide(4 + 2 * d), ACT.Copy), "kn_ready")
                W("o_sums", 1, r)
                inc(A(osq[:, :], wide(0), ACT.Square), "o_squares")
                W("norm_sums", 1, r)
                inc(A(as_halves(rt[:, :]), half_view(ps, 2), ACT.Sqrt, scale=1.0 / P, bias=C["eps"][:, 0:1]), "norm_root")
            S["hact_cnt"] = dict(cnt)

        @block.vector
        def _(dve):
            W = lambda name, n, r: dve.wait_ge(signal(name).sem, signal(name).at(n, r))
            V = nc.vector
            cnt = {}
            dve.sem_inc(signal("raw_free").sem, 1)
            dve.sem_inc(signal("s0_free").sem, 1)
            n0 = [0]

            def once(ins):
                n0[0] += 1
                ins.then_inc(signal("setup_line").sem, 1)
                dve.wait_ge(signal("setup_line").sem, n0[0])
            dve.wait_ge(s_m, 44)
            V.tensor_tensor(lbp[:, 0, :], S["ptab"][:, 2, LB0:LB0 + 16], S["ptab"][:, 2, LB1:LB1 + 16], ALU.subtract)\
                .then_inc(signal("lb_diff").sem, 1)
            dve.wait_ge(signal("lb_tanh").sem, 1)
            once(V.tensor_scalar(lbp[:, 1, :], lbp[:, 0, :], 0.25, 0.75, ALU.mult, ALU.add))
            once(V.tensor_scalar(lbp[:, 2, :], lbp[:, 0, :], -0.25, 0.25, ALU.mult, ALU.add))
            with dve.Fori(0, HG_HEADS) as r:
                cnt.clear()

                def did(ins, name):
                    cnt[name] = cnt.get(name, 0) + 1
                    ins.then_inc(signal(name).sem, 1)
                    dve.wait_ge(signal(name).sem, signal(name).at(cnt[name], r))
                link = lambda ins: did(ins, "vector_line")

                def raised(name):
                    dve.sem_inc(signal(name).sem, 1)
                    cnt[name] = cnt.get(name, 0) + 1
                W("raw_taken", HKINDS, r)
                link(V.scalar_tensor_tensor(out=q[:, :], in0=th[:, 0, :], scalar=1.0, in1=halfraw[:, 0, :], op0=ALU.add, op1=ALU.mult))
                link(V.scalar_tensor_tensor(out=sgate[:, :], in0=th[:, 3, :], scalar=1.0, in1=gh, op0=ALU.add, op1=ALU.mult))
                for d in range(2):
                    link(V.tensor_scalar(incl[d][:, :], th[:, 1 + d, :], lbp[:, 2, bass.ds(r + 8 * d, 1)], lbp[:, 1, bass.ds(r + 8 * d, 1)],
                                         ALU.mult, ALU.add))
                    link(V.tensor_scalar(key[d][:, :], incl[d][:, :], -1.0, 1.0, ALU.mult, ALU.add))
                    if d == 0:
                        link(V.memset(excl[d][:, :], 1.0))
                did(V.tensor_tensor(qs[1][:, :], key[0][:, :], key[1][:, :], ALU.add), "diag_ready")
                i32 = lambda ap: ap.bitcast(I32)

                def take(n, mask, b, beside):
                    W("grams", n, r)
                    beside().then_inc(signal("vector_line").sem, 1)
                    cnt["vector_line"] += 1
                    did(V.copy_predicated(att[:, :, :], i32(bcast(hm[:, mask, :], TT, 1)), wide(b).rearrange("p (c t) -> p c t", t=P)), "att_taken")
                    dve.wait_ge(signal("vector_line").sem, signal("vector_line").at(cnt["vector_line"], r))
                take(1, 0, 6, lambda: V.memset(excl[1][:, :], 1.0))
                for l, m in enumerate(HLEV):
                    for d in range(2):
                        n = 1 + 2 * l + d
                        qh, kh = 1 - d, d
                        link(V.tensor_tensor(seg(qs[d][:, :], m, qh), seg(q[:, :], m, qh), seg(incl[d][:, :], m, qh), ALU.mult))
                        if l == 0:
                            link(V.tensor_copy(seg(qs[d][:, :], m, kh), seg(q[:, :], m, kh)))
                            link(V.tensor_copy(ks[d][:, :], key[d][:, :]))
                        did(V.tensor_tensor(seg(ks[d][:, :], m, kh), seg(key[d][:, :], m, kh), seg(excl[d][:, :], m, kh), ALU.mult), "scaled")
                        end = m - 1 if d == 0 else 0
                        tq = seg(incl[d][:, :], m, kh)[:, :, end:end + 1]
                        tk = seg(incl[d][:, :], m, qh)[:, :, end:end + 1]
                        wide_t = lambda a: a.broadcast_to([P, T // (2 * m), m])
                        link(V.tensor_tensor(seg(excl[d][:, :], m, kh), seg(excl[d][:, :], m, kh), wide_t(tk), ALU.mult))
                        take(n + 1, 1 + 7 * d + l, 4 + 2 * (n % 2 == 0),
                             lambda: V.tensor_tensor(seg(incl[d][:, :], m, qh), seg(incl[d][:, :], m, qh), wide_t(tq), ALU.mult))
                for d in range(2):
                    link(V.tensor_tensor(qs[d][:, :], q[:, :], incl[d][:, :], ALU.mult))
                    did(V.tensor_tensor(ks[d][:, :], key[d][:, :], excl[d][:, :], ALU.mult), "state_factors")
                dve.wait_ge(signal("s0_in").sem, r * 32 + 32)
                W("fin_free", 1, r)
                for d in range(2):
                    W("kv_sums", d + 1, r)
                    did(V.tensor_copy(fin[:, d, :], tok(4 + 2 * d, TT - 1)), "fin_ready")
                    for j in range(TT - 2):
                        c, c2 = (j, j + 1) if d == 0 else (TT - 2 - j, TT - 3 - j)
                        e = c * P + (P - 1 if d == 0 else 0)
                        link(V.scalar_tensor_tensor(out=st[d][:, c2, :], in0=st[d][:, c, :], scalar=incl[d][:, e:e + 1],
                                                    in1=tok(4 + 2 * d, c), op0=ALU.mult, op1=ALU.add))
                raised("states_ready")
                W("norm_root", 1, r)
                raised("s0_free")
                raised("raw_free")
                link(V.reciprocal(rt[:, :], rt[:, :]))
                link(V.tensor_tensor(o1[:, :], wide(0), rt[:, :], ALU.mult))
                did(V.scalar_tensor_tensor(out=outh[:, :], in0=o1[:, :], scalar=S["ptab"][:, 2, bass.ds(r + HGN, 1)], in1=sgate[:, :],
                                           op0=ALU.mult, op1=ALU.mult), "round_done")
            S["hdve_cnt"] = dict(cnt)
        S["hsig"] = sig


def stage_merge(nc, I, S):
    with ExitStack() as ctx:
        sb = lambda name, shape, dt=F32: ctx.enter_context(nc.sbuf_tensor(name, shape, dt))
        sg = lambda name: ctx.enter_context(nc.semaphore("mg_" + name))
        SLOTS = 2
        w = [sb(f"wmg{s}", [P, 3 * KT, P]) for s in range(SLOTS)]
        br = sb("branches", [P, 2, PAIRS, T])
        th = [sb(f"gth{i}", [P, T]) for i in range(2)]
        m1, m2 = sb("m1", [P, T]), sb("m2", [P, T])
        ps = ctx.enter_context(nc.psum_tensor("psM", [P, 8, 512], F32))
        s_w = [sg(f"w_in{s}") for s in range(SLOTS)]
        s_wf = [sg(f"w_free{s}") for s in range(SLOTS)]
        s_br, s_gate, s_branch, s_th, s_m, s_mix = map(sg, ("branches_in", "gates", "branch_sums", "tanhs", "products", "merged"))
        block = ctx.enter_context(nc.Block())

        @block.sync
        def _(sp):
            for i, name in enumerate(("outr", "outh")):
                sp.dma_start(br[:, i], S[name].rearrange("n p t -> p n t")).then_inc(s_br, 16)
            win = I["w_in"][0].rearrange("(k p) n -> p k n", p=P)
            with sp.Fori(0, KT // SLOTS) as r:
                for s in range(SLOTS):
                    sp.wait_ge(s_wf[s], r + 1)
                    for g in range(2):
                        sp.dma_start(w[s][:, g * KT:(g + 1) * KT, :], win[:, :, bass.ds((r * SLOTS + s) * P + (GATE0 + g * D), P)])\
                            .then_inc(s_w[s], 16)
                    for g, name in enumerate(("w_br_rwkv", "w_br_hgrn")):
                        src = I[name][0].rearrange("(k p) n -> p k n", p=P)
                        sp.dma_start(w[s][:, 2 * KT + 8 * g:2 * KT + 8 * g + 8, :], src[:, :, bass.ds((r * SLOTS + s) * P, P)])\
                            .then_inc(s_w[s], 16)

        @block.tensor
        def _(pe):
            for s in range(SLOTS):
                pe.sem_inc(s_wf[s], 1)
            pe.wait_ge(s_br, 32)
            with pe.Fori(0, KT // SLOTS) as r:
                for s in range(SLOTS):
                    pe.wait_ge(s_w[s], r * 64 + 64)
                    for g in range(2):
                        pe.wait_ge(s_th, r * 4 + (2 * s + g + 1))
                        for h in range(2):
                            for k in range(KT):
                                mm = nc.tensor.matmul(ps[:, 2 * g + h, 0:HALF], w[s][:, g * KT + k, :],
                                                      S["hT"][:, k, h * HALF:(h + 1) * HALF], start=(k == 0), stop=(k == KT - 1))
                        mm.then_inc(s_gate, 1)
                    for g in range(2):
                        pe.wait_ge(s_m, r * 4 + (2 * s + g + 1))
                        for h in range(2):
                            for k in range(PAIRS):
                                mm = nc.tensor.matmul(ps[:, 4 + 2 * g + h, 0:HALF], w[s][:, 2 * KT + 8 * g + k, :],
                                                      br[:, g, k, h * HALF:(h + 1) * HALF], start=(k == 0), stop=(k == PAIRS - 1))
                        mm.then_inc(s_branch, 1)
                    pe.wait_ge(s_branch, r * 4 + (2 * s + 2))
                    pe.sem_inc(s_wf[s], 1)

        @block.scalar
        def _(act):
            act.sem_inc(s_th, 2)
            with act.Fori(0, KT // SLOTS) as r:
                for s in range(SLOTS):
                    for g in range(2):
                        act.wait_ge(s_gate, r * 4 + (2 * s + g + 1))
                        act.wait_ge(s_m, r * 4 + (2 * s + g + 1))
                        nc.scalar.activation(as_halves(th[g][:, :]), half_view(ps, 2 * g), ACT.Tanh, scale=0.5).then_inc(s_th, 1)

        @block.vector
        def _(dve):
            dve.sem_inc(s_m, 2)
            with dve.Fori(0, KT // SLOTS) as r:
                for s in range(SLOTS):
                    for g, m in enumerate((m1, m2)):
                        dve.wait_ge(s_branch, r * 4 + (2 * s + g + 1))
                        dve.wait_ge(s_th, r * 4 + (2 * s + g + 3))
                        nc.vector.scalar_tensor_tensor(out=as_halves(m[:, :]), in0=as_halves(th[g][:, :]), scalar=1.0,
                                                       in1=half_view(ps, 4 + 2 * g), op0=ALU.add, op1=ALU.mult).then_inc(s_m, 1)
                    dve.wait_ge(s_m, r * 4 + (2 * s + 4))
                    nc.vector.tensor_tensor(S["mergedT"][:, bass.ds(r * SLOTS + s, 1), :].rearrange("p o n -> p (o n)"), m1[:, :], m2[:, :], ALU.add)\
                        .then_inc(s_mix, 1)
                    dve.wait_ge(s_mix, r * SLOTS + (s + 1))


def stage_out_norm(nc, I, S):
    with ExitStack() as ctx:
        sb = lambda name, shape, dt=F32: ctx.enter_context(nc.sbuf_tensor(name, shape, dt))
        sg = lambda name: ctx.enter_context(nc.semaphore("on_" + name))
        w = [sb(f"wout{s}", [P, KT, P]) for s in range(2)]
        xs = [sb(f"xs{s}", [P, T]) for s in range(2)]
        xq = [sb(f"xq{s}", [P, T]) for s in range(2)]
        gth = sb("gth", [P, KT, 2])
        rstd = sb("rstd2", [P, T])
        wr = sb("wr", [P, KT, NE])
        mx, sm, ex = sb("mx", [P, TT]), sb("sm", [P, TT]), sb("ex", [P, TT, NE])
        ps = ctx.enter_context(nc.psum_tensor("psO", [P, 8, 512], F32))
        s_w = [sg(f"w_in{s}") for s in range(2)]
        (s_x, s_r, s_xt, s_xc, s_o, s_x1, s_q, s_ss, s_root, s_v, s_h2, s_ht, s_hc, s_lg, s_lr, s_ex) = map(sg, (
            "x_in", "router_in", "x_turned", "x_copied", "out_sums", "x1_ready", "squares", "square_sums", "root",
            "vector_line", "h2_ready", "h2_turned", "h2_copied", "logits", "logits_ready", "exps"))
        block = ctx.enter_context(nc.Block())
        xrow, x1T, h2T, mT, h2row = S["rows"], S["x1T"], S["hT"], S["mergedT"], S["rows"]
        wide = lambda b: ps[:, b:b + 2, :].rearrange("p a n -> p (a n)")[:, 0:T]

        def tok(b, t):
            return ps[:, b + t // 4, (t % 4) * P:(t % 4 + 1) * P]

        @block.sync
        def _(sp):
            for t in range(TT):
                src = I["x_sample"][0, t * P:(t + 1) * P, :] if t < TT - 1 else I["x_prompt"][0]
                sp.dma_start(xrow[:, t, :], src).then_inc(s_x, 16)
            sp.dma_start(wr[:, :, :], I["moe_router"][0].rearrange("(k p) e -> p k e", p=P)).then_inc(s_r, 16)
            wo = I["w_out"][0].rearrange("(k p) n -> p k n", p=P)
            for j in range(KT):
                if j >= 2:
                    sp.wait_ge(s_o, j - 1)
                sp.dma_start(w[j % 2][:, :, :], wo[:, :, j * P:(j + 1) * P]).then_inc(s_w[j % 2], 16)

        @block.tensor
        def _(pe):
            ident = S["consts"]["ident"][:, :]
            pe.wait_ge(s_x, 16 * TT)
            for j in range(KT):
                if j:
                    pe.wait_ge(s_xc, j)
                for t in range(TT):
                    mm = nc.tensor.transpose(tok(4, t), xrow[:, t, j * P:(j + 1) * P], ident)
                mm.then_inc(s_xt, 1)
                pe.wait_ge(s_w[j % 2], 16 * (j // 2 + 1))
                if j >= 2:
                    pe.wait_ge(s_x1, 3 * (j - 1))
                for h in range(2):
                    for k in range(KT):
                        mm = nc.tensor.matmul(ps[:, 2 * (j % 2) + h, 0:HALF], w[j % 2][:, k, :], mT[:, k, h * HALF:(h + 1) * HALF],
                                              start=(k == 0), stop=(k == KT - 1))
                mm.then_inc(s_o, 1)
                if j >= 1:
                    pe.wait_ge(s_q, j)
                    for h in range(2):
                        mm = nc.tensor.matmul(ps[:, 6 + h, 0:HALF], S["consts"]["ones"][:, :], xq[(j - 1) % 2][:, h * HALF:(h + 1) * HALF],
                                              start=(j == 1), stop=False)
                    mm.then_inc(s_ss, 1)
            pe.wait_ge(s_q, KT)
            for h in range(2):
                mm = nc.tensor.matmul(ps[:, 6 + h, 0:HALF], S["consts"]["ones"][:, :], xq[(KT - 1) % 2][:, h * HALF:(h + 1) * HALF],
                                      start=False, stop=True)
            mm.then_inc(s_ss, 1)
            for j in range(KT):
                b = 2 * (j % 2)
                pe.wait_ge(s_h2, 2 * (j + 1))
                if j >= 2:
                    pe.wait_ge(s_hc, j - 1)
                for t in range(TT):
                    mm = nc.tensor.transpose(tok(b, t), h2T[:, j, t * P:(t + 1) * P], ident)
                mm.then_inc(s_ht, 1)
            pe.wait_ge(s_r, 16)
            for t in range(TT):
                for k in range(KT):
                    mm = nc.tensor.matmul(ps[:, 4, t * NE:(t + 1) * NE], h2T[:, k, t * P:(t + 1) * P], wr[:, k, :],
                                          start=(k == 0), stop=(k == KT - 1))
            mm.then_inc(s_lg, 1)

        @block.scalar
        def _(act):
            A = nc.scalar.activation
            for j in range(KT):
                act.wait_ge(s_xt, j + 1)
                if j >= 2:
                    act.wait_ge(s_x1, 3 * (j - 1))
                A(xs[j % 2][:, :], wide(4), ACT.Copy).then_inc(s_xc, 1)
                if j >= 1:
                    act.wait_ge(s_x1, 3 * j)
                    if j >= 3:
                        act.wait_ge(s_ss, j - 2)
                    A(xq[(j - 1) % 2][:, :], x1T[:, j - 1, :], ACT.Square).then_inc(s_q, 1)
            act.wait_ge(s_x1, 3 * KT)
            act.wait_ge(s_ss, KT - 2)
            A(xq[(KT - 1) % 2][:, :], x1T[:, KT - 1, :], ACT.Square).then_inc(s_q, 1)
            act.wait_ge(s_ss, KT)
            A(as_halves(rstd[:, :]), half_view(ps, 6), ACT.Sqrt, scale=1.0 / D, bias=S["consts"]["eps"][:, 0:1]).then_inc(s_root, 1)
            for j in range(KT):
                act.wait_ge(s_ht, j + 1)
                A(h2row[:, :, j * P:(j + 1) * P], wide(2 * (j % 2)).rearrange("p (t c) -> p t c", c=P), ACT.Copy).then_inc(s_hc, 1)
            act.wait_ge(s_lr, 1)
            A(ex[:, :, :], ex[:, :, :], ACT.Exp).then_inc(s_ex, 1)

        @block.vector
        def _(dve):
            V = nc.vector
            steps = [0]

            def link(ins):
                steps[0] += 1
                ins.then_inc(s_v, 1)
                dve.wait_ge(s_v, steps[0])
            modT, A2 = S["modT"], S["A2"]
            link(V.tensor_scalar(gth[:, :, :], modT[:, 2 * KT:3 * KT, :], 0.5, None, ALU.mult))
            for j in range(KT):
                dve.wait_ge(s_o, j + 1)
                dve.wait_ge(s_xc, j + 1)
                for s, cut in ((0, slice(0, HALF)), (0, slice(HALF, NS)), (1, slice(NS, T))):
                    b, o = 2 * (j % 2) + cut.start // HALF, cut.start % HALF
                    V.scalar_tensor_tensor(out=x1T[:, j, cut], in0=ps[:, b, o:o + cut.stop - cut.start], scalar=gth[:, j, s:s + 1],
                                           in1=xs[j % 2][:, cut], op0=ALU.mult, op1=ALU.add).then_inc(s_x1, 1)
            dve.wait_ge(s_x1, 3 * KT)
            dve.wait_ge(s_root, 1)
            link(V.reciprocal(rstd[:, :], rstd[:, :]))
            for j in range(KT):
                link(V.tensor_tensor(h2T[:, j, :], x1T[:, j, :], rstd[:, :], ALU.mult))
                for s, cut in enumerate((slice(0, NS), slice(NS, T))):
                    V.tensor_scalar(h2T[:, j, cut], h2T[:, j, cut], A2[:, j, s:s + 1], modT[:, 3 * KT + j, s:s + 1],
                                    ALU.mult, ALU.add).then_inc(s_h2, 1)
            dve.wait_ge(s_h2, 2 * KT)
            dve.wait_ge(s_lg, 1)
            aff = S["aff"]
            lg = ps[:, 4, 0:TT * NE].rearrange("p (t e) -> p t e", e=NE)
            link(V.tensor_reduce(mx[:, :], lg, AX_X, ALU.max))
            V.tensor_tensor(ex[:, :, :], lg, bcast(mx[:, :], NE, 2), ALU.subtract).then_inc(s_lr, 1)
            dve.wait_ge(s_lr, 1)
            dve.wait_ge(s_ex, 1)
            link(V.tensor_reduce(sm[:, :], ex[:, :, :], AX_X, ALU.add))
            link(V.reciprocal(sm[:, :], sm[:, :]))
            link(V.tensor_tensor(aff[:, :, :], ex[:, :, :], bcast(sm[:, :], NE, 2), ALU.mult))


def stage_choose(nc, S):
    with ExitStack() as ctx:
        sb = lambda name, shape, dt=F32: ctx.enter_context(nc.sbuf_tensor(name, shape, dt))
        sg = lambda name: ctx.enter_context(nc.semaphore("ch_" + name))
        left, m8 = sb("left", [NE, T]), sb("m8", [NE, 8])
        one, cum = sb("onerow", [NE, T]), sb("cum", [NE, T])
        ps = ctx.enter_context(nc.psum_tensor("psC", [P, 8, 512], F32))
        s_t, s_v, s_s, s_b = map(sg, ("turned", "vector_line", "slots_ready", "slots_turned"))
        block = ctx.enter_context(nc.Block())
        ident = S["consts"]["ident"]

        @block.tensor
        def _(pe):
            for t in range(TT):
                mm = nc.tensor.transpose(ps[0:NE, t // 4, (t % 4) * P:(t % 4 + 1) * P], S["aff"][:, t, :], ident[:, :])
            mm.then_inc(s_t, 1)
            pe.wait_ge(s_s, 1)
            for t in range(TT):
                mm = nc.tensor.transpose(ps[:, 2, t * NE:(t + 1) * NE], cum[:, t * P:(t + 1) * P], ident[0:NE, 0:NE])
            mm.then_inc(s_b, 1)

        @block.vector
        def _(dve):
            V = nc.vector
            steps = [0]

            def link(ins):
                steps[0] += 1
                ins.then_inc(s_v, 1)
                dve.wait_ge(s_v, steps[0])
            dve.wait_ge(s_t, 1)
            link(V.tensor_copy(left[:, :], ps[0:NE, 0:2, :].rearrange("p a n -> p (a n)")[:, 0:T]))
            for cut, cap in ((slice(0, NS), CAP_S), (slice(NS, T), CAP_P)):
                for _i in range(cap // 8):
                    link(V.max(m8[:, :], left[:, cut]))
                    link(V.match_replace(left[:, cut], m8[:, :], left[:, cut], -1.0))
            link(V.tensor_scalar(left[:, :], left[:, :], 0.0, None, ALU.is_lt))
            link(V.memset(one[:, :], 1.0))
            for cut in (slice(0, NS), slice(NS, T)):
                link(V.tensor_tensor_scan(cum[:, cut], one[:, cut], left[:, cut], 0.0, ALU.mult, ALU.add))
            V.tensor_tensor(cum[:, :], cum[:, :], left[:, :], ALU.mult).then_inc(s_s, 1)
            dve.wait_ge(s_b, 1)
            link(V.tensor_copy(S["slot"][:, :, :].rearrange("p t e -> p (t e)"), ps[:, 2, 0:TT * NE]))


def stage_experts(nc, I, S):
    with ExitStack() as ctx:
        sb = lambda name, shape, dt=F32: ctx.enter_context(nc.sbuf_tensor(name, shape, dt))
        sg = lambda name: ctx.enter_context(nc.semaphore("ex_" + name))
        RING, Q = 8, 4
        M = CAP_S + CAP_P
        FT = FF // P
        KC = 2
        ROUNDS = NE // Q
        gu = lambda e: [("gu", e, k, g) for k in range(KT // KC) for g in range(2)]
        dn = lambda e: [("dn", e, m, 0) for m in range(FT)]
        order = gu(0) + gu(1) + dn(0) + gu(2) + dn(1) + gu(3) + dn(2) + dn(3)
        USES = len(order) // RING
        assert USES * RING == len(order)
        place = {c: n for n, c in enumerate(order)}
        spare = [S[n][:, :, :].rearrange("p k t -> p (k t)")[:, i * 2048:(i + 1) * 2048] for n in ("hT", "mergedT") for i in range(5)]
        ring = spare[0:RING]
        ys, yp = spare[RING], spare[RING + 1][0:64, :]
        xg = sb("xg", [P, KT, Q, M])
        hidT = sb("hidT", [P, FT, M])
        hid = sb("hid", [M, FF])
        sel, selp = sb("sel", [P, 4, Q, CAP_S]), sb("selp", [P, Q, CAP_P])
        selw, selpw = sb("selw", [P, 4, 2, CAP_S]), sb("selpw", [P, 2, 32])
        selT, selpT = sb("selT", [P, NS]), sb("selpT", [64, NP])
        iota = sb("iota", [P, CAP_S])
        gth = sb("gth2", [P, KT, 2])
        ps = ctx.enter_context(nc.psum_tensor("psE", [P, 8, 512], F32))
        s_in = [sg(f"w_in{i}") for i in range(RING)]
        s_free = [sg(f"w_free{i}") for i in range(RING)]
        (s_io, s_sel, s_selw, s_selT, s_selc, s_gath, s_xg, s_gus, s_tanh, s_v, s_hid, s_ht, s_hidT, s_down, s_y, s_sc, s_add, s_z,
         s_gth) = map(sg, (
            "iota", "selected", "weighted_selected", "selection_turned", "selection_copied", "gathered", "xg_ready", "gate_up_sums",
            "gate_tanh", "silu", "hidden", "hidden_turned", "hidden_columns", "down_sums", "y_ready", "scattered", "added", "zeroed",
            "gate_factor"))
        block = ctx.enter_context(nc.Block())
        x1T, rows = S["x1T"], S["rows"]
        wide = lambda b: ps[:, b:b + 2, :].rearrange("p a n -> p (a n)")

        def rounds(eng, body):
            body(0, True, False)
            with eng.Fori(1, ROUNDS - 1) as r:
                body(r, False, False)
            body(ROUNDS - 1, False, True)

        @block.sync
        def _(sp):
            wg, wu, wd = (I[n][0].rearrange("e a b -> (e a) b") for n in ("moe_w_gate", "moe_w_up", "moe_w_down"))
            with sp.Fori(0, ROUNDS) as r:
                for n, (what, e, k, g) in enumerate(order):
                    slot, use = n % RING, n // RING
                    sp.wait_ge(s_free[slot], r * USES + (use + 1))
                    if what == "gu":
                        src = (wg, wu)[g][bass.ds(r * (Q * D) + (e * D + k * KC * P), KC * P), :].rearrange("(k p) f -> p k f", p=P)
                        dst = ring[slot].rearrange("p (k f) -> p k f", k=KC)
                    else:
                        src = wd[bass.ds(r * (Q * FF) + (e * FF + k * P), P), :]
                        dst = ring[slot]
                    sp.dma_start(dst, src).then_inc(s_in[slot], 16)

        @block.gpsimd
        def _(pool):
            nc.gpsimd.iota(iota[:, :], pattern=[[1, CAP_S]], base=1, channel_multiplier=0,
                           allow_small_or_imprecise_dtypes=True).then_inc(s_io, 1)
            nc.gpsimd.memset(selpw[:, :, :], 0.0).then_inc(s_z, 1)
            nc.gpsimd.memset(yp, 0.0).then_inc(s_z, 1)

        @block.tensor
        def _(pe):
            ident = S["consts"]["ident"][:, :]
            for i in range(RING):
                pe.sem_inc(s_free[i], 1)

            def arrived(r, c):
                n = place[c]
                pe.wait_ge(s_in[n % RING], r * (16 * USES) + 16 * (n // RING + 1))
                return ring[n % RING], s_free[n % RING]

            def gather(r):
                pe.wait_ge(s_sel, r + 1)
                for j in range(KT):
                    if j >= 2:
                        pe.wait_ge(s_xg, r * KT + (j - 1))
                    o = ps[:, 4 + j % 2, 0:Q * M].rearrange("p (e s) -> p e s", e=Q)
                    for t in range(4):
                        nc.tensor.matmul(o[:, :, 0:CAP_S], rows[:, t, j * P:(j + 1) * P], sel[:, t, :, :], start=(t == 0), stop=(t == 3))
                    nc.tensor.matmul(o[:, :, CAP_S:M], rows[:, 4, j * P:(j + 1) * P], selp[:, :, :], start=True, stop=True).then_inc(s_gath, 1)

            def gate_up(r, e):
                for what in gu(e):
                    _, _, k, g = what
                    w, free = arrived(r, what)
                    for kk in range(KC):
                        kt = k * KC + kk
                        for c in range(2):
                            mm = nc.tensor.matmul(ps[0:M, 2 * g + c, :], xg[:, kt, e, :], w[:, kk * FF + c * 512:kk * FF + (c + 1) * 512],
                                                  start=(kt == 0), stop=(kt == KT - 1))
                    if k == KT // KC - 1 and g == 1:
                        mm.then_inc(s_gus, 1)
                        pe.wait_ge(s_gus, r * Q + (e + 1))
                        pe.sem_inc(free, 1)
                    else:
                        mm.then_inc(free, 1)

            def turn(r, e):
                pe.wait_ge(s_hid, r * Q + (e + 1))
                for m in range(FT):
                    mm = nc.tensor.transpose(ps[:, m // 4, (m % 4) * M:(m % 4 + 1) * M], hid[:, m * P:(m + 1) * P], ident[0:M, 0:M])
                mm.then_inc(s_ht, 1)
                pe.wait_ge(s_hidT, r * Q + (e + 1))

            def down(r, e):
                for what in dn(e):
                    m = what[2]
                    w, free = arrived(r, what)
                    for c in range(4):
                        mm = nc.tensor.matmul(ps[0:M, 4 + c, :], hidT[:, m, :], w[:, c * 512:(c + 1) * 512], start=(m == 0), stop=(m == FT - 1))
                    if m == FT - 1:
                        mm.then_inc(s_down, 1)
                        pe.wait_ge(s_down, r * Q + (e + 1))
                        pe.sem_inc(free, 1)
                    else:
                        mm.then_inc(free, 1)

            def scatter(r, p):
                pe.wait_ge(s_selw, r * 2 + (p + 1))
                pe.wait_ge(s_y, r * (4 * Q) + 8 * (p + 1))
                for t in range(4):
                    mm = nc.tensor.transpose(ps[:, 6, t * P:(t + 1) * P], selw[:, t].rearrange("p e s -> p (e s)"), ident)
                mm = nc.tensor.transpose(ps[0:64, 7, 0:P], selpw[:, :, :].rearrange("p e s -> p (e s)"), ident)
                mm.then_inc(s_selT, 1)
                pe.wait_ge(s_selc, r * 4 + (2 * p + 2))
                for j in range(KT):
                    b = 4 + 2 * (j % 2)
                    if j >= 2:
                        pe.wait_ge(s_add, r * (4 * KT) + (2 * KT * p + 2 * (j - 1)))
                    nc.tensor.matmul(ps[:, b, :], ys[:, j * P:(j + 1) * P], selT[:, :], start=True, stop=True)
                    nc.tensor.matmul(ps[:, b + 1, 0:P], yp[:, j * P:(j + 1) * P], selpT[:, :], start=True, stop=True).then_inc(s_sc, 1)
                pe.wait_ge(s_add, r * (4 * KT) + 2 * KT * (p + 1))

            def body(r, first, last):
                gate_up(r, 0)
                if not first:
                    scatter(r - 1, 1)
                turn(r, 0)
                gate_up(r, 1)
                down(r, 0)
                turn(r, 1)
                gate_up(r, 2)
                pe.wait_ge(s_y, r * (4 * Q) + 4)
                down(r, 1)
                turn(r, 2)
                gate_up(r, 3)
                scatter(r, 0)
                down(r, 2)
                turn(r, 3)
                pe.wait_ge(s_y, r * (4 * Q) + 12)
                if not last:
                    gather(r + 1)
                    pe.wait_ge(s_xg, r * KT + 2 * KT)
                down(r, 3)
            gather(0)
            pe.wait_ge(s_xg, KT)
            rounds(pe, body)
            scatter(ROUNDS - 1, 1)

        @block.scalar
        def _(act):
            A = nc.scalar.activation

            def gathered(r):
                for j in range(KT):
                    act.wait_ge(s_gath, r * KT + (j + 1))
                    A(xg[:, j, :, :].rearrange("p e s -> p (e s)"), ps[:, 4 + j % 2, 0:Q * M], ACT.Copy).then_inc(s_xg, 1)

            def tanh(r, e):
                act.wait_ge(s_gus, r * Q + (e + 1))
                for c in range(2):
                    A(hid[:, c * 512:(c + 1) * 512], ps[0:M, c, :], ACT.Tanh, scale=0.5).then_inc(s_tanh, 1)

            def columns(r, e):
                act.wait_ge(s_ht, r * Q + (e + 1))
                for c in range(2):
                    t = A(hidT[:, 4 * c:4 * c + 4, :].rearrange("p m s -> p (m s)"), ps[:, c, 0:4 * M], ACT.Copy)
                t.then_inc(s_hidT, 1)

            def results(r, e):
                act.wait_ge(s_down, r * Q + (e + 1))
                for c in range(2, 4):
                    A(ys[64 * (e % 2):64 * (e % 2) + 64, c * 512:(c + 1) * 512], ps[0:64, 4 + c, :], ACT.Copy)
                    A(yp[32 * (e % 2):32 * (e % 2) + CAP_P, c * 512:(c + 1) * 512], ps[64:M, 4 + c, :], ACT.Copy).then_inc(s_y, 1)

            def selection(r, p):
                act.wait_ge(s_selT, r * 2 + (p + 1))
                A(selT[:, :], ps[:, 6, :], ACT.Copy).then_inc(s_selc, 1)
                A(selpT[:, :], ps[0:64, 7, 0:P], ACT.Copy).then_inc(s_selc, 1)

            def body(r, first, last):
                tanh(r, 0)
                if not first:
                    selection(r - 1, 1)
                columns(r, 0)
                tanh(r, 1)
                results(r, 0)
                columns(r, 1)
                tanh(r, 2)
                results(r, 1)
                columns(r, 2)
                tanh(r, 3)
                selection(r, 0)
                results(r, 2)
                columns(r, 3)
                if not last:
                    gathered(r + 1)
                results(r, 3)
            gathered(0)
            rounds(act, body)
            selection(ROUNDS - 1, 1)

        @block.vector
        def _(dve):
            V = nc.vector

            def choose(r):
                for e in range(Q):
                    for t in range(TT):
                        out, cap = (sel[:, t, e, :], CAP_S) if t < 4 else (selp[:, e, :], CAP_P)
                        last = V.tensor_scalar(out, iota[:, 0:cap], S["slot"][:, t, bass.ds(r * Q + e, 1)], None, ALU.is_equal)
                last.then_inc(s_sel, 1)

            def weigh(r, p):
                for e in range(2):
                    for t in range(TT):
                        out, cap = (selw[:, t, e, :], CAP_S) if t < 4 else (selpw[:, e, 0:CAP_P], CAP_P)
                        col = bass.ds(r * Q + (2 * p + e), 1)
                        last = V.tensor_scalar(out, iota[:, 0:cap], S["slot"][:, t, col], S["aff"][:, t, col], ALU.is_equal, ALU.mult)
                last.then_inc(s_selw, 1)

            def silu(r, e):
                for c in range(2):
                    cut = slice(c * 512, (c + 1) * 512)
                    dve.wait_ge(s_tanh, r * (2 * Q) + (2 * e + c + 1))
                    V.scalar_tensor_tensor(out=hid[:, cut], in0=hid[:, cut], scalar=1.0, in1=ps[0:M, c, :], op0=ALU.add, op1=ALU.mult)\
                        .then_inc(s_v, 1)
                for c in range(2):
                    cut = slice(c * 512, (c + 1) * 512)
                    dve.wait_ge(s_v, r * (2 * Q) + (2 * e + c + 1))
                    last = V.tensor_tensor(hid[:, cut], hid[:, cut], ps[0:M, 2 + c, :], ALU.mult)
                last.then_inc(s_hid, 1)

            def results(r, e):
                dve.wait_ge(s_down, r * Q + (e + 1))
                for c in range(2):
                    V.tensor_copy(ys[64 * (e % 2):64 * (e % 2) + 64, c * 512:(c + 1) * 512], ps[0:64, 4 + c, :])
                    V.tensor_copy(yp[32 * (e % 2):32 * (e % 2) + CAP_P, c * 512:(c + 1) * 512], ps[64:M, 4 + c, :]).then_inc(s_y, 1)

            def add(r, p):
                for j in range(KT):
                    b = 4 + 2 * (j % 2)
                    dve.wait_ge(s_sc, r * (2 * KT) + (p * KT + j + 1))
                    for s, (cut, bb) in enumerate(((slice(0, NS), b), (slice(NS, T), b + 1))):
                        V.scalar_tensor_tensor(out=x1T[:, j, cut], in0=ps[:, bb, 0:cut.stop - cut.start], scalar=gth[:, j, s:s + 1],
                                               in1=x1T[:, j, cut], op0=ALU.mult, op1=ALU.add).then_inc(s_add, 1)
                dve.wait_ge(s_add, r * (4 * KT) + 2 * KT * (p + 1))

            def body(r, first, last):
                silu(r, 0)
                if not first:
                    add(r - 1, 1)
                weigh(r, 0)
                silu(r, 1)
                results(r, 0)
                silu(r, 2)
                results(r, 1)
                silu(r, 3)
                add(r, 0)
                results(r, 2)
                weigh(r, 1)
                if not last:
                    choose(r + 1)
                results(r, 3)
            dve.wait_ge(s_io, 1)
            dve.wait_ge(s_z, 2)
            V.tensor_scalar(gth[:, :, :], S["modT"][:, 5 * KT:6 * KT, :], 0.5, None, ALU.mult).then_inc(s_gth, 1)
            dve.wait_ge(s_gth, 1)
            choose(0)
            rounds(dve, body)
            add(ROUNDS - 1, 1)


def stage_final(nc, I, O, S):
    with ExitStack() as ctx:
        sb = lambda name, shape, dt=F32: ctx.enter_context(nc.sbuf_tensor(name, shape, dt))
        sg = lambda name: ctx.enter_context(nc.semaphore("fi_" + name))
        g, junk = (S["mergedT"][:, :, :].rearrange("p k t -> p (k t)")[:, i * D:(i + 1) * D] for i in range(2))
        yv = S["hT"][:, :, :].rearrange("p k t -> p (k t)").rearrange("p (t n) -> p t n", n=D)
        ssq, rs = sb("ssqf", [P, TT]), sb("rsf", [P, TT])
        ps = ctx.enter_context(nc.psum_tensor("psF", [P, 8, 512], F32))
        s_g, s_t, s_c, s_ss, s_root, s_r, s_y, s_out = map(sg, ("g_in", "turned", "copied", "ssq", "root", "rstd", "y_ready", "y_out"))
        block = ctx.enter_context(nc.Block())
        rows = S["rows"]

        @block.sync
        def _(sp):
            sp.dma_start(g, I["final_norm_g"].partition_broadcast(P)).then_inc(s_g, 16)
            for t in range(TT):
                dst = O["y_sample"][0, t * P:(t + 1) * P, :] if t < TT - 1 else O["y_prompt"][0]
                sp.wait_ge(s_y, t + 1)
                sp.dma_start(dst, yv[:, t, :]).then_inc(s_out, 16)
            sp.wait_ge(s_out, 16 * TT)

        @block.tensor
        def _(pe):
            for i in range(4 * TT):
                t, q = divmod(i, 4)
                if i >= 8:
                    pe.wait_ge(s_c, i - 7)
                for n in range(4):
                    mm = nc.tensor.transpose(ps[:, i % 8, n * P:(n + 1) * P], S["x1T"][:, 4 * q + n, t * P:(t + 1) * P],
                                             S["consts"]["ident"][:, :])
                mm.then_inc(s_t, 1)

        @block.scalar
        def _(act):
            A = nc.scalar.activation
            for t in range(TT):
                act.wait_ge(s_c, 4 * t + 4)
                if t:
                    act.wait_ge(s_ss, t)
                A(junk, rows[:, t, :], ACT.Square, accum_out=ssq[:, t:t + 1]).then_inc(s_ss, 1)
            act.wait_ge(s_ss, TT)
            A(rs[:, :], ssq[:, :], ACT.Sqrt, scale=1.0 / D, bias=S["consts"]["eps"][:, 0:1]).then_inc(s_root, 1)

        @block.vector
        def _(dve):
            V = nc.vector
            for i in range(4 * TT):
                t, q = divmod(i, 4)
                dve.wait_ge(s_t, i + 1)
                V.tensor_copy(rows[:, t, q * 512:(q + 1) * 512], ps[:, i % 8, :]).then_inc(s_c, 1)
            dve.wait_ge(s_root, 1)
            dve.wait_ge(s_g, 16)
            V.reciprocal(rs[:, :], rs[:, :]).then_inc(s_r, 1)
            dve.wait_ge(s_r, 1)
            for t in range(TT):
                V.scalar_tensor_tensor(out=yv[:, t, :], in0=rows[:, t, :], scalar=rs[:, t:t + 1], in1=g,
                                       op0=ALU.mult, op1=ALU.mult).then_inc(s_y, 1)


def build_layer(nc, I, O, per=None):
    per = per or PER
    with ExitStack() as ctx:
        sb = lambda name, shape, dt=F32: ctx.enter_context(nc.sbuf_tensor(name, shape, dt))
        S = {"consts": {"ident": sb("ident", [P, P]), "bd": sb("bdmask", [P, 5, 2, L]), "cm": sb("cmask", [P, 4, L]),
                        "ci": sb("cident", [P, L]), "ns": sb("nstart", [P, T]), "ones": sb("ones", [P, P]), "eps": sb("epsv", [P, 2])},
             "ptab": sb("ptab", [P, 3, P]), "modT": sb("modT", [P, 96, 2]),
             "A1": sb("A1", [P, KT, 2]), "A2": sb("A2", [P, KT, 2]), "aff": sb("aff", [P, TT, NE]), "slot": sb("slot", [P, TT, NE]),
             "outr": nc.dram_tensor("outr_scratch", (PAIRS, P, T), F32, kind="Internal").ap(),
             "outh": nc.dram_tensor("outh_scratch", (HG_HEADS, P, T), F32, kind="Internal").ap()}
        with nc.sbuf_tensor("hT", [P, KT, T], F32) as hT:
            S["hT"] = hT
            stage_modulation(nc, I, S)
            stage_masks(nc, S)
            with nc.sbuf_tensor("lora", [P, 3, T], F32) as lora, nc.sbuf_tensor("lw", [P, 3, 2, P], F32) as lw:
                S["lora"], S["lw"] = lora, lw
                stage_lora(nc, I, S)
                with cleared_semaphores(nc):
                    stage_rwkv(nc, I, O, S, per)
            with cleared_semaphores(nc):
                stage_hgrn(nc, I, O, S, per)
            with nc.sbuf_tensor("mergedT", [P, KT, T], F32) as mergedT:
                S["mergedT"] = mergedT
                stage_merge(nc, I, S)
                with nc.sbuf_tensor("x1a", [P, KT, T], F32) as x1T, nc.sbuf_tensor("rows_a", [P, TT, D], F32) as rows:
                    S["x1T"], S["rows"] = x1T, rows
                    stage_out_norm(nc, I, S)
                    stage_choose(nc, S)
                    stage_experts(nc, I, S)
                    stage_final(nc, I, O, S)
        return S


PER = {'bd_factors': 6,
 'bdn_ready': 30,
 'bdnt_ready': 24,
 'bdtt_ready': 6,
 'bdv_ready': 3,
 'bonus_products': 1,
 'bonus_ready': 1,
 'bonus_sums': 1,
 'cn_ready': 48,
 'derived': 1,
 'exps': 8,
 'factors': 8,
 'final_free': 3,
 'final_ready': 2,
 'final_taken': 2,
 'final_turned': 2,
 'gate_sums': 1,
 'grams': 6,
 'grams_taken': 6,
 'hg_att_taken': 15,
 'hg_diag_ready': 1,
 'hg_fin_free': 1,
 'hg_fin_ready': 2,
 'hg_grams': 15,
 'hg_k_turned': 2,
 'hg_kn_ready': 2,
 'hg_kv_sums': 2,
 'hg_norm_root': 1,
 'hg_norm_sums': 1,
 'hg_o_squares': 1,
 'hg_o_sums': 1,
 'hg_projected': 5,
 'hg_raw_free': 1,
 'hg_raw_taken': 5,
 'hg_round_done': 1,
 'hg_s0_free': 1,
 'hg_scaled': 14,
 'hg_state_factors': 2,
 'hg_states_ready': 1,
 'hg_v_turned': 1,
 'hg_vector_line': 64,
 'hg_vn_ready': 1,
 'hg_w_free': 1,
 'kk_max': 1,
 'kk_raw': 1,
 'kk_ready': 1,
 'kk_root': 1,
 'kk_squares': 1,
 'kk_sums': 1,
 'ln_root': 1,
 'logs': 2,
 'lora_sums': 2,
 'lora_taken': 4,
 'lw_free': 1,
 'mean_sums': 1,
 'mixed': 3,
 'n_turned': 24,
 'nr_ready': 20,
 'projected': 3,
 'r_sums': 20,
 'raw_free': 1,
 'raw_ready': 3,
 'round_done': 1,
 'rows_taken': 12,
 'rows_turned': 12,
 's0_free': 2,
 's0_ready': 2,
 's0_spread': 2,
 's0_turned': 2,
 'sa_ready': 40,
 'sa_sums': 20,
 'squared': 30,
 'state_ready': 20,
 'state_sums': 20,
 'tt_ready': 30,
 'tt_sums': 30,
 'v_spread': 2,
 'v_turned': 3,
 'var_sums': 1,
 'vector_line': 106,
 'w_free': 1,
 'y_squares': 1,
 'y_squares_in': 1,
 'y_sums': 20,
 'y_taken': 2}


_INS = ["x_prompt", "x_sample", "c", "state_rwkv", "state_hgrn", "c_ctx", "norm1_g", "norm2_g", "final_norm_g",
        "ada_w", "ada_b", "w_in", "rw_mu", "rw_w0", "rw_w2", "rw_a0", "rw_a2", "rw_g2", "rw_k_k", "rw_k_a", "rw_r_k",
        "rw_ln_w", "rw_ln_b", "hg_lb", "hg_norm_g", "w_br_rwkv", "w_br_hgrn", "w_out", "moe_router",
        "moe_w_gate", "moe_w_up", "moe_w_down"]
_OUTS = [("y_prompt", (1, NP, D)), ("y_sample", (1, NS, D)), ("new_state_rwkv", (1, 1, 2, RW_HEADS, 64, 64)),
         ("new_state_hgrn", (1, 1, 2, HG_HEADS, P, P))]


def kernel(**inputs):
    import numpy as _np
    import concourse.bacc as _bacc
    from concourse.bass_utils import run_bass_kernel_spmd as _run

    nc = _bacc.Bacc("TRN2", target_bir_lowering=False, num_devices=1)
    arrays, I, O = {}, {}, {}
    for name in _INS:
        a = _np.ascontiguousarray(inputs[name])
        arrays[f"in_{name}"] = a
        I[name] = nc.dram_tensor(f"in_{name}", a.shape, F32, kind="ExternalInput").ap()
    for name, shape in _OUTS:
        O[name] = nc.dram_tensor(f"out_{name}", shape, F32, kind="ExternalOutput").ap()
    build_layer(nc, I, O)
    r = _run(nc, [arrays], core_ids=[0])
    return tuple(r.results[0][f"out_{name}"] for name, _ in _OUTS)
```

```python
from contextlib import ExitStack, contextmanager
import math

import concourse.bass as bass
from concourse import mybir

P = 128
D = 2048
KT = D // P
NS, NP = 512, 128
T = NS + NP
TT = T // P
GRID_W = 64
RW_HEADS, RW_DIM = 16, 1024
PAIRS = RW_HEADS // 2
L = 64
NCH = T // L
HG_HEADS = 8
RW_COLS = 3456
HG0 = RW_COLS
HG_DIM = 1024
GATE0 = RW_COLS + 5 * HG_DIM
NE, FF = 16, 1024
CAP_S, CAP_P = 2 * NS // NE, 2 * NP // NE
EPS = 1e-6
LN_EPS = 64e-5
DECAY_SCALE = math.exp(-0.5)

F32 = mybir.dt.float32
I32 = mybir.dt.int32
ALU = mybir.AluOpType
ACT = mybir.ActivationFunctionType
AX_X = mybir.AxisListType.X

ADA_B, C_S, C_P = 0, 96, 112
MU0, MU1, K_K, K_A, R_K, W0, A0, LN_W, LN_B, MUL0, MUL1 = 0, 24, 48, 56, 64, 72, 88, 104, 112, 120, 123
G1, G2, LB0, LB1, HGN = 0, 16, 32, 48, 64


@contextmanager
def cleared_semaphores(nc):
    before = nc.snapshot_sems()
    yield
    nc.clear_and_free_semaphores(nc.allocated_since(before))
    nc.all_engine_barrier()


class Signal:

    def __init__(self, ctx, nc, name, per=0):
        self.sem, self.name, self.per = nc.alloc_semaphore(name), name, per

    def at(self, n, rnd=None):
        assert n > 0, self.name
        return n if rnd is None else rnd * self.per + n


def bcast(ap, n, axis):
    v = ap.unsqueeze(axis)
    shape = list(v.shape)
    shape[axis] = n
    return v.broadcast_to(shape)


def stage_modulation(nc, I, S):
    with ExitStack() as ctx:
        sb = lambda name, shape, dt=F32: ctx.enter_context(nc.sbuf_tensor(name, shape, dt))
        sg = lambda name: ctx.enter_context(nc.semaphore(name))
        RING, CT = 3, 4
        NBLK = 6 * D // (CT * P)
        rows = sb("rows", [P, 3, P])
        xt = sb("xt", [P, TT, D])
        junk = sb("junk", [P, D])
        ssq = sb("ssq", [P, TT])
        std = sb("std", [P, TT])
        rstd = sb("rstd", [P, TT])
        th = sb("th", [P, 2 * KT])
        cond = sb("cond", [P, KT, 2])
        eps = sb("eps", [P, 1])
        ring = [sb(f"ada{i}", [P, KT, CT * P]) for i in range(RING)]
        modrow = [S["hT"][0:2, :, :].rearrange("p k t -> p (k t)"), junk[0:2, :]]
        ps = ctx.enter_context(nc.psum_tensor("psA", [P, 8, 512], F32))
        s_masks = sg("mask_steps")
        s_par, s_x, s_id, s_const = sg("params_in"), sg("x_in"), sg("ident_made"), sg("consts_made")
        s_ada = [sg(f"ada_in{i}") for i in range(RING)]
        s_adaf = [sg(f"ada_free{i}") for i in range(RING)]
        s_modc = [sg(f"mod_copied{i}") for i in range(RING)]
        s_ptr, s_ptab, s_th, s_cond = sg("param_rows_turned"), sg("param_tables"), sg("cond_tanh"), sg("cond_ready")
        s_mod, s_modT, s_ssq, s_std, s_xn = sg("mod_sums"), sg("mod_ready"), sg("ssq_ready"), sg("std_ready"), sg("x_normed")
        s_xT, s_h, s_hd, s_v = sg("x_turned"), sg("h_ready"), sg("h_bank_free"), sg("vector_line")
        block = ctx.enter_context(nc.Block())
        mod = ps[:, 3, 0:192].rearrange("p (n s) -> p n s", s=2)

        @block.sync
        def _(sp):
            def rowv(name, r):
                a = I[name]
                if name == "rw_r_k":
                    a = a.rearrange("o (n h) k -> (o n) (h k)", h=2)
                else:
                    letters = "abc"[:len(a.shape) - 1]
                    a = a.rearrange(" ".join(letters) + " (n p) -> (" + " ".join(letters) + " n) p", p=P)
                return a if r is None else a[r[0]:r[1], :]
            table = [(0, ADA_B, "ada_b", None), (0, C_S, "c", None),
                     (1, K_K, "rw_k_k", None), (1, K_A, "rw_k_a", None), (1, R_K, "rw_r_k", None),
                     (1, W0, "rw_w0", None), (1, A0, "rw_a0", None), (1, LN_W, "rw_ln_w", None),
                     (1, LN_B, "rw_ln_b", None),
                     (1, MU0, "rw_mu", (0, 24)), (1, MUL0, "rw_mu", (24, 27)), (1, MU1, "rw_mu", (27, 51)),
                     (1, MUL1, "rw_mu", (51, 54)),
                     (2, G1, "norm1_g", None), (2, G2, "norm2_g", None), (2, LB0, "hg_lb", None),
                     (2, HGN, "hg_norm_g", None)]
            n = 0
            for t, r, name, cut in table:
                v = rowv(name, cut)
                sp.dma_start(rows[r:r + v.shape[0], t, :], v).then_inc(s_par, 16)
                n += 1
            sp.dma_start(rows[C_P:C_P + KT, 0, :], I["c_ctx"].rearrange("(n p) -> n p", p=P)).then_inc(s_par, 16)
            assert n + 1 == 18
            w = I["ada_w"][0].rearrange("(k p) n -> p k n", p=P)
            for r in range(RING):
                sp.dma_start(ring[r][:, :, :], w[:, :, r * CT * P:(r + 1) * CT * P]).then_inc(s_ada[r], 16)
                if r == RING - 1:
                    for t in range(TT):
                        src = I["x_sample"][0, t * P:(t + 1) * P, :] if t < TT - 1 else I["x_prompt"][0]
                        sp.dma_start(xt[:, t, :], src).then_inc(s_x, 16)
            with sp.Fori(1, NBLK // RING) as i:
                for r in range(RING):
                    sp.wait_ge(s_adaf[r], i)
                    sp.dma_start(ring[r][:, :, :], w[:, :, bass.ds((i * RING + r) * (CT * P), CT * P)]).then_inc(s_ada[r], 16)

        @block.gpsimd
        def _(pool):
            C = S["consts"]
            steps = [0]

            def link(ins):
                steps[0] += 1
                ins.then_inc(s_id, 1)
                pool.wait_ge(s_id, steps[0])
            link(nc.gpsimd.memset(C["ident"][:, :], 0.0))
            link(nc.gpsimd.affine_select(out=C["ident"][:, :], in_=C["ident"][:, :], compare_op=ALU.not_equal, fill=1.0,
                                         base=0, pattern=[[-1, P]], channel_multiplier=1))
            nc.gpsimd.memset(eps[:, :], EPS).then_inc(s_const, 1)
            make_masks(nc, pool, s_masks, C)

        @block.tensor
        def _(pe):
            ident = S["consts"]["ident"]
            pe.wait_ge(s_id, 2)
            pe.wait_ge(s_par, 18 * 16)
            for t, n in enumerate((128, 126, 72)):
                mm = nc.tensor.transpose(ps[:, 4 + t, 0:n], rows[0:n, t, :], ident[0:n, 0:n])
            mm.then_inc(s_ptr, 1)
            pe.wait_ge(s_cond, 1)
            with pe.Fori(0, NBLK // RING) as i:
                for r in range(RING):
                    pe.wait_ge(s_ada[r], i * 16 + 16)
                    pe.wait_ge(s_modc[r], i + 1)
                    for k in range(KT):
                        mm = nc.tensor.matmul(ps[0:2, r, :], cond[:, k, :], ring[r][:, k, :], start=(k == 0), stop=(k == KT - 1))
                    mm.then_inc(s_adaf[r], 1)
            for r in range(RING):
                pe.wait_ge(s_modc[r], NBLK // RING + 1)
            for n in range(NBLK * CT):
                mm = nc.tensor.transpose(ps[:, 3, 2 * n:2 * n + 2], modrow[n // (5 * KT)][:, n % (5 * KT) * P:(n % (5 * KT) + 1) * P],
                                         ident[0:2, 0:2])
            mm.then_inc(s_mod, 1)
            pe.wait_ge(s_xn, TT)
            for j in range(KT):
                b = 4 + 2 * (j % 2)
                if j >= 2:
                    pe.wait_ge(s_h, 2 * (j - 1))
                for t in range(TT):
                    bank = ps[:, b, t * P:(t + 1) * P] if t < TT - 1 else ps[:, b + 1, 0:P]
                    mm = nc.tensor.transpose(bank, xt[:, t, j * P:(j + 1) * P], ident[:, :])
                mm.then_inc(s_xT, 1)

        @block.scalar
        def _(act):
            for r in range(RING):
                act.sem_inc(s_modc[r], 1)
            act.wait_ge(s_const, 1)
            act.wait_ge(s_ptab, 3)
            nc.scalar.activation(th[:, :], S["ptab"][:, 0, C_S:C_S + 2 * KT], ACT.Tanh, scale=0.5).then_inc(s_th, 1)
            for t in range(TT):
                act.wait_ge(s_x, 16 * TT)
                if t:
                    act.wait_ge(s_ssq, t)
                nc.scalar.activation(junk[:, :], xt[:, t, :], ACT.Square, accum_out=ssq[:, t:t + 1]).then_inc(s_ssq, 1)
            act.wait_ge(s_ssq, TT)
            nc.scalar.activation(std[:, :], ssq[:, :], ACT.Sqrt, scale=1.0 / D, bias=eps[:, 0:1]).then_inc(s_std, 1)
            inner = 5 * D // (CT * P) // RING
            with act.Fori(0, inner) as i:
                for r in range(RING):
                    act.wait_ge(s_adaf[r], i + 1)
                    nc.scalar.activation(modrow[0][:, bass.ds((i * RING + r) * (CT * P), CT * P)], ps[0:2, r, :], ACT.Copy)\
                        .then_inc(s_modc[r], 1)
            for n in range(inner * RING, NBLK):
                place, col = divmod(n * CT * P, 5 * D)
                act.wait_ge(s_adaf[n % RING], n // RING + 1)
                nc.scalar.activation(modrow[place][:, col:col + CT * P], ps[0:2, n % RING, :], ACT.Copy).then_inc(s_modc[n % RING], 1)

        @block.vector
        def _(dve):
            steps = [0]

            def link(ins):
                steps[0] += 1
                ins.then_inc(s_v, 1)
                dve.wait_ge(s_v, steps[0])
            ptab, modT, A1, A2 = S["ptab"], S["modT"], S["A1"], S["A2"]
            dve.wait_ge(s_ptr, 1)
            for t, n in enumerate((128, 126, 72)):
                nc.vector.tensor_copy(ptab[:, t, 0:n], ps[:, 4 + t, 0:n]).then_inc(s_ptab, 1)
            dve.wait_ge(s_ptab, 3)
            dve.wait_ge(s_th, 1)
            link(nc.vector.tensor_scalar(th[:, :], th[:, :], 0.5, 0.5, ALU.mult, ALU.add))
            nc.vector.tensor_tensor(cond[:, :, :].rearrange("p k s -> p s k"), th[:, :].rearrange("p (s k) -> p s k", s=2),
                                    ptab[:, 0, C_S:C_S + 2 * KT].rearrange("p (s k) -> p s k", s=2), ALU.mult).then_inc(s_cond, 1)
            dve.wait_ge(s_std, 1)
            link(nc.vector.reciprocal(rstd[:, :], std[:, :]))
            for t in range(TT):
                nc.vector.tensor_scalar(xt[:, t, :], xt[:, t, :], rstd[:, t:t + 1], None, ALU.mult).then_inc(s_xn, 1)
            dve.wait_ge(s_mod, 1)
            link(nc.vector.tensor_tensor(modT[:, :, :], mod, bcast(ptab[:, 0, 0:96], 2, 2), ALU.add))
            for A, c, g in ((A1, KT, G1), (A2, 4 * KT, G2)):
                link(nc.vector.scalar_tensor_tensor(out=A[:, :, :], in0=modT[:, c:c + KT, :], scalar=1.0,
                                                    in1=bcast(ptab[:, 2, g:g + KT], 2, 2), op0=ALU.add, op1=ALU.mult))
            for j in range(KT):
                dve.wait_ge(s_xT, j + 1)
                b = 4 + 2 * (j % 2)
                nc.vector.tensor_scalar(S["hT"][:, j, 0:NS], ps[:, b, :], A1[:, j, 0:1], modT[:, j, 0:1],
                                        ALU.mult, ALU.add).then_inc(s_h, 1)
                nc.vector.tensor_scalar(S["hT"][:, j, NS:T], ps[:, b + 1, 0:NP], A1[:, j, 1:2], modT[:, j, 1:2],
                                        ALU.mult, ALU.add).then_inc(s_h, 1)
            dve.wait_ge(s_h, 2 * KT)


GROUPS = ((0, 4), (4, 4), (8, 2))
HALF = T // 2
LEVELS = 5


def half_view(ps, b):
    return ps[:, b:b + 2, 0:HALF]


def as_halves(ap):
    return ap.rearrange("p (a n) -> p a n", a=2)


def chunks(ap):
    return ap.rearrange("p (c l) -> p c l", l=L)


def make_masks(nc, pool, s_m, C):
    n = [0]

    def link(ins):
        n[0] += 1
        ins.then_inc(s_m, 1)
        pool.wait_ge(s_m, n[0])

    def sel(ap, op, base, pattern, cm):
        link(nc.gpsimd.affine_select(out=ap, in_=ap, compare_op=op, fill=0.0, base=base, pattern=pattern,
                                     channel_multiplier=cm))
    bd = C["bd"]
    link(nc.gpsimd.memset(bd[:, :, :, :], 1.0))
    link(nc.gpsimd.memset(bd[:, 3:5, :, :], -1.0))
    for m in range(5):
        sel(bd[:, m], ALU.is_ge, 0, [[-L, 2], [0, L]], 1)
        sel(bd[:, m], ALU.is_ge, L - 1, [[L, 2], [0, L]], -1)
    sel(bd[:, 1], ALU.is_gt, 0, [[L, 2], [1, L]], -1)
    sel(bd[:, 2], ALU.is_gt, 0, [[-L, 2], [-1, L]], 1)
    sel(bd[:, 3], ALU.is_gt, 0, [[L, 2], [1, L]], -1)
    sel(bd[:, 4], ALU.is_gt, 0, [[-L, 2], [-1, L]], 1)
    cm = C["cm"]
    link(nc.gpsimd.memset(cm[:, :, :], 1.0))
    link(nc.gpsimd.memset(cm[:, 0, :], -1.0))
    link(nc.gpsimd.memset(cm[:, 2, :], -1.0))
    for h in range(2):
        q = slice(L * h, L * h + L)
        sel(cm[q, 0, :], ALU.is_gt, 0, [[1, L]], -1)
        sel(cm[q, 1, :], ALU.is_ge, 0, [[1, L]], -1)
        sel(cm[q, 2, :], ALU.is_gt, 0, [[-1, L]], 1)
        sel(cm[q, 3, :], ALU.is_ge, 0, [[-1, L]], 1)
    link(nc.gpsimd.memset(C["ci"][:, :], 0.0))
    for h in range(2):
        link(nc.gpsimd.affine_select(out=C["ci"][L * h:L * h + L, :], in_=C["ci"][L * h:L * h + L, :],
                                     compare_op=ALU.not_equal, fill=1.0, base=0, pattern=[[-1, L]],
                                     channel_multiplier=1))
    link(nc.gpsimd.memset(C["ns"][:, :], 1.0))
    link(nc.gpsimd.memset(chunks(C["ns"][:, :])[:, :, 0:1], 0.0))
    link(nc.gpsimd.memset(C["ones"][:, :], 1.0))
    link(nc.gpsimd.memset(C["eps"][:, 0:1], EPS))
    link(nc.gpsimd.memset(C["eps"][:, 1:2], LN_EPS))


def mix_neighbours(nc, link, out, raw, c, mu0, mu1):
    link(nc.vector.tensor_scalar(out, raw, c, None, ALU.mult))
    for cut, w in ((slice(0, NS), GRID_W), (slice(NS, T), NP)):
        o, r = (a[:, cut].rearrange("p (n w) -> p n w", w=w) for a in (out, raw))
        link(nc.vector.scalar_tensor_tensor(out=o[:, :, 1:w], in0=r[:, :, 0:w - 1], scalar=mu0, in1=o[:, :, 1:w],
                                            op0=ALU.mult, op1=ALU.add))
        link(nc.vector.scalar_tensor_tensor(out=o[:, :, 0:w - 1], in0=r[:, :, 1:w], scalar=mu1, in1=o[:, :, 0:w - 1],
                                            op0=ALU.mult, op1=ALU.add))


def stage_lora(nc, I, S):
    with ExitStack() as ctx:
        sb = lambda name, shape, dt=F32: ctx.enter_context(nc.sbuf_tensor(name, shape, dt))
        sg = lambda name: ctx.enter_context(nc.semaphore(name))
        w = sb("wlora", [P, KT, 3 * P])
        raw = sb("rawlora", [P, 3, T])
        cl = sb("clora", [P, 3])
        ps = ctx.enter_context(nc.psum_tensor("psL", [P, 8, 512], F32))
        s_w, s_p, s_raw, s_v, s_mix, s_th, s_z, s_out = map(sg, (
            "lora_w_in", "lora_projected", "lora_raw", "lora_vec", "lora_mixed", "lora_tanh", "lora_zeroed", "lora_rows"))
        block = ctx.enter_context(nc.Block())
        lora = S["lora"]

        @block.sync
        def _(sp):
            sp.dma_start(w[:, :, :], I["w_in"][0].rearrange("(k p) n -> p k n", p=P)[:, :, 3 * RW_DIM:RW_COLS]).then_inc(s_w, 16)

        @block.gpsimd
        def _(pool):
            nc.gpsimd.memset(S["lw"][:, :, :, :], 0.0).then_inc(s_z, 1)
            pool.wait_ge(s_z, 1)

        @block.tensor
        def _(pe):
            pe.wait_ge(s_w, 16)
            for i in range(3):
                for h in range(2):
                    for k in range(KT):
                        mm = nc.tensor.matmul(ps[:, 2 * i + h, 0:HALF], w[:, k, i * P:(i + 1) * P],
                                              S["hT"][:, k, h * HALF:(h + 1) * HALF], start=(k == 0), stop=(k == KT - 1))
                mm.then_inc(s_p, 1)

        @block.scalar
        def _(act):
            for i in range(3):
                act.wait_ge(s_p, i + 1)
                nc.scalar.activation(as_halves(raw[:, i, :]), half_view(ps, 2 * i), ACT.Copy).then_inc(s_raw, 1)
            act.wait_ge(s_mix, 1)
            nc.scalar.activation(lora[:, 0, :], lora[:, 0, :], ACT.Tanh).then_inc(s_th, 1)
            nc.scalar.activation(lora[:, 2, :], lora[:, 2, :], ACT.Tanh, scale=0.5).then_inc(s_th, 1)

        @block.vector
        def _(dve):
            steps = [0]

            def link(ins):
                steps[0] += 1
                ins.then_inc(s_v, 1)
                dve.wait_ge(s_v, steps[0])
            t1 = S["ptab"][:, 1, :]
            link(nc.vector.tensor_tensor(cl[:, :], t1[:, MUL0:MUL0 + 3], t1[:, MUL1:MUL1 + 3], ALU.add))
            link(nc.vector.tensor_scalar(cl[:, :], cl[:, :], -1.0, 1.0, ALU.mult, ALU.add))
            for i in range(3):
                dve.wait_ge(s_raw, i + 1)
                mix_neighbours(nc, link, lora[:, i, :], raw[:, i, :], cl[:, i:i + 1], t1[:, MUL0 + i:MUL0 + i + 1],
                               t1[:, MUL1 + i:MUL1 + i + 1])
            dve.sem_inc(s_mix, 1)
            dve.wait_ge(s_th, 2)
            link(nc.vector.tensor_scalar(lora[:, 2, :], lora[:, 2, :], 0.5, 0.5, ALU.mult, ALU.add))


def stage_rwkv(nc, I, O, S, per):
    with ExitStack() as ctx:
        sb = lambda name, shape, dt=F32: ctx.enter_context(nc.sbuf_tensor(name, shape, dt))
        C = S["consts"]
        sig = {}

        def signal(name):
            if name not in sig:
                sig[name] = Signal(ctx, nc, "rw_" + name, per.get(name, 0))
            return sig[name]
        w = sb("wrkv", [P, 3, KT, P])
        raw = sb("raw", [P, 3, T])
        mix = sb("mix", [P, 3, T])
        kk, kds, ysum = sb("kk", [P, T]), sb("kds", [P, T]), sb("ysum", [P, T])
        t1, t2, t3, t4, t5 = (sb(f"t{i}", [P, T]) for i in range(1, 6))
        outr = sb("outr", [P, T])
        gate = [sb(f"gate{i}", [P, T]) for i in range(2)]
        t6, t7, t8 = (raw[:, i, :] for i in range(3))
        pp, dp, tot, etot = sb("pp", [P, 15]), sb("dp", [P, 9]), sb("tot", [P, NCH]), sb("etot", [P, NCH])
        KR = sb("KR", [P, NCH, 2, L])
        cB = sb("cB", [P, NCH, L])
        bdB, bdK, bdKW, bdBn, bdKn, bdV = (sb(n, [P, NCH, 2, L]) for n in ("bdB", "bdK", "bdKW", "bdBn", "bdKn", "bdV"))
        cV, RbT, RkT, TTc, cN = (sb(n, [P, NCH, L]) for n in ("cV", "RbT", "RkT", "TTc", "cN"))
        bdAk, bdTT, bdNT = (sb(n, [P, NCH, 2, L]) for n in ("bdAk", "bdTT", "bdNT"))
        bdN = bdTT
        Sc, bdS, nR, cSA, bdSA = (sb("Sc", [P, 2, L]), sb("bdS", [P, 2, 2, L]), sb("nR", [P, L]), sb("cSA", [P, L]),
                                  sb("bdSA", [P, 2, L]))
        s0 = sb("s0", [P, 2, L])
        sout = sb("sout", [P, 2, L])
        ps = ctx.enter_context(nc.psum_tensor("psR", [P, 8, 512], F32))
        block = ctx.enter_context(nc.Block())
        g2 = S["lw"]
        lora = S["lora"]
        ident = C["ident"][:, :]
        blk = C["bd"][:, 0]
        blockones = blk.rearrange("p g l -> p (g l)")

        def bank(b, n, width):
            return ps[:, b, 0:n * width].rearrange("p (c l) -> p c l", l=width)
        GB = (4, 5, 6)

        def sq_view(g, n):
            return ps[:, GB[g], 0:n * L].rearrange("p (c l) -> p c l", l=L)

        def tt_view(g, n):
            return ps[:, GB[g], n * L:2 * n * L].rearrange("p (c l) -> p c l", l=L)

        def tr_view(g, n):
            return ps[:, 7, 0:n * P].rearrange("p (c l) -> p c l", l=P)

        def chain():
            return lambda d: [(c, c == 0, c == 7) if d == 0 else (7 - c, c == 0, c == 7) for c in range(8)] + \
                [(8 + e if d == 0 else 9 - e, e == 0, e == 1) for e in range(2)]
        steps_of = chain()
        TILE = 2 * KT
        SLOT = (1, 2, 0, 1, 2, 0, 2)
        BANK = (0, 2, 0, 2, 0, 2, 0)
        SLOT_BEFORE = (0, 3, 2, 4, 5, 6, 8)
        BANK_BEFORE = (3, 2, 4, 5, 6, 7, 8)
        NT = len(SLOT)

        def slot_turn(i):
            return SLOT[:i + 1].count(SLOT[i]), SLOT.count(SLOT[i]), SLOT[4:].count(SLOT[i])

        def tile_columns(r, i):
            return r * (4 * P) + (GATE0 + i * P) if i < 4 else r * P + (P + (i - 4) * RW_DIM)

        @block.sync
        def _(sp):
            win = I["w_in"][0].rearrange("(k p) n -> p k n", p=P)
            rw = lambda n: signal(n)
            sp.sem_inc(rw("final_free").sem, 3)
            for i in range(3):
                if i == 2:
                    sp.wait_ge(rw("tile_done").sem, 1)
                sp.dma_start(w[:, SLOT[4 + i], :, :], win[:, :, i * RW_DIM:i * RW_DIM + P]).then_inc(rw(f"w_in{SLOT[4 + i]}").sem, 16)
                if i == 1:
                    sp.dma_start(w[:, SLOT[0], :, :], win[:, :, GATE0:GATE0 + P]).then_inc(rw(f"w_in{SLOT[0]}").sem, 16)

            def load(r, i):
                sp.wait_ge(rw("tile_done").sem, r * NT + SLOT_BEFORE[i])
                sp.dma_start(w[:, SLOT[i], :, :], win[:, :, bass.ds(tile_columns(r, i), P)]).then_inc(rw(f"w_in{SLOT[i]}").sem, 16)

            def store(r, i):
                sp.wait_ge(rw("tile_taken").sem, r * NT + (3 + i + 1))
                sp.dma_start(S["gates"][bass.ds(r * 4 + i, 1)].rearrange("o p n -> (o p) n"), gate[i % 2][:, :])\
                    .then_inc(rw(f"gate_out{i % 2}").sem, 16)
            for i in (2, 1):
                load(0, i)

            def body(r, last):
                sp.wait_ge(rw("lw_free").sem, r * rw("lw_free").per + 1)
                for j, name in enumerate(("rw_w2", "rw_a2")):
                    for d in range(2):
                        sp.dma_start(g2[L * d:L * d + L, j, d, :], I[name][0, d][:, bass.ds(r * P, P)]).then_inc(rw("lw_in").sem, 16)
                sp.dma_start(g2[:, 2, 0, :], I["rw_g2"][0][:, bass.ds(r * P, P)]).then_inc(rw("lw_in").sem, 16)
                for d in range(2):
                    sp.wait_ge(rw("s0_free").sem, r * 2 + d + 1)
                    sp.dma_start(s0[:, d, :], I["state_rwkv"][0, 0, d].rearrange("h v k -> (h v) k")[bass.ds(r * P, P), :])\
                        .then_inc(rw(f"s0_in{d}").sem, 16)
                for i in range(4):
                    if i == 0 or (i < 3 and not last):
                        load(r, 3 + i)
                    store(r, i)
                if not last:
                    load(r + 1, 0)
                    load(r, 6)
                for d in range(2):
                    sp.wait_ge(rw("final_ready").sem, r * 2 + d + 1)
                    sp.dma_start(O["new_state_rwkv"][0, 0, d].rearrange("h v k -> (h v) k")[bass.ds(r * P, P), :], sout[:, d, :])\
                        .then_inc(rw("final_out").sem, 16)
                    sp.wait_ge(rw("final_out").sem, r * 48 + 16 * (d + 1))
                    sp.sem_inc(rw("final_free").sem, 1)
                if not last:
                    load(r + 1, 2)
                    load(r + 1, 1)
                sp.wait_ge(rw("round_done").sem, r + 1)
                sp.dma_start(S["outr"][bass.ds(r, 1)].rearrange("o p n -> (o p) n"), outr[:, :]).then_inc(rw("final_out").sem, 16)
                sp.wait_ge(rw("final_out").sem, r * 48 + 48)
                sp.sem_inc(rw("final_free").sem, 1)
            with sp.Fori(0, PAIRS - 1) as r:
                body(r, False)
            body(PAIRS - 1, True)
            for i in range(2):
                sp.wait_ge(rw(f"gate_out{i}").sem, 16 + 32 * PAIRS)

        @block.gpsimd
        def _(pool):
            nc.gpsimd.memset(bdK[:, :, :, :], 0.0).then_inc(signal("bdk_zeroed").sem, 1)
            with pool.Fori(0, PAIRS) as r:
                for d in range(2):
                    def bd(out, src, need):
                        pool.wait_ge(signal("factors").sem, signal("factors").at(5 * d + need, r))
                        nc.gpsimd.tensor_tensor(out[:, :, :, :], bcast(src, 2, 2), bcast(blk, NCH, 1), ALU.mult)\
                            .then_inc(signal("bd_factors").sem, 1)
                    bd(bdKW, KR[:, :, 0, :], 1)
                    bd(bdB, cB[:, :, :], 3)

        @block.tensor
        def _(pe):
            W = lambda name, n, r: pe.wait_ge(signal(name).sem, signal(name).at(n, r))
            cnt = {}

            def inc(mm, name):
                mm.then_inc(signal(name).sem, 1)
                cnt[name] = cnt.get(name, 0) + 1
            pe.sem_inc(signal("lw_free").sem, 1)

            def product(i, n):
                h, k = n // KT, n % KT
                mm = nc.tensor.matmul(ps[:, BANK[i] + h, 0:HALF], w[:, SLOT[i], k, :], S["hT"][:, k, h * HALF:(h + 1) * HALF],
                                      start=(k == 0), stop=(k == KT - 1))
                if n == TILE - 1:
                    inc(mm, "tile_done")

            def body(r, last):
                ahead = [0]

                def fill(count):
                    for p in range(ahead[0], ahead[0] + count):
                        i, n = divmod(p, TILE)
                        if last and i >= 4:
                            break
                        if n == 0:
                            turn, turns, before = slot_turn(i)
                            pe.wait_ge(signal(f"w_in{SLOT[i]}").sem, r * (16 * turns) + 16 * (turn + before))
                            pe.wait_ge(signal("tile_taken").sem, r * NT + BANK_BEFORE[i])
                        product(i, n)
                    ahead[0] += count

                def sums(lhsT, rhs, b):
                    for h in range(2):
                        mm = nc.tensor.matmul(ps[:, b + h, 0:HALF], lhsT, rhs[:, h * HALF:(h + 1) * HALF], start=True, stop=True)
                    return mm
                fill(20)
                W("kk_squares", 1, r)
                inc(sums(blockones, t1[:, :], 4), "kk_sums")
                W("v_spread", 2, r)
                W("kk_max", 1, r)
                for g, (c0, n) in enumerate(GROUPS):
                    for c in range(c0, c0 + n):
                        mm = nc.tensor.transpose(ps[:, 4 + g, (c - c0) * P:(c - c0 + 1) * P], bdK[:, c].rearrange("p g l -> p (g l)"), ident)
                    inc(mm, "v_turned")
                W("bdv_ready", 3, r)
                pe.wait_ge(signal("lw_in").sem, r * 80 + 80)
                for d in range(2):
                    if d:
                        W("y_taken", 1, r)
                        W("final_taken", 1, r)
                    sums(g2[:, 0, d, :], lora[:, 0, :], 4)
                    inc(sums(g2[:, 1, d, :], lora[:, 1, :], 6), "lora_sums")
                    fill(40 - 2 * d)
                    W("lora_taken", 2 * d + 2, r)
                    W("bd_factors", 2 * d + 2, r)
                    W("factors", 5 * d + 5, r)
                    flat = lambda a, c: a[:, c].rearrange("p g l -> p (g l)")
                    for g, (c0, n) in enumerate(GROUPS):
                        if g:
                            W("grams_taken", 3 * d + g, r)
                        for b, lhs in ((4, bdB), (5, bdK)):
                            for c in range(c0, c0 + n):
                                nc.tensor.matmul(ps[:, b, (c - c0) * P:(c - c0 + 1) * P], flat(lhs, c), flat(KR, c), start=True, stop=True)
                        for c in range(c0, c0 + n):
                            mm = nc.tensor.matmul(ps[:, 6, (c - c0) * L:(c - c0 + 1) * L], flat(bdKW, c), cB[:, c, :], start=True, stop=True)
                        inc(mm, "grams")
                        for b, src in ((7, bdB), (7, bdK)):
                            k = 6 * d + 2 * g + (src is bdK)
                            if k:
                                W("rows_taken", k, r)
                            for c in range(c0, c0 + n):
                                mm = nc.tensor.transpose(ps[:, b, (c - c0) * P:(c - c0 + 1) * P], flat(src, c), ident)
                            inc(mm, "rows_turned")
                        fill(4 if g < 2 else 3)
                    W("grams_taken", 3 * d + 3, r)
                    W("rows_taken", 6 * d + 6, r)
                    for i in range(LEVELS):
                        top = i == LEVELS - 1
                        for g, (c0, n) in enumerate(GROUPS):
                            if i:
                                W("bdnt_ready", 4 * 3 * d + 3 * (i - 1) + g + 1, r)
                                W("cn_ready", 2 * (12 * d + 3 * (i - 1) + g + 1), r)
                                W("tt_ready", 15 * d + 3 * (i - 1) + g + 1, r)
                            for c in range(c0, c0 + n):
                                mm = nc.tensor.matmul(sq_view(g, n)[:, c - c0, :], flat(bdNT, c), cN[:, c, :], start=True, stop=True)
                            inc(mm, "squared")
                        for g, (c0, n) in enumerate(GROUPS):
                            k = 15 * d + 3 * i + g + 1
                            W("bdn_ready", k, r)
                            for c in range(c0, c0 + n):
                                mm = nc.tensor.matmul(tt_view(g, n)[:, c - c0, :], flat(bdN, c), TTc[:, c, :], start=True, stop=True)
                            inc(mm, "tt_sums")
                            if not top:
                                if g:
                                    W("bdnt_ready", 12 * d + 3 * i + g, r)
                                for c in range(c0, c0 + n):
                                    mm = nc.tensor.transpose(tr_view(g, n)[:, c - c0, :], flat(bdN, c), ident)
                                inc(mm, "n_turned")
                            fill(2 if g == 0 else 1)
                    fill(3)
                    W("bdtt_ready", 3 * d + 3, r)
                    W("s0_spread", d + 1, r)
                    inc(nc.tensor.transpose(ps[:, 4, 0:P], bdSA[:, :, :].rearrange("p g l -> p (g l)"), ident), "s0_turned")
                    Yv = lambda c: ps[:, 6, c * L:(c + 1) * L] if c < 8 else ps[:, 7, (c - 8) * L:(c - 7) * L]
                    steps = steps_of(d)

                    def first_sum(j):
                        c, first, _ = steps[j]
                        alone = c >= 8 and first
                        mm = nc.tensor.matmul(ps[:, 5, P:P + L], flat(bdAk, c), cV[:, c, :], start=True, stop=alone)
                        if alone:
                            inc(mm, "r_sums")
                    first_sum(0)
                    for j, (c, first, lastc) in enumerate(steps):
                        hs = c < 8 or not first
                        q = j % 2
                        k = 10 * d + j + 1
                        if j == 0:
                            W("s0_ready", d + 1, r)
                        else:
                            W("state_ready", k - 1, r)
                        if hs:
                            inc(nc.tensor.matmul(ps[:, 5, P:P + L], flat(bdKW, c), Sc[:, q, :], start=False, stop=True), "r_sums")
                        nc.tensor.matmul(Yv(c), flat(bdV, c), RkT[:, c, :], start=True, stop=False)
                        if j:
                            W("state_spread", k - 1, r)
                        nc.tensor.matmul(ps[:, 4, P:P + L], flat(bdKn, c), cV[:, c, :], start=True, stop=False)
                        fill(1)
                        W("nr_ready", k, r)
                        inc(nc.tensor.matmul(ps[:, 5, 0:L], flat(bdTT, c), nR[:, :], start=True, stop=True), "sa_sums")
                        if hs:
                            nc.tensor.matmul(ps[:, 4, P:P + L], ident, Sc[:, q, :], start=False, stop=False)
                            nc.tensor.matmul(Yv(c), bdS[:, q].rearrange("p g l -> p (g l)"), KR[:, c, 1, :], start=False, stop=False)
                        W("sa_ready", k, r)
                        inc(nc.tensor.matmul(ps[:, 4, P:P + L], flat(bdBn, c), cSA[:, :], start=False, stop=True), "state_sums")
                        W("sa_spread", k, r)
                        inc(nc.tensor.matmul(Yv(c), bdSA[:, :, :].rearrange("p g l -> p (g l)"), RbT[:, c, :], start=False, stop=True), "y_sums")
                        if j < 9:
                            first_sum(j + 1)
                        if j % 2 == 0:
                            fill(1)
                    W("state_spread", 10 * d + 10, r)
                    inc(nc.tensor.transpose(ps[:, 4, 0:P], bdS[:, 0].rearrange("p g l -> p (g l)"), ident), "final_turned")
                    fill(8 if d else 2)
                W("y_taken", 2, r)
                W("final_taken", 2, r)
                W("bonus_products", 1, r)
                inc(sums(blockones, t1[:, :], 4), "bonus_sums")
                inc(sums(blockones, ysum[:, :], 6), "mean_sums")
                fill(4)
                W("bonus_ready", 1, r)
                inc(sums(g2[:, 2, 0, :], lora[:, 2, :], 4), "gate_sums")
                W("y_squares", 1, r)
                inc(sums(blockones, t2[:, :], 6), "var_sums")
                pe.wait_ge(signal("var_sums").sem, signal("var_sums").at(1, r))
                pe.sem_inc(signal("lw_free").sem, 1)
                fill(14)
                W("round_done", 1, r)
                assert ahead[0] == NT * TILE
            for i in range(4, NT):
                pe.wait_ge(signal(f"w_in{SLOT[i]}").sem, 16 * SLOT[4:i + 1].count(SLOT[i]))
                if i == 6:
                    pe.wait_ge(signal("tile_taken").sem, 1)
                for n in range(TILE):
                    product(i, n)
            cnt.clear()
            with pe.Fori(0, PAIRS - 1) as r:
                body(r, False)
            S["pe_cnt"] = dict(cnt)
            body(PAIRS - 1, True)

        @block.scalar
        def _(act):
            W = lambda name, n, r: act.wait_ge(signal(name).sem, signal(name).at(n, r))
            cnt = {}

            def inc(ins, name):
                ins.then_inc(signal(name).sem, 1)
                cnt[name] = cnt.get(name, 0) + 1
            act.wait_ge(signal("bdk_zeroed").sem, 1)
            A = nc.scalar.activation
            for i in range(2):
                act.sem_inc(signal(f"gate_out{i}").sem, 16)

            def take_raw(r, i):
                act.wait_ge(signal("tile_done").sem, NT * (r + 1) + (i + 1))
                act.wait_ge(signal("raw_free").sem, (r + 1) + 1)
                inc(A(as_halves(raw[:, i, :]), half_view(ps, BANK[4 + i]), ACT.Copy), "tile_taken")

            def take_gate(r, i):
                act.wait_ge(signal("tile_done").sem, r * NT + (3 + i + 1))
                act.wait_ge(signal(f"gate_out{i % 2}").sem, r * 32 + 16 * (i // 2 + 1))
                inc(A(as_halves(gate[i % 2][:, :]), half_view(ps, BANK[i]), ACT.Tanh, scale=0.5), "tile_taken")

            def body(r, last):
                W("mixed", 3, r)
                for h in range(2):
                    q = slice(L * h, L * h + L)
                    inc(A(bdK[q, :, h, :], chunks(mix[q, 2, :]), ACT.Copy), "v_spread")
                W("kk_raw", 1, r)
                inc(A(t1[:, :], kk[:, :], ACT.Square), "kk_squares")
                W("kk_max", 1, r)
                inc(A(t2[:, :], t2[:, :], ACT.Sqrt), "kk_root")
                for g, (c0, n) in enumerate(GROUPS):
                    W("v_turned", g + 1, r)
                    inc(A(bdV[:, c0:c0 + n].rearrange("p c g l -> p c (g l)"), bank(4 + g, n, P), ACT.Copy), "bdv_ready")
                for d in range(2):
                    W("lora_sums", d + 1, r)
                    if d == 0:
                        W("kk_ready", 1, r)
                    W("derived", 1, r)
                    inc(A(as_halves(t1[:, :]), half_view(ps, 4), ACT.Tanh, scale=0.5, bias=dp[:, 3 + d:4 + d]), "lora_taken")
                    if d:
                        W("bd_factors", 2, r)
                    inc(A(as_halves(t2[:, :]), half_view(ps, 6), ACT.Tanh, scale=0.5, bias=dp[:, 5 + d:6 + d]), "lora_taken")
                    W("logs", d + 1, r)
                    inc(A(etot[:, :], tot[:, :], ACT.Exp), "exps")
                    inc(A(t6, t5[:, :], ACT.Exp), "exps")
                    inc(A(t7, t4[:, :], ACT.Exp), "exps")
                    inc(A(t8, t4[:, :], ACT.Exp, scale=-1.0), "exps")
                    take_gate(r, 3 * d)
                    for g, (c0, n) in enumerate(GROUPS):
                        for m, out in enumerate((bdBn, bdKn)):
                            W("rows_turned", 6 * d + 2 * g + m + 1, r)
                            inc(A(out[:, c0:c0 + n].rearrange("p c g l -> p c (g l)"), bank(7, n, P), ACT.Copy), "rows_taken")
                    for i in range(LEVELS - 1):
                        for g, (c0, n) in enumerate(GROUPS):
                            W("bdn_ready", 15 * d + 3 * i + g + 1, r)
                            for h in range(2):
                                q = slice(L * h, L * h + L)
                                inc(A(cN[q, c0:c0 + n, :], bdN[q, c0:c0 + n, h, :], ACT.Copy), "cn_ready")
                        for g, (c0, n) in enumerate(GROUPS):
                            W("n_turned", 12 * d + 3 * i + g + 1, r)
                            inc(A(bdNT[:, c0:c0 + n].rearrange("p c g l -> p c (g l)"), tr_view(g, n), ACT.Copy), "bdnt_ready")
                        if i == 0 and d == 0:
                            take_gate(r, 1)
                        if i == 0 and d and not last:
                            take_raw(r, 0)
                    for j in range(10):
                        k = 10 * d + j + 1
                        W("r_sums", k, r)
                        inc(A(nR[:, :], ps[:, 5, P:P + L], ACT.Copy, scale=-1.0), "nr_ready")
                        if d == 0 and j == 1:
                            take_gate(r, 2)
                        if d == 1 and j == 6 and not last:
                            take_raw(r, 1)
                W("y_squares_in", 1, r)
                inc(A(t2[:, :], t4[:, :], ACT.Square), "y_squares")
                W("var_sums", 1, r)
                inc(A(as_halves(t5[:, :]), half_view(ps, 6), ACT.Sqrt, scale=1.0 / L, bias=C["eps"][:, 1:2]), "ln_root")
                if not last:
                    take_raw(r, 2)
            for i in range(3):
                take_raw(-1, i)
            cnt.clear()
            with act.Fori(0, PAIRS - 1) as r:
                body(r, False)
            S["act_cnt"] = dict(cnt)
            body(PAIRS - 1, True)

        @block.vector
        def _(dve):
            W = lambda name, n, r: dve.wait_ge(signal(name).sem, signal(name).at(n, r))
            V = nc.vector
            dve.sem_inc(signal("raw_free").sem, 1)
            dve.sem_inc(signal("s0_free").sem, 2)
            cnt = {}
            with dve.Fori(0, PAIRS) as r:
                cnt.clear()

                def did(ins, name):
                    cnt[name] = cnt.get(name, 0) + 1
                    ins.then_inc(signal(name).sem, 1)
                    dve.wait_ge(signal(name).sem, signal(name).at(cnt[name], r))
                link = lambda ins: did(ins, "vector_line")

                def raised(name, k=1):
                    dve.sem_inc(signal(name).sem, k)
                    cnt[name] = cnt.get(name, 0) + k
                link(V.tensor_copy(pp[:, :], S["ptab"][:, 1, 0:120].rearrange("p (n e) -> p n e", e=PAIRS)[:, :, bass.ds(r, 1)].rearrange("p n e -> p (n e)")))
                link(V.tensor_tensor(dp[:, 0:3], pp[:, 0:3], pp[:, 3:6], ALU.add))
                link(V.tensor_scalar(dp[:, 0:3], dp[:, 0:3], -1.0, 1.0, ALU.mult, ALU.add))
                link(V.tensor_scalar(dp[:, 3:7], pp[:, 9:13], 0.5, None, ALU.mult))
                link(V.tensor_scalar(dp[:, 7:8], pp[:, 7:8], 0.5, None, ALU.mult))
                did(V.tensor_scalar(dp[:, 8:9], pp[:, 7:8], -0.5, 1.0, ALU.mult, ALU.add), "derived")
                for i in range(3):
                    W("tile_taken", i + 1, r)
                    mix_neighbours(nc, link, mix[:, i, :], raw[:, i, :], dp[:, i:i + 1], pp[:, i:i + 1], pp[:, 3 + i:4 + i])
                    raised("mixed")
                rT, kT, vT = mix[:, 0, :], mix[:, 1, :], mix[:, 2, :]
                did(V.tensor_scalar(kk[:, :], kT, pp[:, 6:7], None, ALU.mult), "kk_raw")
                W("kk_sums", 1, r)
                did(V.tensor_scalar(as_halves(t2[:, :]), half_view(ps, 4), 1e-24, None, ALU.max), "kk_max")
                W("kk_root", 1, r)
                link(V.reciprocal(t2[:, :], t2[:, :]))
                did(V.tensor_tensor(kk[:, :], kk[:, :], t2[:, :], ALU.mult), "kk_ready")
                W("bdv_ready", 3, r)
                link(V.tensor_tensor(cV[:, :, :], bdV[:, :, 0, :], bdV[:, :, 1, :], ALU.add))
                for d in range(2):
                    mT, mI, mN = (1, 1, 2) if d == 0 else (2, 3, 1)
                    W("lora_taken", 2 * d + 2, r)
                    link(V.tensor_scalar(t1[:, :], t1[:, :], -0.5 * DECAY_SCALE, -0.5 * DECAY_SCALE, ALU.mult, ALU.add))
                    link(V.tensor_scalar(t3[:, :], t2[:, :], dp[:, 7:8], dp[:, 8:9], ALU.mult, ALU.add))
                    link(V.tensor_tensor(t3[:, :], t3[:, :], kT, ALU.mult))
                    if d == 0:
                        link(V.tensor_copy(kds[:, :], t3[:, :]))
                    else:
                        link(V.tensor_tensor(kds[:, :], kds[:, :], t3[:, :], ALU.add))
                    link(V.tensor_scalar(t2[:, :], t2[:, :], 0.5, 0.5, ALU.mult, ALU.add))
                    link(V.tensor_tensor(t2[:, :], t2[:, :], kk[:, :], ALU.mult))
                    link(V.tensor_tensor_scan(t4[:, :], C["ns"][:, :], t1[:, :], 0.0, ALU.mult, ALU.add))
                    link(V.tensor_copy(tot[:, :].rearrange("p (c o) -> p c o", o=1), chunks(t4[:, :])[:, :, L - 1:L]))
                    if d == 0:
                        did(V.tensor_tensor(t5[:, :], t4[:, :], t1[:, :], ALU.subtract), "logs")
                    else:
                        link(V.tensor_tensor(chunks(t5[:, :]), bcast(tot[:, :], L, 2), chunks(t4[:, :]), ALU.subtract))
                        did(V.tensor_tensor(t4[:, :], t5[:, :], t1[:, :], ALU.add), "logs")
                    W("exps", 4 * d + 4, r)
                    did(V.tensor_tensor(KR[:, :, 0, :], chunks(kk[:, :]), chunks(t6), ALU.mult), "factors")
                    did(V.tensor_tensor(KR[:, :, 1, :], chunks(rT), chunks(t7), ALU.mult), "factors")
                    did(V.tensor_tensor(cB[:, :, :], chunks(t2[:, :]), chunks(t8), ALU.mult), "factors")
                    did(V.tensor_tensor(t3[:, :], t3[:, :], t8, ALU.mult), "factors")
                    did(V.tensor_tensor(bdK[:, :, :, :], bcast(chunks(t3[:, :]), 2, 2), bcast(blk, NCH, 1), ALU.mult), "factors")
                    if d:
                        raised("raw_free")
                    for g, (c0, n) in enumerate(GROUPS):
                        cs = slice(c0, c0 + n)
                        W("grams", 3 * d + g + 1, r)
                        G1, G2, G3 = bank(4, n, P), bank(5, n, P), bank(6, n, L)
                        link(V.tensor_tensor(bdNT[:, cs], bcast(G1[:, :, 0:L], 2, 2), bcast(C["bd"][:, 2 + mT], n, 1), ALU.mult))
                        link(V.tensor_tensor(TTc[:, cs], G1[:, :, 0:L], bcast(C["cm"][:, 2 * d], n, 1), ALU.mult))
                        link(V.tensor_tensor(TTc[:, cs], TTc[:, cs], bcast(C["ci"][:, :], n, 1), ALU.add))
                        link(V.tensor_tensor(RbT[:, cs], G1[:, :, L:P], bcast(C["cm"][:, mI], n, 1), ALU.mult))
                        link(V.tensor_tensor(bdAk[:, cs], bcast(G2[:, :, 0:L], 2, 2), bcast(C["bd"][:, mT], n, 1), ALU.mult))
                        link(V.tensor_tensor(RkT[:, cs], G2[:, :, L:P], bcast(C["cm"][:, mI], n, 1), ALU.mult))
                        did(V.tensor_tensor(cN[:, cs], G3, bcast(C["cm"][:, 2 - 2 * d], n, 1), ALU.mult), "grams_taken")
                    for i in range(LEVELS):
                        for g, (c0, n) in enumerate(GROUPS):
                            W("squared", 15 * d + 3 * i + g + 1, r)
                            did(V.tensor_tensor(bdN[:, c0:c0 + n], bcast(sq_view(g, n), 2, 2), bcast(blk, n, 1), ALU.mult), "bdn_ready")
                        for g, (c0, n) in enumerate(GROUPS):
                            W("tt_sums", 15 * d + 3 * i + g + 1, r)
                            did(V.tensor_tensor(TTc[:, c0:c0 + n], TTc[:, c0:c0 + n], tt_view(g, n), ALU.add), "tt_ready")
                    for g, (c0, n) in enumerate(GROUPS):
                        did(V.tensor_tensor(bdTT[:, c0:c0 + n], bcast(TTc[:, c0:c0 + n], 2, 2), bcast(blk, n, 1), ALU.mult), "bdtt_ready")
                    dve.wait_ge(signal(f"s0_in{d}").sem, r * 16 + 16)
                    did(V.tensor_tensor(bdSA[:, :, :], bcast(s0[:, d, :], 2, 1), blk, ALU.mult), "s0_spread")
                    raised("s0_free")
                    W("s0_turned", d + 1, r)
                    link(V.tensor_copy(bdS[:, 0].rearrange("p g l -> p (g l)"), ps[:, 4, 0:P]))
                    did(V.tensor_tensor(Sc[:, 0, :], bdS[:, 0, 0, :], bdS[:, 0, 1, :], ALU.add), "s0_ready")
                    for j, (c, first, lastc) in enumerate(steps_of(d)):
                        k = 10 * d + j + 1
                        q = (j + 1) % 2
                        W("sa_sums", k, r)
                        did(V.tensor_copy(cSA[:, :], ps[:, 5, 0:L]), "sa_ready")
                        if j:
                            W("y_sums", k - 1, r)
                        did(V.tensor_tensor(bdSA[:, :, :], bcast(ps[:, 5, 0:L], 2, 1), blk, ALU.mult), "sa_spread")
                        W("state_sums", k, r)
                        did(V.tensor_scalar(Sc[:, q, :], ps[:, 4, P:P + L], etot[:, c:c + 1], None, ALU.mult), "state_ready")
                        did(V.scalar_tensor_tensor(out=bdS[:, q], in0=bcast(ps[:, 4, P:P + L], 2, 1), scalar=etot[:, c:c + 1],
                                                   in1=blk, op0=ALU.mult, op1=ALU.mult), "state_spread")
                    W("y_sums", 10 * d + 10, r)
                    if d == 0:
                        link(V.tensor_copy(ysum[:, 0:NS], ps[:, 6, :]))
                        did(V.tensor_copy(ysum[:, NS:T], ps[:, 7, 0:NP]), "y_taken")
                    else:
                        link(V.tensor_tensor(ysum[:, 0:NS], ysum[:, 0:NS], ps[:, 6, :], ALU.add))
                        did(V.tensor_tensor(ysum[:, NS:T], ysum[:, NS:T], ps[:, 7, 0:NP], ALU.add), "y_taken")
                    W("final_turned", d + 1, r)
                    link(V.tensor_copy(bdSA[:, :, :].rearrange("p g l -> p (g l)"), ps[:, 4, 0:P]))
                    raised("final_taken")
                    W("final_free", d + 1, r)
                    did(V.tensor_tensor(sout[:, d, :], bdSA[:, 0, :], bdSA[:, 1, :], ALU.add), "final_ready")
                link(V.tensor_tensor(t1[:, :], kds[:, :], rT, ALU.mult))
                did(V.tensor_scalar(t1[:, :], t1[:, :], pp[:, 8:9], None, ALU.mult), "bonus_products")
                W("mean_sums", 1, r)
                did(V.tensor_tensor(as_halves(t3[:, :]), half_view(ps, 4), as_halves(vT), ALU.mult), "bonus_ready")
                did(V.scalar_tensor_tensor(out=as_halves(t4[:, :]), in0=half_view(ps, 6), scalar=-1.0 / L,
                                           in1=as_halves(ysum[:, :]), op0=ALU.mult, op1=ALU.add), "y_squares_in")
                W("ln_root", 1, r)
                link(V.reciprocal(t5[:, :], t5[:, :]))
                link(V.tensor_tensor(t4[:, :], t4[:, :], t5[:, :], ALU.mult))
                link(V.tensor_scalar(t4[:, :], t4[:, :], pp[:, 13:14], pp[:, 14:15], ALU.mult, ALU.add))
                link(V.tensor_tensor(t4[:, :], t4[:, :], t3[:, :], ALU.add))
                W("gate_sums", 1, r)
                W("final_free", 3, r)
                did(V.tensor_tensor(as_halves(outr[:, :]), as_halves(t4[:, :]),
                                    half_view(ps, 4), ALU.mult), "round_done")
            S["dve_cnt"] = dict(cnt)
        S["sig"] = sig


HLEV = (1, 2, 4, 8, 16, 32, 64)
HKINDS = 5


def stage_hgrn(nc, I, O, S, per):
    with ExitStack() as ctx:
        sb = lambda name, shape, dt=F32: ctx.enter_context(nc.sbuf_tensor(name, shape, dt))
        C = S["consts"]
        sig = {}

        def signal(name):
            if name not in sig:
                sig[name] = Signal(ctx, nc, "hg_" + name, per.get("hg_" + name, 0))
            return sig[name]
        w = sb("whg", [P, HKINDS, KT, P])
        halfraw = sb("halfraw", [P, 3, T])
        th = sb("hth", [P, 4, T])
        vT, gh = halfraw[:, 1, :], halfraw[:, 2, :]
        q, sgate = sb("hq", [P, T]), sb("sgate", [P, T])
        key = [sb(f"key{d}", [P, T]) for d in range(2)]
        incl = [sb(f"incl{d}", [P, T]) for d in range(2)]
        excl = [sb(f"excl{d}", [P, T]) for d in range(2)]
        qs = [sb(f"qs{d}", [P, T]) for d in range(2)]
        ks = [sb(f"ks{d}", [P, T]) for d in range(2)]
        att = sb("att", [P, TT, P])
        kn = [sb(f"kn{d}", [P, TT, P]) for d in range(2)]
        vn = sb("vn", [P, TT, P])
        st = [sb(f"hst{d}", [P, TT - 1, P]) for d in range(2)]
        fin = sb("hfin", [P, 2, P])
        o1, rt, outh, osq = sb("o1", [P, T]), sb("hrt", [P, T]), sb("outh", [P, T]), sb("osq", [P, T])
        lbp = sb("lbp", [P, 3, 16])
        hm = sb("hmask", [P, 15, P])
        ps = ctx.enter_context(nc.psum_tensor("psH", [P, 8, 512], F32))
        s_m = ctx.enter_context(nc.semaphore("hg_mask_steps"))
        block = ctx.enter_context(nc.Block())
        wide = lambda b: ps[:, b:b + 2, :].rearrange("p a n -> p (a n)")[:, 0:T]

        def tok(ps_b, c):
            return ps[:, ps_b + c // 4, (c % 4) * P:(c % 4 + 1) * P]

        def seg(ap, m, half):
            return ap.rearrange("p (j a r) -> p j a r", a=2, r=m)[:, :, half, :]

        @block.sync
        def _(sp):
            win = I["w_in"][0].rearrange("(k p) n -> p k n", p=P)
            sp.sem_inc(signal("fin_free").sem, 1)
            for h in range(2):
                for i in range(HKINDS):
                    if h:
                        sp.wait_ge(signal("projected").sem, i + 1)
                    c = HG0 + i * HG_DIM + h * P
                    sp.dma_start(w[:, i, :, :], win[:, :, c:c + P]).then_inc(signal(f"w_in{i}").sem, 16)

            def load(r, i):
                sp.wait_ge(signal("projected").sem, r * HKINDS + (HKINDS + i + 1))
                sp.dma_start(w[:, i, :, :], win[:, :, bass.ds(r * P + (HG0 + i * HG_DIM + 2 * P), P)]).then_inc(signal(f"w_in{i}").sem, 16)

            def body(r, ahead):
                sp.wait_ge(signal("s0_free").sem, r + 1)
                for d, c in ((0, 0), (1, TT - 2)):
                    sp.dma_start(st[d][:, c, :], I["state_hgrn"][0, 0, d].rearrange("h k v -> (h k) v")[bass.ds(r * P, P), :])\
                        .then_inc(signal("s0_in").sem, 16)
                if ahead:
                    for i in range(HKINDS - 1):
                        load(r, i)
                sp.wait_ge(signal("fin_ready").sem, r * 2 + 2)
                for d in range(2):
                    sp.dma_start(O["new_state_hgrn"][0, 0, d].rearrange("h k v -> (h k) v")[bass.ds(r * P, P), :], fin[:, d, :])\
                        .then_inc(signal("out").sem, 16)
                if ahead:
                    load(r, HKINDS - 1)
                sp.wait_ge(signal("round_done").sem, r + 1)
                sp.dma_start(S["outh"][bass.ds(r, 1)].rearrange("o p n -> (o p) n"), outh[:, :]).then_inc(signal("out").sem, 16)
                sp.wait_ge(signal("out").sem, r * 48 + 48)
                sp.sem_inc(signal("fin_free").sem, 1)
            with sp.Fori(0, HG_HEADS - 2) as r:
                body(r, True)
            for r in range(HG_HEADS - 2, HG_HEADS):
                body(r, False)

        @block.gpsimd
        def _(pool):
            n = [0]

            def link(ins):
                n[0] += 1
                ins.then_inc(s_m, 1)
                pool.wait_ge(s_m, n[0])
            link(nc.gpsimd.memset(hm[:, :, :], 0.0))
            link(nc.gpsimd.tensor_copy(hm[:, 0, :], C["ident"][:, :]))
            for l, m in enumerate(HLEV):
                nj = P // (2 * m)
                for d in range(2):
                    v = seg(hm[:, 1 + 7 * d + l, :], m, 1 - d)
                    link(nc.gpsimd.memset(v, 1.0))
                    link(nc.gpsimd.affine_select(out=v, in_=v, compare_op=ALU.is_ge, fill=0.0, base=-m * d,
                                                 pattern=[[-2 * m, nj], [0, m]], channel_multiplier=1))
                    link(nc.gpsimd.affine_select(out=v, in_=v, compare_op=ALU.is_ge, fill=0.0, base=m - 1 + m * d,
                                                 pattern=[[2 * m, nj], [0, m]], channel_multiplier=-1))
            assert n[0] == 44

        @block.tensor
        def _(pe):
            W = lambda name, n, r: pe.wait_ge(signal(name).sem, signal(name).at(n, r))
            cnt = {}

            def inc(mm, name):
                mm.then_inc(signal(name).sem, 1)
                cnt[name] = cnt.get(name, 0) + 1
            ident = C["ident"][:, :]

            def project(r, a, n, first=False):
                for p in range(a, a + n):
                    i, h, k = p // (2 * KT), p // KT % 2, p % KT
                    if p % (2 * KT) == 0:
                        pe.wait_ge(signal(f"w_in{i}").sem, 16 * (r + 1) + 16)
                        if i >= 2:
                            pe.wait_ge(signal("raw_taken").sem, HKINDS * (r + 1) + (i - 1))
                        elif not first:
                            pe.wait_ge(signal("raw_taken").sem, HKINDS * (r + 1))
                    mm = nc.tensor.matmul(ps[:, 2 * (i % 2) + h, 0:HALF], w[:, i, k, :], S["hT"][:, k, h * HALF:(h + 1) * HALF],
                                          start=(k == 0), stop=(k == KT - 1))
                    if p % (2 * KT) == 2 * KT - 1:
                        inc(mm, "projected")

            def body(r, last):
                ahead = [0]

                def fill(n):
                    if not last:
                        project(r, ahead[0], n)
                        ahead[0] += n
                W("raw_taken", 4, r)
                for c in range(TT):
                    mm = nc.tensor.transpose(tok(4, c), halfraw[:, 1, c * P:(c + 1) * P], ident)
                inc(mm, "v_turned")
                fill(16)
                W("diag_ready", 1, r)
                for c in range(TT):
                    mm = nc.tensor.matmul(tok(6, c), qs[1][:, c * P:(c + 1) * P], q[:, c * P:(c + 1) * P], start=True, stop=True)
                inc(mm, "grams")
                W("vn_ready", 1, r)
                n = 1
                for l in range(len(HLEV)):
                    for d in range(2):
                        W("scaled", n, r)
                        if n > 1:
                            W("att_taken", n - 1, r)
                        for c in range(TT):
                            mm = nc.tensor.matmul(tok(4 + 2 * (n % 2 == 0), c), ks[d][:, c * P:(c + 1) * P],
                                                  qs[d][:, c * P:(c + 1) * P], start=True, stop=True)
                        inc(mm, "grams")
                        n += 1
                        fill(8)
                for d in range(2):
                    W("state_factors", d + 1, r)
                    if d == 0:
                        W("att_taken", 15, r)
                    for c in range(TT):
                        mm = nc.tensor.transpose(tok(4 + 2 * d, c), ks[d][:, c * P:(c + 1) * P], ident)
                    inc(mm, "k_turned")
                fill(8)
                for d in range(2):
                    W("kn_ready", d + 1, r)
                    for c in range(TT):
                        mm = nc.tensor.matmul(tok(4 + 2 * d, c), kn[d][:, c, :], vn[:, c, :], start=True, stop=True)
                    inc(mm, "kv_sums")
                fill(8)
                W("states_ready", 1, r)
                for c in range(TT):
                    mm = nc.tensor.matmul(tok(4, c), vn[:, c, :], att[:, c, :], start=True, stop=(c == TT - 1))
                    if c < TT - 1:
                        for d in range(2):
                            mm = nc.tensor.matmul(tok(4, c), st[d][:, c, :], qs[d][:, c * P:(c + 1) * P], start=False, stop=(d == 1))
                inc(mm, "o_sums")
                fill(8)
                W("o_squares", 1, r)
                for h in range(2):
                    mm = nc.tensor.matmul(ps[:, 6 + h, 0:HALF], C["ones"][:, :], osq[:, h * HALF:(h + 1) * HALF], start=True, stop=True)
                inc(mm, "norm_sums")
                fill(8)
                assert last or ahead[0] == HKINDS * 2 * KT
                W("round_done", 1, r)
            project(-1, 0, HKINDS * 2 * KT, first=True)
            cnt.clear()
            with pe.Fori(0, HG_HEADS - 1) as r:
                body(r, False)
            S["hpe_cnt"] = dict(cnt)
            body(HG_HEADS - 1, True)

        @block.scalar
        def _(act):
            W = lambda name, n, r: act.wait_ge(signal(name).sem, signal(name).at(n, r))
            cnt = {}
            A = nc.scalar.activation

            def inc(ins, name):
                ins.then_inc(signal(name).sem, 1)
                cnt[name] = cnt.get(name, 0) + 1
            act.wait_ge(signal("lb_diff").sem, 1)
            A(lbp[:, 0, :], lbp[:, 0, :], ACT.Tanh, scale=0.5).then_inc(signal("lb_tanh").sem, 1)

            def take_raw(r, kinds):
                for i in kinds:
                    act.wait_ge(signal("projected").sem, HKINDS * (r + 1) + (i + 1))
                    act.wait_ge(signal("raw_free").sem, (r + 1) + 1)
                    src = half_view(ps, 2 * (i % 2))
                    raw = {0: (0, 0.5), 3: (1, 1.0), 4: (2, 0.5)}.get(i)
                    tan = {0: 0, 1: 1, 2: 2, 4: 3}.get(i)
                    if tan is not None:
                        t = A(as_halves(th[:, tan, :]), src, ACT.Tanh, scale=0.5)
                    if raw is not None:
                        t = A(as_halves(halfraw[:, raw[0], :]), src, ACT.Copy, scale=raw[1])
                    inc(t, "raw_taken")

            def body(r, last):
                W("v_turned", 1, r)
                inc(A(vn[:, :, :].rearrange("p a b -> p (a b)"), wide(4), ACT.Copy), "vn_ready")
                if not last:
                    take_raw(r, range(4))
                for d in range(2):
                    W("k_turned", d + 1, r)
                    inc(A(kn[d][:, :, :].rearrange("p a b -> p (a b)"), wide(4 + 2 * d), ACT.Copy), "kn_ready")
                W("o_sums", 1, r)
                inc(A(osq[:, :], wide(4), ACT.Square), "o_squares")
                W("norm_sums", 1, r)
                inc(A(as_halves(rt[:, :]), half_view(ps, 6), ACT.Sqrt, scale=1.0 / P, bias=C["eps"][:, 0:1]), "norm_root")
                if not last:
                    take_raw(r, (4,))
            take_raw(-1, range(HKINDS))
            cnt.clear()
            with act.Fori(0, HG_HEADS - 1) as r:
                body(r, False)
            S["hact_cnt"] = dict(cnt)
            body(HG_HEADS - 1, True)

        @block.vector
        def _(dve):
            W = lambda name, n, r: dve.wait_ge(signal(name).sem, signal(name).at(n, r))
            V = nc.vector
            cnt = {}
            dve.sem_inc(signal("raw_free").sem, 1)
            dve.sem_inc(signal("s0_free").sem, 1)
            n0 = [0]

            def once(ins):
                n0[0] += 1
                ins.then_inc(signal("setup_line").sem, 1)
                dve.wait_ge(signal("setup_line").sem, n0[0])
            dve.wait_ge(s_m, 44)
            V.tensor_tensor(lbp[:, 0, :], S["ptab"][:, 2, LB0:LB0 + 16], S["ptab"][:, 2, LB1:LB1 + 16], ALU.subtract)\
                .then_inc(signal("lb_diff").sem, 1)
            dve.wait_ge(signal("lb_tanh").sem, 1)
            once(V.tensor_scalar(lbp[:, 1, :], lbp[:, 0, :], 0.25, 0.75, ALU.mult, ALU.add))
            once(V.tensor_scalar(lbp[:, 2, :], lbp[:, 0, :], -0.25, 0.25, ALU.mult, ALU.add))
            with dve.Fori(0, HG_HEADS) as r:
                cnt.clear()

                def did(ins, name):
                    cnt[name] = cnt.get(name, 0) + 1
                    ins.then_inc(signal(name).sem, 1)
                    dve.wait_ge(signal(name).sem, signal(name).at(cnt[name], r))
                link = lambda ins: did(ins, "vector_line")

                def raised(name):
                    dve.sem_inc(signal(name).sem, 1)
                    cnt[name] = cnt.get(name, 0) + 1
                W("raw_taken", HKINDS, r)
                link(V.scalar_tensor_tensor(out=q[:, :], in0=th[:, 0, :], scalar=1.0, in1=halfraw[:, 0, :], op0=ALU.add, op1=ALU.mult))
                link(V.scalar_tensor_tensor(out=sgate[:, :], in0=th[:, 3, :], scalar=1.0, in1=gh, op0=ALU.add, op1=ALU.mult))
                for d in range(2):
                    link(V.tensor_scalar(incl[d][:, :], th[:, 1 + d, :], lbp[:, 2, bass.ds(r + 8 * d, 1)], lbp[:, 1, bass.ds(r + 8 * d, 1)],
                                         ALU.mult, ALU.add))
                    link(V.tensor_scalar(key[d][:, :], incl[d][:, :], -1.0, 1.0, ALU.mult, ALU.add))
                    if d == 0:
                        link(V.memset(excl[d][:, :], 1.0))
                did(V.tensor_tensor(qs[1][:, :], key[0][:, :], key[1][:, :], ALU.add), "diag_ready")
                W("vn_ready", 1, r)
                raised("raw_free")
                i32 = lambda ap: ap.bitcast(I32)

                def take(n, mask, b, beside):
                    W("grams", n, r)
                    beside().then_inc(signal("vector_line").sem, 1)
                    cnt["vector_line"] += 1
                    did(V.copy_predicated(att[:, :, :], i32(bcast(hm[:, mask, :], TT, 1)), wide(b).rearrange("p (c t) -> p c t", t=P)), "att_taken")
                    dve.wait_ge(signal("vector_line").sem, signal("vector_line").at(cnt["vector_line"], r))
                levels = [(m, d, 1 + 7 * d + l) for l, m in enumerate(HLEV) for d in range(2)]

                def scale(n):
                    m, d, _ = levels[n - 1]
                    qh, kh = 1 - d, d
                    link(V.tensor_tensor(seg(qs[d][:, :], m, qh), seg(q[:, :], m, qh), seg(incl[d][:, :], m, qh), ALU.mult))
                    if m == HLEV[0]:
                        link(V.tensor_copy(seg(qs[d][:, :], m, kh), seg(q[:, :], m, kh)))
                        link(V.tensor_copy(ks[d][:, :], key[d][:, :]))
                    did(V.tensor_tensor(seg(ks[d][:, :], m, kh), seg(key[d][:, :], m, kh), seg(excl[d][:, :], m, kh), ALU.mult), "scaled")
                scale(1)
                take(1, 0, 6, lambda: V.memset(excl[1][:, :], 1.0))
                for n, (m, d, mask) in enumerate(levels, 1):
                    qh, kh = 1 - d, d
                    end = m - 1 if d == 0 else 0
                    tq = seg(incl[d][:, :], m, kh)[:, :, end:end + 1]
                    tk = seg(incl[d][:, :], m, qh)[:, :, end:end + 1]
                    wide_t = lambda a: a.broadcast_to([P, T // (2 * m), m])
                    link(V.tensor_tensor(seg(excl[d][:, :], m, kh), seg(excl[d][:, :], m, kh), wide_t(tk), ALU.mult))
                    if n < len(levels):
                        scale(n + 1)
                    take(n + 1, mask, 4 + 2 * (n % 2 == 0),
                         lambda: V.tensor_tensor(seg(incl[d][:, :], m, qh), seg(incl[d][:, :], m, qh), wide_t(tq), ALU.mult))
                for d in range(2):
                    link(V.tensor_tensor(qs[d][:, :], q[:, :], incl[d][:, :], ALU.mult))
                    did(V.tensor_tensor(ks[d][:, :], key[d][:, :], excl[d][:, :], ALU.mult), "state_factors")
                dve.wait_ge(signal("s0_in").sem, r * 32 + 32)
                W("fin_free", 1, r)
                for d in range(2):
                    W("kv_sums", d + 1, r)
                    did(V.tensor_copy(fin[:, d, :], tok(4 + 2 * d, TT - 1)), "fin_ready")
                    for j in range(TT - 2):
                        c, c2 = (j, j + 1) if d == 0 else (TT - 2 - j, TT - 3 - j)
                        e = c * P + (P - 1 if d == 0 else 0)
                        link(V.scalar_tensor_tensor(out=st[d][:, c2, :], in0=st[d][:, c, :], scalar=incl[d][:, e:e + 1],
                                                    in1=tok(4 + 2 * d, c), op0=ALU.mult, op1=ALU.add))
                raised("states_ready")
                W("norm_root", 1, r)
                raised("s0_free")
                link(V.reciprocal(rt[:, :], rt[:, :]))
                link(V.tensor_tensor(o1[:, :], wide(4), rt[:, :], ALU.mult))
                did(V.scalar_tensor_tensor(out=outh[:, :], in0=o1[:, :], scalar=S["ptab"][:, 2, bass.ds(r + HGN, 1)], in1=sgate[:, :],
                                           op0=ALU.mult, op1=ALU.mult), "round_done")
            S["hdve_cnt"] = dict(cnt)
        S["hsig"] = sig


def stage_merge(nc, I, S):
    with ExitStack() as ctx:
        sb = lambda name, shape, dt=F32: ctx.enter_context(nc.sbuf_tensor(name, shape, dt))
        sg = lambda name: ctx.enter_context(nc.semaphore("mg_" + name))
        SLOTS = 2
        w = [sb(f"wmg{s}", [P, KT, P]) for s in range(SLOTS)]
        br = sb("branches", [P, 2, PAIRS, T])
        th = [sb(f"gth{s}", [P, 2, T]) for s in range(SLOTS)]
        m1, m2 = sb("m1", [P, T]), sb("m2", [P, T])
        ps = ctx.enter_context(nc.psum_tensor("psM", [P, 8, 512], F32))
        s_w = [sg(f"w_in{s}") for s in range(SLOTS)]
        s_wf = [sg(f"w_free{s}") for s in range(SLOTS)]
        s_th = [sg(f"tanh_in{s}") for s in range(SLOTS)]
        s_br = [sg(f"branch_in{i}") for i in range(2)]
        s_branch, s_m, s_mix = map(sg, ("branch_sums", "products", "merged"))
        block = ctx.enter_context(nc.Block())

        @block.sync
        def _(sp):
            win = I["w_in"][0].rearrange("(k p) n -> p k n", p=P)
            for i, name in enumerate(("outr", "outh")):
                sp.dma_start(br[:, i], S[name].rearrange("n p t -> p n t")).then_inc(s_br[i], 16)
            with sp.Fori(0, KT // SLOTS) as r:
                for s in range(SLOTS):
                    sp.wait_ge(s_wf[s], r + 1)
                    for g, name in enumerate(("w_br_rwkv", "w_br_hgrn")):
                        src = I[name][0].rearrange("(k p) n -> p k n", p=P)
                        sp.dma_start(w[s][:, PAIRS * g:PAIRS * (g + 1), :], src[:, :, bass.ds((r * SLOTS + s) * P, P)])\
                            .then_inc(s_w[s], 16)
                    sp.wait_ge(s_mix, r * SLOTS + (s + 1))
                    for g in range(2):
                        sp.dma_start(th[s][:, g, :], S["gates"][bass.ds(r * SLOTS + (s + g * KT), 1)].rearrange("o p n -> (o p) n"))\
                            .then_inc(s_th[s], 16)

        @block.tensor
        def _(pe):
            for s in range(SLOTS):
                pe.sem_inc(s_wf[s], 1)
            with pe.Fori(0, KT // SLOTS) as r:
                for s in range(SLOTS):
                    pe.wait_ge(s_w[s], r * 32 + 32)
                    for g in range(2):
                        pe.wait_ge(s_m, r * 4 + (2 * s + g + 1))
                        pe.wait_ge(s_br[g], 16)
                        for h in range(2):
                            for k in range(PAIRS):
                                mm = nc.tensor.matmul(ps[:, 4 * s + 2 * g + h, 0:HALF], w[s][:, PAIRS * g + k, :],
                                                      br[:, g, k, h * HALF:(h + 1) * HALF], start=(k == 0), stop=(k == PAIRS - 1))
                        mm.then_inc(s_branch, 1)
                    pe.wait_ge(s_branch, r * 4 + (2 * s + 2))
                    pe.sem_inc(s_wf[s], 1)

        @block.vector
        def _(dve):
            dve.sem_inc(s_m, 4)
            dve.sem_inc(s_mix, 2)
            with dve.Fori(0, KT // SLOTS) as r:
                for s in range(SLOTS):
                    dve.wait_ge(s_th[s], r * 32 + 32)
                    for g, m in enumerate((m1, m2)):
                        dve.wait_ge(s_branch, r * 4 + (2 * s + g + 1))
                        nc.vector.scalar_tensor_tensor(out=as_halves(m[:, :]), in0=as_halves(th[s][:, g, :]), scalar=1.0,
                                                       in1=half_view(ps, 4 * s + 2 * g), op0=ALU.add, op1=ALU.mult).then_inc(s_m, 1)
                    dve.wait_ge(s_m, r * 4 + (2 * s + 6))
                    nc.vector.tensor_tensor(S["mergedT"][:, bass.ds(r * SLOTS + s, 1), :].rearrange("p o n -> p (o n)"), m1[:, :], m2[:, :], ALU.add)\
                        .then_inc(s_mix, 1)
                    dve.wait_ge(s_mix, r * SLOTS + (s + 3))


def stage_out_norm(nc, I, S):
    with ExitStack() as ctx:
        sb = lambda name, shape, dt=F32: ctx.enter_context(nc.sbuf_tensor(name, shape, dt))
        sg = lambda name: ctx.enter_context(nc.semaphore("on_" + name))
        w = [sb(f"wout{s}", [P, KT, P]) for s in range(2)]
        xs = [sb(f"xs{s}", [P, T]) for s in range(2)]
        xq = [sb(f"xq{s}", [P, T]) for s in range(2)]
        gth = sb("gth", [P, KT, 2])
        rstd = sb("rstd2", [P, T])
        wr = sb("wr", [P, KT, NE])
        mx, sm, ex = sb("mx", [P, TT]), sb("sm", [P, TT]), sb("ex", [P, TT, NE])
        ps = ctx.enter_context(nc.psum_tensor("psO", [P, 8, 512], F32))
        s_w = [sg(f"w_in{s}") for s in range(2)]
        (s_x, s_r, s_xt, s_xc, s_o, s_x1, s_q, s_ss, s_root, s_v, s_h2, s_ht, s_hc, s_lg, s_lr, s_ex) = map(sg, (
            "x_in", "router_in", "x_turned", "x_copied", "out_sums", "x1_ready", "squares", "square_sums", "root",
            "vector_line", "h2_ready", "h2_turned", "h2_copied", "logits", "logits_ready", "exps"))
        block = ctx.enter_context(nc.Block())
        xrow, x1T, h2T, mT, h2row = S["rows"], S["x1T"], S["hT"], S["mergedT"], S["rows"]
        wide = lambda b: ps[:, b:b + 2, :].rearrange("p a n -> p (a n)")[:, 0:T]

        def tok(b, t):
            return ps[:, b + t // 4, (t % 4) * P:(t % 4 + 1) * P]

        @block.sync
        def _(sp):
            wo = I["w_out"][0].rearrange("(k p) n -> p k n", p=P)
            for j in range(KT):
                if j >= 2:
                    sp.wait_ge(s_o, j - 1)
                sp.dma_start(w[j % 2][:, :, :], wo[:, :, j * P:(j + 1) * P]).then_inc(s_w[j % 2], 16)
                if j == 0:
                    for t in range(TT):
                        src = I["x_sample"][0, t * P:(t + 1) * P, :] if t < TT - 1 else I["x_prompt"][0]
                        sp.dma_start(xrow[:, t, :], src).then_inc(s_x, 16)
                    sp.dma_start(wr[:, :, :], I["moe_router"][0].rearrange("(k p) e -> p k e", p=P)).then_inc(s_r, 16)

        @block.tensor
        def _(pe):
            ident = S["consts"]["ident"][:, :]
            for j in range(KT):
                pe.wait_ge(s_w[j % 2], 16 * (j // 2 + 1))
                if j >= 2:
                    pe.wait_ge(s_x1, 3 * (j - 1))
                for h in range(2):
                    for k in range(KT):
                        mm = nc.tensor.matmul(ps[:, 2 * (j % 2) + h, 0:HALF], w[j % 2][:, k, :], mT[:, k, h * HALF:(h + 1) * HALF],
                                              start=(k == 0), stop=(k == KT - 1))
                mm.then_inc(s_o, 1)
                if j:
                    pe.wait_ge(s_xc, j)
                pe.wait_ge(s_x, 16 * TT)
                for t in range(TT):
                    mm = nc.tensor.transpose(tok(4, t), xrow[:, t, j * P:(j + 1) * P], ident)
                mm.then_inc(s_xt, 1)
                if j >= 1:
                    pe.wait_ge(s_q, j)
                    for h in range(2):
                        mm = nc.tensor.matmul(ps[:, 6 + h, 0:HALF], S["consts"]["ones"][:, :], xq[(j - 1) % 2][:, h * HALF:(h + 1) * HALF],
                                              start=(j == 1), stop=False)
                    mm.then_inc(s_ss, 1)
            pe.wait_ge(s_q, KT)
            for h in range(2):
                mm = nc.tensor.matmul(ps[:, 6 + h, 0:HALF], S["consts"]["ones"][:, :], xq[(KT - 1) % 2][:, h * HALF:(h + 1) * HALF],
                                      start=False, stop=True)
            mm.then_inc(s_ss, 1)
            for j in range(KT):
                b = 2 * (j % 2)
                pe.wait_ge(s_h2, 2 * (j + 1))
                if j >= 2:
                    pe.wait_ge(s_hc, j - 1)
                for t in range(TT):
                    mm = nc.tensor.transpose(tok(b, t), h2T[:, j, t * P:(t + 1) * P], ident)
                mm.then_inc(s_ht, 1)
            pe.wait_ge(s_r, 16)
            for t in range(TT):
                for k in range(KT):
                    mm = nc.tensor.matmul(ps[:, 4, t * NE:(t + 1) * NE], h2T[:, k, t * P:(t + 1) * P], wr[:, k, :],
                                          start=(k == 0), stop=(k == KT - 1))
            mm.then_inc(s_lg, 1)

        @block.scalar
        def _(act):
            A = nc.scalar.activation
            for j in range(KT):
                if j >= 1:
                    act.wait_ge(s_x1, 3 * j)
                    if j >= 3:
                        act.wait_ge(s_ss, j - 2)
                    A(xq[(j - 1) % 2][:, :], x1T[:, j - 1, :], ACT.Square).then_inc(s_q, 1)
                act.wait_ge(s_xt, j + 1)
                A(xs[j % 2][:, :], wide(4), ACT.Copy).then_inc(s_xc, 1)
            act.wait_ge(s_x1, 3 * KT)
            act.wait_ge(s_ss, KT - 2)
            A(xq[(KT - 1) % 2][:, :], x1T[:, KT - 1, :], ACT.Square).then_inc(s_q, 1)
            act.wait_ge(s_ss, KT)
            A(as_halves(rstd[:, :]), half_view(ps, 6), ACT.Sqrt, scale=1.0 / D, bias=S["consts"]["eps"][:, 0:1]).then_inc(s_root, 1)
            for j in range(KT):
                act.wait_ge(s_ht, j + 1)
                A(h2row[:, :, j * P:(j + 1) * P], wide(2 * (j % 2)).rearrange("p (t c) -> p t c", c=P), ACT.Copy).then_inc(s_hc, 1)
            act.wait_ge(s_lr, 1)
            A(ex[:, :, :], ex[:, :, :], ACT.Exp).then_inc(s_ex, 1)

        @block.vector
        def _(dve):
            V = nc.vector
            steps = [0]

            def link(ins):
                steps[0] += 1
                ins.then_inc(s_v, 1)
                dve.wait_ge(s_v, steps[0])
            modT, A2 = S["modT"], S["A2"]
            link(V.tensor_scalar(gth[:, :, :], modT[:, 2 * KT:3 * KT, :], 0.5, None, ALU.mult))
            for j in range(KT):
                dve.wait_ge(s_o, j + 1)
                dve.wait_ge(s_xc, j + 1)
                for s, cut in ((0, slice(0, HALF)), (0, slice(HALF, NS)), (1, slice(NS, T))):
                    b, o = 2 * (j % 2) + cut.start // HALF, cut.start % HALF
                    V.scalar_tensor_tensor(out=x1T[:, j, cut], in0=ps[:, b, o:o + cut.stop - cut.start], scalar=gth[:, j, s:s + 1],
                                           in1=xs[j % 2][:, cut], op0=ALU.mult, op1=ALU.add).then_inc(s_x1, 1)
            dve.wait_ge(s_x1, 3 * KT)
            dve.wait_ge(s_root, 1)
            link(V.reciprocal(rstd[:, :], rstd[:, :]))
            for j in range(KT):
                link(V.tensor_tensor(h2T[:, j, :], x1T[:, j, :], rstd[:, :], ALU.mult))
                for s, cut in enumerate((slice(0, NS), slice(NS, T))):
                    V.tensor_scalar(h2T[:, j, cut], h2T[:, j, cut], A2[:, j, s:s + 1], modT[:, 3 * KT + j, s:s + 1],
                                    ALU.mult, ALU.add).then_inc(s_h2, 1)
            dve.wait_ge(s_h2, 2 * KT)
            dve.wait_ge(s_lg, 1)
            aff = S["aff"]
            lg = ps[:, 4, 0:TT * NE].rearrange("p (t e) -> p t e", e=NE)
            link(V.tensor_reduce(mx[:, :], lg, AX_X, ALU.max))
            V.tensor_tensor(ex[:, :, :], lg, bcast(mx[:, :], NE, 2), ALU.subtract).then_inc(s_lr, 1)
            dve.wait_ge(s_lr, 1)
            dve.wait_ge(s_ex, 1)
            link(V.tensor_reduce(sm[:, :], ex[:, :, :], AX_X, ALU.add))
            link(V.reciprocal(sm[:, :], sm[:, :]))
            link(V.tensor_tensor(aff[:, :, :], ex[:, :, :], bcast(sm[:, :], NE, 2), ALU.mult))


def stage_choose(nc, S):
    with ExitStack() as ctx:
        sb = lambda name, shape, dt=F32: ctx.enter_context(nc.sbuf_tensor(name, shape, dt))
        sg = lambda name: ctx.enter_context(nc.semaphore("ch_" + name))
        left, m8 = sb("left", [NE, T]), sb("m8", [NE, 8])
        one, cum = sb("onerow", [NE, T]), sb("cum", [NE, T])
        ps = ctx.enter_context(nc.psum_tensor("psC", [P, 8, 512], F32))
        s_t, s_v, s_s, s_b = map(sg, ("turned", "vector_line", "slots_ready", "slots_turned"))
        block = ctx.enter_context(nc.Block())
        ident = S["consts"]["ident"]

        @block.tensor
        def _(pe):
            for t in range(TT):
                mm = nc.tensor.transpose(ps[0:NE, t // 4, (t % 4) * P:(t % 4 + 1) * P], S["aff"][:, t, :], ident[:, :])
            mm.then_inc(s_t, 1)
            pe.wait_ge(s_s, 1)
            for t in range(TT):
                mm = nc.tensor.transpose(ps[:, 2, t * NE:(t + 1) * NE], cum[:, t * P:(t + 1) * P], ident[0:NE, 0:NE])
            mm.then_inc(s_b, 1)

        @block.vector
        def _(dve):
            V = nc.vector
            steps = [0]

            def link(ins):
                steps[0] += 1
                ins.then_inc(s_v, 1)
                dve.wait_ge(s_v, steps[0])
            dve.wait_ge(s_t, 1)
            link(V.tensor_copy(left[:, :], ps[0:NE, 0:2, :].rearrange("p a n -> p (a n)")[:, 0:T]))
            for cut, cap in ((slice(0, NS), CAP_S), (slice(NS, T), CAP_P)):
                for _i in range(cap // 8):
                    link(V.max(m8[:, :], left[:, cut]))
                    link(V.match_replace(left[:, cut], m8[:, :], left[:, cut], -1.0))
            link(V.tensor_scalar(left[:, :], left[:, :], 0.0, None, ALU.is_lt))
            link(V.memset(one[:, :], 1.0))
            for cut in (slice(0, NS), slice(NS, T)):
                link(V.tensor_tensor_scan(cum[:, cut], one[:, cut], left[:, cut], 0.0, ALU.mult, ALU.add))
            V.tensor_tensor(cum[:, :], cum[:, :], left[:, :], ALU.mult).then_inc(s_s, 1)
            dve.wait_ge(s_b, 1)
            link(V.tensor_copy(S["slot"][:, :, :].rearrange("p t e -> p (t e)"), ps[:, 2, 0:TT * NE]))


def stage_experts(nc, I, S):
    with ExitStack() as ctx:
        sb = lambda name, shape, dt=F32: ctx.enter_context(nc.sbuf_tensor(name, shape, dt))
        sg = lambda name: ctx.enter_context(nc.semaphore("ex_" + name))
        RING, Q = 8, 4
        M = CAP_S + CAP_P
        FT = FF // P
        KC = 2
        ROUNDS = NE // Q
        gu = lambda e: [("gu", e, k, g) for k in range(KT // KC) for g in range(2)]
        dn = lambda e: [("dn", e, m, 0) for m in range(FT)]
        order = gu(0) + gu(1) + dn(0) + gu(2) + dn(1) + gu(3) + dn(2) + dn(3)
        USES = len(order) // RING
        assert USES * RING == len(order)
        place = {c: n for n, c in enumerate(order)}
        spare = [S[n][:, :, :].rearrange("p k t -> p (k t)")[:, i * 2048:(i + 1) * 2048] for n in ("hT", "mergedT") for i in range(5)]
        ring = spare[0:RING]
        ys, yp = spare[RING], spare[RING + 1][0:64, :]
        xg = sb("xg", [P, KT, Q, M])
        hidT = sb("hidT", [P, FT, M])
        hid = sb("hid", [M, FF])
        sel, selp = sb("sel", [P, 4, Q, CAP_S]), sb("selp", [P, Q, CAP_P])
        selw, selpw = sb("selw", [P, 4, 2, CAP_S]), sb("selpw", [P, 2, 32])
        selT, selpT = sb("selT", [P, NS]), sb("selpT", [64, NP])
        iota = sb("iota", [P, CAP_S])
        gth = sb("gth2", [P, KT, 2])
        ps = ctx.enter_context(nc.psum_tensor("psE", [P, 8, 512], F32))
        s_in = [sg(f"w_in{i}") for i in range(RING)]
        s_free = [sg(f"w_free{i}") for i in range(RING)]
        (s_io, s_sel, s_selw, s_selT, s_selc, s_gath, s_xg, s_gus, s_tanh, s_v, s_hid, s_ht, s_hidT, s_down, s_y, s_sc, s_add, s_z,
         s_gth) = map(sg, (
            "iota", "selected", "weighted_selected", "selection_turned", "selection_copied", "gathered", "xg_ready", "gate_up_sums",
            "gate_tanh", "silu", "hidden", "hidden_turned", "hidden_columns", "down_sums", "y_ready", "scattered", "added", "zeroed",
            "gate_factor"))
        block = ctx.enter_context(nc.Block())
        x1T, rows = S["x1T"], S["rows"]
        wide = lambda b: ps[:, b:b + 2, :].rearrange("p a n -> p (a n)")

        def rounds(eng, body):
            body(0, True, False)
            with eng.Fori(1, ROUNDS - 1) as r:
                body(r, False, False)
            body(ROUNDS - 1, False, True)

        @block.sync
        def _(sp):
            wg, wu, wd = (I[n][0].rearrange("e a b -> (e a) b") for n in ("moe_w_gate", "moe_w_up", "moe_w_down"))
            with sp.Fori(0, ROUNDS) as r:
                for n, (what, e, k, g) in enumerate(order):
                    slot, use = n % RING, n // RING
                    sp.wait_ge(s_free[slot], r * USES + (use + 1))
                    if what == "gu":
                        src = (wg, wu)[g][bass.ds(r * (Q * D) + (e * D + k * KC * P), KC * P), :].rearrange("(k p) f -> p k f", p=P)
                        dst = ring[slot].rearrange("p (k f) -> p k f", k=KC)
                    else:
                        src = wd[bass.ds(r * (Q * FF) + (e * FF + k * P), P), :]
                        dst = ring[slot]
                    sp.dma_start(dst, src).then_inc(s_in[slot], 16)

        @block.gpsimd
        def _(pool):
            nc.gpsimd.iota(iota[:, :], pattern=[[1, CAP_S]], base=1, channel_multiplier=0,
                           allow_small_or_imprecise_dtypes=True).then_inc(s_io, 1)
            nc.gpsimd.memset(selpw[:, :, :], 0.0).then_inc(s_z, 1)
            nc.gpsimd.memset(yp, 0.0).then_inc(s_z, 1)

        @block.tensor
        def _(pe):
            ident = S["consts"]["ident"][:, :]
            for i in range(RING):
                pe.sem_inc(s_free[i], 1)

            def arrived(r, c):
                n = place[c]
                pe.wait_ge(s_in[n % RING], r * (16 * USES) + 16 * (n // RING + 1))
                return ring[n % RING], s_free[n % RING]

            def gather(r):
                pe.wait_ge(s_sel, r + 1)
                for j in range(KT):
                    if j >= 2:
                        pe.wait_ge(s_xg, r * KT + (j - 1))
                    o = ps[:, 4 + j % 2, 0:Q * M].rearrange("p (e s) -> p e s", e=Q)
                    for t in range(4):
                        nc.tensor.matmul(o[:, :, 0:CAP_S], rows[:, t, j * P:(j + 1) * P], sel[:, t, :, :], start=(t == 0), stop=(t == 3))
                    nc.tensor.matmul(o[:, :, CAP_S:M], rows[:, 4, j * P:(j + 1) * P], selp[:, :, :], start=True, stop=True).then_inc(s_gath, 1)

            def gate_up(r, e):
                for what in gu(e):
                    _, _, k, g = what
                    w, free = arrived(r, what)
                    for kk in range(KC):
                        kt = k * KC + kk
                        for c in range(2):
                            mm = nc.tensor.matmul(ps[0:M, 2 * g + c, :], xg[:, kt, e, :], w[:, kk * FF + c * 512:kk * FF + (c + 1) * 512],
                                                  start=(kt == 0), stop=(kt == KT - 1))
                    if k == KT // KC - 1 and g == 1:
                        mm.then_inc(s_gus, 1)
                        pe.wait_ge(s_gus, r * Q + (e + 1))
                        pe.sem_inc(free, 1)
                    else:
                        mm.then_inc(free, 1)

            def turn(r, e):
                pe.wait_ge(s_hid, r * Q + (e + 1))
                for m in range(FT):
                    mm = nc.tensor.transpose(ps[:, m // 4, (m % 4) * M:(m % 4 + 1) * M], hid[:, m * P:(m + 1) * P], ident[0:M, 0:M])
                mm.then_inc(s_ht, 1)
                pe.wait_ge(s_hidT, r * Q + (e + 1))

            def down(r, e):
                for what in dn(e):
                    m = what[2]
                    w, free = arrived(r, what)
                    for c in range(4):
                        mm = nc.tensor.matmul(ps[0:M, 4 + c, :], hidT[:, m, :], w[:, c * 512:(c + 1) * 512], start=(m == 0), stop=(m == FT - 1))
                    if m == FT - 1:
                        mm.then_inc(s_down, 1)
                        pe.wait_ge(s_down, r * Q + (e + 1))
                        pe.sem_inc(free, 1)
                    else:
                        mm.then_inc(free, 1)

            def scatter(r, p):
                pe.wait_ge(s_selw, r * 2 + (p + 1))
                pe.wait_ge(s_y, r * (4 * Q) + 8 * (p + 1))
                for t in range(4):
                    mm = nc.tensor.transpose(ps[:, 6, t * P:(t + 1) * P], selw[:, t].rearrange("p e s -> p (e s)"), ident)
                mm = nc.tensor.transpose(ps[0:64, 7, 0:P], selpw[:, :, :].rearrange("p e s -> p (e s)"), ident)
                mm.then_inc(s_selT, 1)
                pe.wait_ge(s_selc, r * 4 + (2 * p + 2))
                for j in range(KT):
                    b = 4 + 2 * (j % 2)
                    if j >= 2:
                        pe.wait_ge(s_add, r * (4 * KT) + (2 * KT * p + 2 * (j - 1)))
                    nc.tensor.matmul(ps[:, b, :], ys[:, j * P:(j + 1) * P], selT[:, :], start=True, stop=True)
                    nc.tensor.matmul(ps[:, b + 1, 0:P], yp[:, j * P:(j + 1) * P], selpT[:, :], start=True, stop=True).then_inc(s_sc, 1)
                pe.wait_ge(s_add, r * (4 * KT) + 2 * KT * (p + 1))

            def body(r, first, last):
                gate_up(r, 0)
                if not first:
                    scatter(r - 1, 1)
                turn(r, 0)
                gate_up(r, 1)
                down(r, 0)
                turn(r, 1)
                gate_up(r, 2)
                pe.wait_ge(s_y, r * (4 * Q) + 4)
                down(r, 1)
                turn(r, 2)
                gate_up(r, 3)
                scatter(r, 0)
                down(r, 2)
                turn(r, 3)
                pe.wait_ge(s_y, r * (4 * Q) + 12)
                if not last:
                    gather(r + 1)
                    pe.wait_ge(s_xg, r * KT + 2 * KT)
                down(r, 3)
            gather(0)
            pe.wait_ge(s_xg, KT)
            rounds(pe, body)
            scatter(ROUNDS - 1, 1)

        @block.scalar
        def _(act):
            A = nc.scalar.activation

            def gathered(r):
                for j in range(KT):
                    act.wait_ge(s_gath, r * KT + (j + 1))
                    A(xg[:, j, :, :].rearrange("p e s -> p (e s)"), ps[:, 4 + j % 2, 0:Q * M], ACT.Copy).then_inc(s_xg, 1)

            def tanh(r, e):
                act.wait_ge(s_gus, r * Q + (e + 1))
                for c in range(2):
                    A(hid[:, c * 512:(c + 1) * 512], ps[0:M, c, :], ACT.Tanh, scale=0.5).then_inc(s_tanh, 1)

            def columns(r, e):
                act.wait_ge(s_ht, r * Q + (e + 1))
                for c in range(2):
                    t = A(hidT[:, 4 * c:4 * c + 4, :].rearrange("p m s -> p (m s)"), ps[:, c, 0:4 * M], ACT.Copy)
                t.then_inc(s_hidT, 1)

            def results(r, e):
                act.wait_ge(s_down, r * Q + (e + 1))
                for c in range(2, 4):
                    A(ys[64 * (e % 2):64 * (e % 2) + 64, c * 512:(c + 1) * 512], ps[0:64, 4 + c, :], ACT.Copy)
                    A(yp[32 * (e % 2):32 * (e % 2) + CAP_P, c * 512:(c + 1) * 512], ps[64:M, 4 + c, :], ACT.Copy).then_inc(s_y, 1)

            def selection(r, p):
                act.wait_ge(s_selT, r * 2 + (p + 1))
                A(selT[:, :], ps[:, 6, :], ACT.Copy).then_inc(s_selc, 1)
                A(selpT[:, :], ps[0:64, 7, 0:P], ACT.Copy).then_inc(s_selc, 1)

            def body(r, first, last):
                tanh(r, 0)
                if not first:
                    selection(r - 1, 1)
                columns(r, 0)
                tanh(r, 1)
                results(r, 0)
                columns(r, 1)
                tanh(r, 2)
                results(r, 1)
                columns(r, 2)
                tanh(r, 3)
                selection(r, 0)
                results(r, 2)
                columns(r, 3)
                if not last:
                    gathered(r + 1)
                results(r, 3)
            gathered(0)
            rounds(act, body)
            selection(ROUNDS - 1, 1)

        @block.vector
        def _(dve):
            V = nc.vector

            def choose(r):
                for e in range(Q):
                    for t in range(TT):
                        out, cap = (sel[:, t, e, :], CAP_S) if t < 4 else (selp[:, e, :], CAP_P)
                        last = V.tensor_scalar(out, iota[:, 0:cap], S["slot"][:, t, bass.ds(r * Q + e, 1)], None, ALU.is_equal)
                last.then_inc(s_sel, 1)

            def weigh(r, p):
                for e in range(2):
                    for t in range(TT):
                        out, cap = (selw[:, t, e, :], CAP_S) if t < 4 else (selpw[:, e, 0:CAP_P], CAP_P)
                        col = bass.ds(r * Q + (2 * p + e), 1)
                        last = V.tensor_scalar(out, iota[:, 0:cap], S["slot"][:, t, col], S["aff"][:, t, col], ALU.is_equal, ALU.mult)
                last.then_inc(s_selw, 1)

            def silu(r, e):
                for c in range(2):
                    cut = slice(c * 512, (c + 1) * 512)
                    dve.wait_ge(s_tanh, r * (2 * Q) + (2 * e + c + 1))
                    V.scalar_tensor_tensor(out=hid[:, cut], in0=hid[:, cut], scalar=1.0, in1=ps[0:M, c, :], op0=ALU.add, op1=ALU.mult)\
                        .then_inc(s_v, 1)
                for c in range(2):
                    cut = slice(c * 512, (c + 1) * 512)
                    dve.wait_ge(s_v, r * (2 * Q) + (2 * e + c + 1))
                    last = V.tensor_tensor(hid[:, cut], hid[:, cut], ps[0:M, 2 + c, :], ALU.mult)
                last.then_inc(s_hid, 1)

            def results(r, e):
                dve.wait_ge(s_down, r * Q + (e + 1))
                for c in range(2):
                    V.tensor_copy(ys[64 * (e % 2):64 * (e % 2) + 64, c * 512:(c + 1) * 512], ps[0:64, 4 + c, :])
                    V.tensor_copy(yp[32 * (e % 2):32 * (e % 2) + CAP_P, c * 512:(c + 1) * 512], ps[64:M, 4 + c, :]).then_inc(s_y, 1)

            def add(r, p):
                for j in range(KT):
                    b = 4 + 2 * (j % 2)
                    dve.wait_ge(s_sc, r * (2 * KT) + (p * KT + j + 1))
                    for s, (cut, bb) in enumerate(((slice(0, NS), b), (slice(NS, T), b + 1))):
                        V.scalar_tensor_tensor(out=x1T[:, j, cut], in0=ps[:, bb, 0:cut.stop - cut.start], scalar=gth[:, j, s:s + 1],
                                               in1=x1T[:, j, cut], op0=ALU.mult, op1=ALU.add).then_inc(s_add, 1)
                dve.wait_ge(s_add, r * (4 * KT) + 2 * KT * (p + 1))

            def body(r, first, last):
                silu(r, 0)
                if not first:
                    add(r - 1, 1)
                weigh(r, 0)
                silu(r, 1)
                results(r, 0)
                silu(r, 2)
                results(r, 1)
                silu(r, 3)
                add(r, 0)
                results(r, 2)
                weigh(r, 1)
                if not last:
                    choose(r + 1)
                results(r, 3)
            dve.wait_ge(s_io, 1)
            dve.wait_ge(s_z, 2)
            V.tensor_scalar(gth[:, :, :], S["modT"][:, 5 * KT:6 * KT, :], 0.5, None, ALU.mult).then_inc(s_gth, 1)
            dve.wait_ge(s_gth, 1)
            choose(0)
            rounds(dve, body)
            add(ROUNDS - 1, 1)


def stage_final(nc, I, O, S):
    with ExitStack() as ctx:
        sb = lambda name, shape, dt=F32: ctx.enter_context(nc.sbuf_tensor(name, shape, dt))
        sg = lambda name: ctx.enter_context(nc.semaphore("fi_" + name))
        g, junk = (S["mergedT"][:, :, :].rearrange("p k t -> p (k t)")[:, i * D:(i + 1) * D] for i in range(2))
        yv = S["hT"][:, :, :].rearrange("p k t -> p (k t)").rearrange("p (t n) -> p t n", n=D)
        ssq, rs = sb("ssqf", [P, TT]), sb("rsf", [P, TT])
        ps = ctx.enter_context(nc.psum_tensor("psF", [P, 8, 512], F32))
        s_g, s_t, s_c, s_ss, s_root, s_r, s_y, s_out = map(sg, ("g_in", "turned", "copied", "ssq", "root", "rstd", "y_ready", "y_out"))
        block = ctx.enter_context(nc.Block())
        rows = S["rows"]

        @block.sync
        def _(sp):
            sp.dma_start(g, I["final_norm_g"].partition_broadcast(P)).then_inc(s_g, 16)
            for t in range(TT):
                dst = O["y_sample"][0, t * P:(t + 1) * P, :] if t < TT - 1 else O["y_prompt"][0]
                sp.wait_ge(s_y, t + 1)
                sp.dma_start(dst, yv[:, t, :]).then_inc(s_out, 16)
            sp.wait_ge(s_out, 16 * TT)

        @block.tensor
        def _(pe):
            for i in range(4 * TT):
                t, q = divmod(i, 4)
                if i >= 8:
                    pe.wait_ge(s_c, i - 7)
                for n in range(4):
                    mm = nc.tensor.transpose(ps[:, i % 8, n * P:(n + 1) * P], S["x1T"][:, 4 * q + n, t * P:(t + 1) * P],
                                             S["consts"]["ident"][:, :])
                mm.then_inc(s_t, 1)

        @block.scalar
        def _(act):
            A = nc.scalar.activation
            for t in range(TT):
                act.wait_ge(s_c, 4 * t + 4)
                if t:
                    act.wait_ge(s_ss, t)
                A(junk, rows[:, t, :], ACT.Square, accum_out=ssq[:, t:t + 1]).then_inc(s_ss, 1)
            act.wait_ge(s_ss, TT)
            A(rs[:, :], ssq[:, :], ACT.Sqrt, scale=1.0 / D, bias=S["consts"]["eps"][:, 0:1]).then_inc(s_root, 1)

        @block.vector
        def _(dve):
            V = nc.vector
            for i in range(4 * TT):
                t, q = divmod(i, 4)
                dve.wait_ge(s_t, i + 1)
                V.tensor_copy(rows[:, t, q * 512:(q + 1) * 512], ps[:, i % 8, :]).then_inc(s_c, 1)
            dve.wait_ge(s_root, 1)
            dve.wait_ge(s_g, 16)
            V.reciprocal(rs[:, :], rs[:, :]).then_inc(s_r, 1)
            dve.wait_ge(s_r, 1)
            for t in range(TT):
                V.scalar_tensor_tensor(out=yv[:, t, :], in0=rows[:, t, :], scalar=rs[:, t:t + 1], in1=g,
                                       op0=ALU.mult, op1=ALU.mult).then_inc(s_y, 1)


def build_layer(nc, I, O, per=None):
    per = per or PER
    with ExitStack() as ctx:
        sb = lambda name, shape, dt=F32: ctx.enter_context(nc.sbuf_tensor(name, shape, dt))
        S = {"consts": {"ident": sb("ident", [P, P]), "bd": sb("bdmask", [P, 5, 2, L]), "cm": sb("cmask", [P, 4, L]),
                        "ci": sb("cident", [P, L]), "ns": sb("nstart", [P, T]), "ones": sb("ones", [P, P]), "eps": sb("epsv", [P, 2])},
             "ptab": sb("ptab", [P, 3, P]), "modT": sb("modT", [P, 96, 2]),
             "A1": sb("A1", [P, KT, 2]), "A2": sb("A2", [P, KT, 2]), "aff": sb("aff", [P, TT, NE]), "slot": sb("slot", [P, TT, NE]),
             "gates": nc.dram_tensor("gates_scratch", (2 * KT, P, T), F32, kind="Internal").ap(),
             "outr": nc.dram_tensor("outr_scratch", (PAIRS, P, T), F32, kind="Internal").ap(),
             "outh": nc.dram_tensor("outh_scratch", (HG_HEADS, P, T), F32, kind="Internal").ap()}
        with nc.sbuf_tensor("hT", [P, KT, T], F32) as hT:
            S["hT"] = hT
            stage_modulation(nc, I, S)
            with nc.sbuf_tensor("lora", [P, 3, T], F32) as lora, nc.sbuf_tensor("lw", [P, 3, 2, P], F32) as lw:
                S["lora"], S["lw"] = lora, lw
                stage_lora(nc, I, S)
                with cleared_semaphores(nc):
                    stage_rwkv(nc, I, O, S, per)
            with cleared_semaphores(nc):
                stage_hgrn(nc, I, O, S, per)
            with nc.sbuf_tensor("mergedT", [P, KT, T], F32) as mergedT:
                S["mergedT"] = mergedT
                stage_merge(nc, I, S)
                with nc.sbuf_tensor("x1a", [P, KT, T], F32) as x1T, nc.sbuf_tensor("rows_a", [P, TT, D], F32) as rows:
                    S["x1T"], S["rows"] = x1T, rows
                    stage_out_norm(nc, I, S)
                    stage_choose(nc, S)
                    stage_experts(nc, I, S)
                    stage_final(nc, I, O, S)
        return S


PER = {'bd_factors': 4,
 'bdn_ready': 30,
 'bdnt_ready': 24,
 'bdtt_ready': 6,
 'bdv_ready': 3,
 'bonus_products': 1,
 'bonus_ready': 1,
 'bonus_sums': 1,
 'cn_ready': 48,
 'derived': 1,
 'exps': 8,
 'factors': 10,
 'final_free': 3,
 'final_ready': 2,
 'final_taken': 2,
 'final_turned': 2,
 'gate_sums': 1,
 'grams': 6,
 'grams_taken': 6,
 'hg_att_taken': 15,
 'hg_diag_ready': 1,
 'hg_fin_free': 1,
 'hg_fin_ready': 2,
 'hg_grams': 15,
 'hg_k_turned': 2,
 'hg_kn_ready': 2,
 'hg_kv_sums': 2,
 'hg_norm_root': 1,
 'hg_norm_sums': 1,
 'hg_o_squares': 1,
 'hg_o_sums': 1,
 'hg_projected': 5,
 'hg_raw_free': 1,
 'hg_raw_taken': 5,
 'hg_round_done': 1,
 'hg_s0_free': 1,
 'hg_scaled': 14,
 'hg_state_factors': 2,
 'hg_states_ready': 1,
 'hg_v_turned': 1,
 'hg_vector_line': 64,
 'hg_vn_ready': 1,
 'kk_max': 1,
 'kk_raw': 1,
 'kk_ready': 1,
 'kk_root': 1,
 'kk_squares': 1,
 'kk_sums': 1,
 'ln_root': 1,
 'logs': 2,
 'lora_sums': 2,
 'lora_taken': 4,
 'lw_free': 1,
 'mean_sums': 1,
 'mixed': 3,
 'n_turned': 24,
 'nr_ready': 20,
 'r_sums': 20,
 'raw_free': 1,
 'round_done': 1,
 'rows_taken': 12,
 'rows_turned': 12,
 's0_free': 2,
 's0_ready': 2,
 's0_spread': 2,
 's0_turned': 2,
 'sa_ready': 20,
 'sa_spread': 20,
 'sa_sums': 20,
 'squared': 30,
 'state_ready': 20,
 'state_spread': 20,
 'state_sums': 20,
 'tile_done': 7,
 'tile_taken': 7,
 'tt_ready': 30,
 'tt_sums': 30,
 'v_spread': 2,
 'v_turned': 3,
 'var_sums': 1,
 'vector_line': 86,
 'y_squares': 1,
 'y_squares_in': 1,
 'y_sums': 20,
 'y_taken': 2}


_INS = ["x_prompt", "x_sample", "c", "state_rwkv", "state_hgrn", "c_ctx", "norm1_g", "norm2_g", "final_norm_g",
        "ada_w", "ada_b", "w_in", "rw_mu", "rw_w0", "rw_w2", "rw_a0", "rw_a2", "rw_g2", "rw_k_k", "rw_k_a", "rw_r_k",
        "rw_ln_w", "rw_ln_b", "hg_lb", "hg_norm_g", "w_br_rwkv", "w_br_hgrn", "w_out", "moe_router",
        "moe_w_gate", "moe_w_up", "moe_w_down"]
_OUTS = [("y_prompt", (1, NP, D)), ("y_sample", (1, NS, D)), ("new_state_rwkv", (1, 1, 2, RW_HEADS, 64, 64)),
         ("new_state_hgrn", (1, 1, 2, HG_HEADS, P, P))]


def kernel(**inputs):
    import numpy as _np
    import concourse.bacc as _bacc
    from concourse.bass_utils import run_bass_kernel_spmd as _run

    nc = _bacc.Bacc("TRN2", target_bir_lowering=False, num_devices=1)
    arrays, I, O = {}, {}, {}
    for name in _INS:
        a = _np.ascontiguousarray(inputs[name])
        arrays[f"in_{name}"] = a
        I[name] = nc.dram_tensor(f"in_{name}", a.shape, F32, kind="ExternalInput").ap()
    for name, shape in _OUTS:
        O[name] = nc.dram_tensor(f"out_{name}", shape, F32, kind="ExternalOutput").ap()
    build_layer(nc, I, O)
    r = _run(nc, [arrays], core_ids=[0])
    return tuple(r.results[0][f"out_{name}"] for name, _ in _OUTS)
```
